# Optimizing a Trainium2 kernel written in Bass

```python
import math
import jax, jax.numpy as jnp
from jax import lax
import numpy as np

D_MODEL = 2048
BATCH = 1
SEQ = 256
DEPTH = 1

MIX_WIDTH = D_MODEL
GDN_WIDTH = MIX_WIDTH // 2
GDN_HEAD_DIM = 128
GDN_HEADS = GDN_WIDTH // GDN_HEAD_DIM
GDN_CHUNK = 64
CONV_WIDTH = 4
RG_WIDTH = MIX_WIDTH - GDN_WIDTH
RG_BLOCKS = 8
RG_BLOCK_DIM = RG_WIDTH // RG_BLOCKS
LRU_C = 8.0
N_GROUPS = 4
EXPERTS_PER_GROUP = 8
N_EXPERTS = N_GROUPS * EXPERTS_PER_GROUP
TOP_K = 2
EXPERT_FF = D_MODEL // 4
NORM_EPS = 1e-6
IN_COLS = 4 * GDN_WIDTH + 2 * GDN_HEADS + 2 * RG_WIDTH

kernel_name = "hymba_gdn_rglru_hmoe_block"

def rms_norm(x, w):
    xf = x.astype(jnp.float32)
    y = xf * lax.rsqrt(jnp.mean(xf * xf, axis=-1, keepdims=True) + NORM_EPS)
    return (y * w.astype(jnp.float32)).astype(x.dtype)

def l2_normalize(x):
    return x * lax.rsqrt(jnp.sum(x * x, axis=-1, keepdims=True) + NORM_EPS)

def causal_depthwise_conv(x, w):
    c = x.shape[-1]
    return lax.conv_general_dilated(
        x, w[:, None, :].astype(x.dtype), window_strides=(1,),
        padding=[(w.shape[0] - 1, 0)], dimension_numbers=("NWC", "WIO", "NWC"),
        feature_group_count=c)

def chunk_gated_delta_rule(q, k, v, g, beta):
    b_, t_, h_, dk = q.shape
    dv = v.shape[-1]
    c_ = GDN_CHUNK
    n_ = t_ // c_

    def to_chunks(t):
        return t.reshape(b_, n_, c_, h_, -1).transpose(0, 3, 1, 2, 4)

    q, k, v = to_chunks(q), to_chunks(k), to_chunks(v)
    g = g.reshape(b_, n_, c_, h_).transpose(0, 3, 1, 2)
    beta = beta.reshape(b_, n_, c_, h_).transpose(0, 3, 1, 2)
    g_cum = jnp.cumsum(g, axis=-1)

    causal = jnp.tril(jnp.ones((c_, c_), dtype=bool))
    strict = jnp.tril(jnp.ones((c_, c_), dtype=bool), -1)
    diff = g_cum[..., :, None] - g_cum[..., None, :]
    decay = jnp.exp(jnp.where(causal, diff, -jnp.inf))

    kk = jnp.einsum("bhnik,bhnjk->bhnij", k, k)
    a_strict = jnp.where(strict, beta[..., :, None] * kk * decay, 0.0)
    lhs = a_strict + jnp.eye(c_, dtype=jnp.float32)
    rhs = jnp.concatenate(
        [v * beta[..., None], k * (beta * jnp.exp(g_cum))[..., None]], axis=-1)
    sol = lax.linalg.triangular_solve(lhs, rhs, left_side=True, lower=True,
                                      unit_diagonal=True)
    u = sol[..., :dv]
    w = sol[..., dv:]

    attn_intra = jnp.einsum("bhnik,bhnjk->bhnij", q, k) * decay

    def move(t):
        return jnp.moveaxis(t, 2, 0)

    def step(state, inp):
        q_c, k_c, u_c, w_c, g_c, at_c = inp
        v_new = u_c - jnp.einsum("bhck,bhkv->bhcv", w_c, state)
        o_c = (jnp.einsum("bhck,bhkv->bhcv", q_c * jnp.exp(g_c)[..., None], state)
               + jnp.einsum("bhij,bhjv->bhiv", at_c, v_new))
        g_last = g_c[..., -1]
        k_dec = k_c * jnp.exp(g_last[..., None] - g_c)[..., None]
        state = (state * jnp.exp(g_last)[..., None, None]
                 + jnp.einsum("bhck,bhcv->bhkv", k_dec, v_new))
        return state, o_c

    s0 = jnp.zeros((b_, h_, dk, dv), jnp.float32)
    _, o = lax.scan(step, s0, (move(q), move(k), move(u), move(w), move(g_cum),
                               move(attn_intra)))
    return o.transpose(1, 0, 3, 2, 4).reshape(b_, t_, h_, dv)

def gated_deltanet_group(q, k, v, z, b, a, conv_w, a_log, dt_bias, norm_w):
    b_, t_, _ = q.shape
    qkv = jax.nn.silu(causal_depthwise_conv(jnp.concatenate([q, k, v], axis=-1), conv_w))
    qkv = qkv.astype(jnp.float32)
    q, k, v = jnp.split(qkv, 3, axis=-1)
    shp = (b_, t_, GDN_HEADS, GDN_HEAD_DIM)
    q = l2_normalize(q.reshape(shp)) * (GDN_HEAD_DIM ** -0.5)
    k = l2_normalize(k.reshape(shp))
    v = v.reshape(shp)
    beta = jax.nn.sigmoid(b.astype(jnp.float32))
    g = -jnp.exp(a_log.astype(jnp.float32)) * jax.nn.softplus(
        a.astype(jnp.float32) + dt_bias.astype(jnp.float32))
    o = chunk_gated_delta_rule(q, k, v, g, beta)
    o = rms_norm(o, norm_w) * jax.nn.silu(z.astype(jnp.float32).reshape(shp))
    return o.reshape(b_, t_, GDN_WIDTH)

def lru_combine(c1, c2):
    a1, b1 = c1
    a2, b2 = c2
    return a1 * a2, a2 * b1 + b2

def rglru_group(xr, gate, conv_w, conv_b, w_rgate, b_rgate, w_igate, b_igate, lam, norm_w):
    b_, t_, _ = xr.shape
    xc = (causal_depthwise_conv(xr, conv_w) + conv_b).astype(jnp.float32)
    xb = xc.reshape(b_, t_, RG_BLOCKS, RG_BLOCK_DIM)
    r = jax.nn.sigmoid(jnp.einsum("btni,nij->btnj", xb, w_rgate.astype(jnp.float32))
                       + b_rgate.astype(jnp.float32).reshape(RG_BLOCKS, RG_BLOCK_DIM))
    i = jax.nn.sigmoid(jnp.einsum("btni,nij->btnj", xb, w_igate.astype(jnp.float32))
                       + b_igate.astype(jnp.float32).reshape(RG_BLOCKS, RG_BLOCK_DIM))
    r = r.reshape(b_, t_, RG_WIDTH)
    i = i.reshape(b_, t_, RG_WIDTH)
    log_a = -LRU_C * r * jax.nn.softplus(-lam.astype(jnp.float32))
    a_t = jnp.exp(log_a)
    mult = jnp.sqrt(-jnp.expm1(2.0 * log_a))
    _, h = lax.associative_scan(lru_combine, (a_t, mult * (i * xc)), axis=1)
    y = h * jax.nn.gelu(gate.astype(jnp.float32))
    y = rms_norm(y.reshape(b_, t_, RG_BLOCKS, RG_BLOCK_DIM),
                 norm_w.reshape(RG_BLOCKS, RG_BLOCK_DIM))
    return y.reshape(b_, t_, RG_WIDTH)

def hierarchical_moe(h, w_group, b_group, w_expert, b_expert, w1, w3, w2):
    b_, t_, d_ = h.shape
    xt = h.reshape(-1, d_)
    grp_prob = jax.nn.softmax((xt @ w_group).astype(jnp.float32)
                              + b_group.astype(jnp.float32), axis=-1)
    grp_p, grp_idx = lax.top_k(grp_prob, 1)
    exp_logits = ((xt @ w_expert).astype(jnp.float32) + b_expert.astype(jnp.float32)
                  ).reshape(-1, N_GROUPS, EXPERTS_PER_GROUP)
    sel_logits = jnp.take_along_axis(exp_logits, grp_idx[:, :, None], axis=1)[:, 0]
    top_p, top_idx = lax.top_k(jax.nn.softmax(sel_logits, axis=-1), TOP_K)
    top_p = top_p / jnp.sum(top_p, axis=-1, keepdims=True)
    gate = grp_p * top_p
    global_idx = grp_idx * EXPERTS_PER_GROUP + top_idx
    combine = jnp.sum(jax.nn.one_hot(global_idx, N_EXPERTS, dtype=jnp.float32)
                      * gate[..., None], axis=1)
    y = jnp.zeros(xt.shape, jnp.float32)
    for e in range(N_EXPERTS):
        he = jax.nn.silu(xt @ w1[e]) * (xt @ w3[e])
        y = y + combine[:, e:e + 1] * (he @ w2[e]).astype(jnp.float32)
    return y.astype(h.dtype).reshape(b_, t_, d_)

def setup_inputs(seed: int = 0) -> dict:
    key = jax.random.key(seed)
    ks = jax.random.split(key, 25)
    L = DEPTH
    f32 = jnp.float32

    def nrm(k, shape, scale):
        return jax.random.normal(k, shape, f32) * scale

    def gain(k, shape):
        return 1.0 + 0.02 * jax.random.normal(k, shape, f32)

    dt = jnp.exp(jax.random.uniform(ks[5], (L, GDN_HEADS), f32,
                                    minval=math.log(1e-3), maxval=math.log(1e-1)))
    a_init = jax.random.uniform(ks[13], (L, RG_WIDTH), f32, minval=0.9, maxval=0.999)
    a_base = a_init ** (1.0 / LRU_C)
    return {
        "x": nrm(ks[0], (BATCH, SEQ, D_MODEL), 1.0),
        "norm_mix_w": gain(ks[1], (L, D_MODEL)),
        "w_in": nrm(ks[2], (L, D_MODEL, IN_COLS), D_MODEL ** -0.5),
        "gdn_conv_w": nrm(ks[3], (L, CONV_WIDTH, 3 * GDN_WIDTH), CONV_WIDTH ** -0.5),
        "gdn_a_log": jnp.log(jax.random.uniform(ks[4], (L, GDN_HEADS), f32,
                                                minval=1.0, maxval=16.0)),
        "gdn_dt_bias": dt + jnp.log(-jnp.expm1(-dt)),
        "gdn_norm_w": gain(ks[6], (L, GDN_HEAD_DIM)),
        "rg_conv_w": nrm(ks[7], (L, CONV_WIDTH, RG_WIDTH), CONV_WIDTH ** -0.5),
        "rg_conv_b": nrm(ks[8], (L, RG_WIDTH), 0.01),
        "rg_w_rgate": nrm(ks[9], (L, RG_BLOCKS, RG_BLOCK_DIM, RG_BLOCK_DIM), RG_BLOCK_DIM ** -0.5),
        "rg_b_rgate": nrm(ks[10], (L, RG_WIDTH), 0.01),
        "rg_w_igate": nrm(ks[11], (L, RG_BLOCKS, RG_BLOCK_DIM, RG_BLOCK_DIM), RG_BLOCK_DIM ** -0.5),
        "rg_b_igate": nrm(ks[12], (L, RG_WIDTH), 0.01),
        "rg_lambda": jnp.log(a_base) - jnp.log1p(-a_base),
        "rg_norm_w": gain(ks[14], (L, RG_WIDTH)),
        "w_out": nrm(ks[15], (L, MIX_WIDTH, D_MODEL), MIX_WIDTH ** -0.5),
        "norm_ffn_w": gain(ks[16], (L, D_MODEL)),
        "router_w_group": nrm(ks[17], (L, D_MODEL, N_GROUPS), D_MODEL ** -0.5),
        "router_b_group": nrm(ks[18], (L, N_GROUPS), 0.01),
        "router_w_expert": nrm(ks[19], (L, D_MODEL, N_EXPERTS), D_MODEL ** -0.5),
        "router_b_expert": nrm(ks[20], (L, N_EXPERTS), 0.01),
        "expert_w1": nrm(ks[21], (L, N_EXPERTS, D_MODEL, EXPERT_FF), D_MODEL ** -0.5),
        "expert_w3": nrm(ks[22], (L, N_EXPERTS, D_MODEL, EXPERT_FF), D_MODEL ** -0.5),
        "expert_w2": nrm(ks[23], (L, N_EXPERTS, EXPERT_FF, D_MODEL), EXPERT_FF ** -0.5),
        "norm_final_w": gain(ks[24], (D_MODEL,)),
    }

def reference(x, norm_mix_w, w_in, gdn_conv_w, gdn_a_log, gdn_dt_bias, gdn_norm_w,
              rg_conv_w, rg_conv_b, rg_w_rgate, rg_b_rgate, rg_w_igate, rg_b_igate,
              rg_lambda, rg_norm_w, w_out, norm_ffn_w, router_w_group, router_b_group,
              router_w_expert, router_b_expert, expert_w1, expert_w3, expert_w2,
              norm_final_w):
    widths = [GDN_WIDTH, GDN_WIDTH, GDN_WIDTH, GDN_WIDTH, GDN_HEADS, GDN_HEADS,
              RG_WIDTH, RG_WIDTH]
    split_points = [int(s) for s in np.cumsum(widths)[:-1]]
    for l in range(DEPTH):
        h = rms_norm(x, norm_mix_w[l])
        proj = h @ w_in[l]
        q, k, v, z, b, a, rx, rgate = jnp.split(proj, split_points, axis=-1)
        y_gdn = gated_deltanet_group(q, k, v, z, b, a, gdn_conv_w[l], gdn_a_log[l],
                                     gdn_dt_bias[l], gdn_norm_w[l])
        y_rg = rglru_group(rx, rgate, rg_conv_w[l], rg_conv_b[l], rg_w_rgate[l],
                           rg_b_rgate[l], rg_w_igate[l], rg_b_igate[l], rg_lambda[l],
                           rg_norm_w[l])
        mix = jnp.concatenate([y_gdn, y_rg], axis=-1).astype(x.dtype)
        x = x + mix @ w_out[l]
        h = rms_norm(x, norm_ffn_w[l])
        x = x + hierarchical_moe(h, router_w_group[l], router_b_group[l],
                                 router_w_expert[l], router_b_expert[l],
                                 expert_w1[l], expert_w3[l], expert_w2[l])
    return rms_norm(x, norm_final_w)


_drawn_inputs = setup_inputs


def setup_inputs(seed=0):
    import zlib

    import numpy as np

    out = dict(_drawn_inputs(seed))
    spreads = {}
    factors = {'gdn_norm_w': 16.179,
     'rg_b_rgate': 26.314,
     'rg_b_igate': 16.987,
     'rg_norm_w': 12.401,
     'router_b_group': 18.828,
     'router_b_expert': 18.044,
     'norm_final_w': 8.008,
     'norm_ffn_w': 5.207}
    for name, (base, spread) in spreads.items():
        noise = np.random.default_rng([zlib.crc32(name.encode()), seed]).standard_normal(out[name].shape)
        drawn = base * np.exp(spread * noise) if base else spread * noise
        out[name] = __import__('jax').numpy.asarray(drawn.astype(out[name].dtype))
    for name, factor in factors.items():
        out[name] = (out[name] * factor).astype(out[name].dtype)
    return out
```

```python
from contextlib import ExitStack

import numpy as np
import concourse.bass as bass
from concourse import mybir

F32 = mybir.dt.float32
I32 = mybir.dt.int32
U32 = mybir.dt.uint32
ALU = mybir.AluOpType
ACT = mybir.ActivationFunctionType
AX = mybir.AxisListType

P = 128
D = 2048
T = 256
NT = T // P
KD = D // P
NH = 8
HD = 128
CH = 64
NC = T // CH
TAPS = 4
GW = NH * HD
NG = 4
EG = 8
NE = NG * EG
FF = 512
FC = FF // P
SLOTS = 64
LEVELS = 6
EPS = 1e-6
QSCALE = float(HD) ** -0.5
GELU_C = 0.044715
GELU_S = 0.7978845608028654
HD2 = D // 2
NONE = 1.0e6

C_ID = 0
C_MQ = C_ID + P
C_MS = C_MQ + P
C_LV = C_MS + P
C_TRI = C_LV + LEVELS * P
C_ONE = C_TRI + P
C_IO = C_ONE + P
C_GRP = C_IO + NE
C_SEL = C_GRP + NE
C_COL = C_SEL + 16
C_END = C_COL + 4

Q_CONV = 0
Q_RGC = 12
Q_CB = 16
Q_BR = 17
Q_BI = 18
Q_LAM = 19
Q_RGN = 20
Q_VB = 21
Q_KB = 23
Q_KDEC = 25
Q_GC = 27
NQ = 29


def constants():
    c = np.zeros((P, C_END), np.float32)
    j, i = np.meshgrid(np.arange(P), np.arange(P), indexing="ij")
    same = j // CH == i // CH
    c[:, C_ID:C_ID + P] = j == i
    c[:, C_MQ:C_MQ + P] = (same & (j <= i)) * QSCALE
    c[:, C_MS:C_MS + P] = same & (j < i)
    for l in range(LEVELS):
        b = 1 << l
        c[:, C_LV + l * P:C_LV + (l + 1) * P] = (j // (2 * b) == i // (2 * b)) & (j // b % 2 == 0) & (i // b % 2 == 1)
    c[:, C_TRI:C_TRI + P] = j < i
    c[:, C_ONE:C_ONE + P] = 1
    c[:, C_IO:C_IO + NE] = np.arange(NE)
    c[:, C_GRP:C_GRP + NE] = np.arange(NE) // EG
    c[:16, C_SEL:C_SEL + 16] = np.eye(16)
    p = np.arange(P)
    c[:, C_COL], c[:, C_COL + 1], c[:, C_COL + 2], c[:, C_COL + 3] = p, p >= SLOTS, 2 * p, 4 * p
    return c


class Link:

    def __init__(self, eng, sem):
        self.eng, self.sem, self.base, self.n = eng, sem, 0, 0

    def __call__(self, ins):
        ins.then_inc(self.sem, 1)
        self.n += 1
        self.eng.wait_ge(self.sem, self.base + self.n)
        return ins

    def enter(self, turn, per):
        if not isinstance(self.base, int) or self.n:
            self.start = self.base + self.n
        else:
            self.start = self.base
        self.base, self.n, self.per = self.start + turn * per, 0, per

    def leave(self, turns):
        assert self.n == self.per, f"{self.sem} per body: {self.n}, not {self.per}"
        self.base, self.n = self.start + turns * self.per, 0


PER_DVE = 23


def build(nc, ins, out, slots=SLOTS):
    (x, norm_mix_w, w_in, gdn_conv_w, gdn_a_log, gdn_dt_bias, gdn_norm_w, rg_conv_w, rg_conv_b, rg_w_rgate,
     rg_b_rgate, rg_w_igate, rg_b_igate, rg_lambda, rg_norm_w, w_out, norm_ffn_w, router_w_group,
     router_b_group, router_w_expert, router_b_expert, expert_w1, expert_w3, expert_w2, norm_final_w, const) = ins
    h_dram = nc.dram_tensor("h_rows", [T * 2, HD2], F32, kind="Internal").ap()
    tab_dram = nc.dram_tensor("slot_table", [SLOTS * NE, 2], F32, kind="Internal").ap()
    y_dram = nc.dram_tensor("expert_rows", [T * 4, HD2], F32, kind="Internal").ap()

    with ExitStack() as ctx:
        def sb(name, shape, dt=F32):
            return ctx.enter_context(nc.sbuf_tensor(name, shape, dt))

        def sem(name):
            return ctx.enter_context(nc.semaphore(name))

        bank = [ctx.enter_context(nc.psum_tensor(f"bank{i}", [P, 512], F32)) for i in range(8)]

        ew = sb("ew", [P, 6, 4096])
        fw = sb("fw", [P, 6 * 2048])
        hT = sb("hT", [P, KD, T])
        mixT = sb("mixT", [P, KD, T])
        cst = sb("cst", [P, C_END])
        ye = sb("ye", [P, 2, 1024])
        misc = sb("misc", [P, 2688])

        class Region:

            def __init__(self, ap, size):
                self.ap, self.size, self.at = ap, size, 0

            def take(self, *dims):
                n = int(np.prod(dims))
                a = self.ap[:, self.at:self.at + n]
                self.at += n
                assert self.at <= self.size, (self.at, self.size)
                if len(dims) == 1:
                    return a
                names = "abcd"[:len(dims)]
                return a.rearrange(f"p ({' '.join(names)}) -> p {' '.join(names)}", **dict(zip(names, dims)))

        fws = fw[:, :].rearrange("p (s k n) -> p s k n", s=6, k=KD)
        R1 = Region(ew[:, 4:6, :].rearrange("p a b -> p (a b)"), 8192)
        R2 = Region(ye[:, :, :].rearrange("p a b -> p (a b)"), 2048)
        R3 = Region(misc[:, :], 2688)
        cq = R1.take(3, T)
        th = R1.take(3, T)
        nat = R1.take(2, NT, HD)
        rhs = R1.take(2, NT, HD)
        kdec = R1.take(NT, HD)
        qkT = R1.take(NT, 2, P)
        dec = R1.take(NT, 2, P)
        aa = R1.take(NT, 2, P)
        atm = R1.take(LEVELS, NT, P)
        tt = R1.take(NT, 2, P)
        pm = R1.take(NT, P)
        nwT = R1.take(T)
        vn = R1.take(NT, HD)
        qg = R1.take(T)
        egb = R1.take(T)
        sq = R1.take(2, T)
        rr = R2.take(2, T)
        gexp = R2.take(NT, P)
        bm = R2.take(NT, P)
        xc = R2.take(T)
        gg = R2.take(T)
        sz = R2.take(T)
        zr = R2.take(T)
        lru = R3.take(6, T)
        thz = R3.take(T)
        xr = R3.take(T)
        gl2 = R3.take(T)
        S = R3.take(HD)
        rgw = R3.take(2, P)
        prm = sb("prm", [P, NQ, NH])
        pc = sb("pc", [P, NQ])
        ph = sb("ph", [P, NQ])
        gnw = sb("gnw", [P, 1])
        mixw = sb("mixw", [P, KD])
        ss4 = sb("ss4", [P, 4])
        sd4 = sb("sd4", [P, 4])
        r4 = sb("r4", [P, 4])
        eps_c = sb("eps_c", [P, 2])
        stat = sb("stat", [P, 8])
        rows = sb("rows", [16, 2, T])
        rsel = sb("rsel", [16, 2, T])
        R0 = Region(ew[:, 0:4, :].rearrange("p a b -> p (a b)"), 16384)
        xn = R0.take(NT, D)
        junk = R0.take(D)
        wba = R0.take(KD, 16)
        vec = R0.take(2, P)
        bar = R0.take(12, T)
        tkn = R0.take(4, NT, 16)
        lamt = R0.take(6, NH)
        par16 = R0.take(4)
        cmask = R0.take(T)
        wq_slot = [ew[:, 0:2, :], ew[:, 2:4, :], None, ew[:, 0:2, :]]
        wq_view = [None if a is None else a.rearrange("p a (k n) -> p (a k) n", n=512) for a in wq_slot]
        wq_view[2] = fw[:, 0:8192].rearrange("p (k n) -> p k n", n=512)
        x2 = fw[:, 8192:12288].rearrange("p (t d) -> p t d", t=NT)
        hn = fw[:, 0:4096].rearrange("p (t d) -> p t d", t=NT)
        wfin = fw[:, 4096:6144]
        wffn = ye[:, :, :].rearrange("p a b -> p (a b)")
        rw = fw[:, 6144:6144 + KD * 36].rearrange("p (k n) -> p k n", k=KD)
        rb = fw[:, 6720:6756]
        R4 = Region(fw[:, 6756:8192], 1436)
        lg = R4.take(NT, 8)
        le = R4.take(NT, NE)
        lm = R4.take(NT, NE)
        oh = R4.take(2, NT, NE)
        rk = R4.take(2, NT, NE)
        cnt = R4.take(NE)
        m8 = R4.take(NT, 8)
        i8 = R4.take(NT, 8)
        gts = R4.take(NT, 8)
        idf = R4.take(2, NT, 4)
        payload = R4.take(2, NT, 2)
        tabf = R4.take(NE, 2)
        fill = R4.take(32)
        gcur = sb("gcur", [P, 2], U32)
        scur = sb("scur", [P, 2], U32)
        gcol = sb("gcol", [P, NT, 2])
        i8u = sb("i8u", [P, NT, 8], U32)
        slot_f = sb("slot_f", [P, NT, 2])
        slot_u = sb("slot_u", [P, NT, 2], U32)
        gidx = sb("gidx", [P, NE], U32)
        sidx = sb("sidx", [P, NE], U32)
        nrounds = sb("nrounds", [P, 1], I32)
        R5 = Region(mixT[:, :, :].rearrange("p a b -> p (a b)"), 4096)
        xg = R5.take(2, HD2)
        xT = R5.take(KD // 2, P)
        hs = R5.take(FF)
        eth = R5.take(FC, SLOTS)
        gT = R5.take(FC, SLOTS)
        y2 = ew[:, 0:4, :].rearrange("p (t a) b -> p t (a b)", t=NT)

        ident = cst[:, C_ID:C_ID + P]
        ones = cst[:, C_ONE:C_ONE + P]

        s_cst = sem("s_cst")
        s_x = sem("s_x")
        s_vec = sem("s_vec")
        s_wba = sem("s_wba")
        s_win = [sem(f"s_win{b}") for b in range(6)]
        s_rgw = sem("s_rgw")
        s_init = sem("s_init")
        s_vecT = sem("s_vecT")
        s_xss = sem("s_xss")
        s_xh = sem("s_xh")
        s_xT = sem("s_xT")
        s_hT = sem("s_hT")
        s_hTa = sem("s_hTa")
        s_ba = sem("s_ba")
        s_bath = sem("s_bath")
        s_barow = sem("s_barow")
        s_lex = sem("s_lex")
        s_par = sem("s_par")
        s_alog = sem("s_alog")
        s_eg = sem("s_eg")
        s_tokT = sem("s_tokT")
        s_prm = sem("s_prm")
        s_proj = sem("s_proj")
        s_conv = sem("s_conv")
        s_th = sem("s_th")
        s_silu = sem("s_silu")
        s_evac = sem("s_evac")
        s_z = sem("s_z")
        s_rx = sem("s_rx")
        s_gsq = sem("s_gsq")
        s_gv = sem("s_gv")
        s_gth = sem("s_gth")
        s_gate = sem("s_gate")
        s_sel = sem("s_sel")
        s_gb = sem("s_gb")
        s_rgmm = sem("s_rgmm")
        s_ri = sem("s_ri")
        s_la = sem("s_la")
        s_a = sem("s_a")
        s_m2 = sem("s_m2")
        s_mu = sem("s_mu")
        s_y = sem("s_y")
        s_nat_mm = sem("s_nat_mm")
        s_ss = sem("s_ss")
        s_nat = sem("s_nat")
        s_vb = sem("s_vb")
        s_diff = sem("s_diff")
        s_exp = sem("s_exp")
        s_dec = sem("s_dec")
        s_kb = sem("s_kb")
        s_back = sem("s_back")
        s_qkT = sem("s_qkT")
        s_qg = sem("s_qg")
        s_kk = sem("s_kk")
        s_aa = sem("s_aa")
        s_atm = sem("s_atm")
        s_P = sem("s_P")
        s_Pc = sem("s_Pc")
        s_U = sem("s_U")
        s_T = sem("s_T")
        s_w = sem("s_w")
        s_nw = sem("s_nw")
        s_v = sem("s_v")
        s_vn = sem("s_vn")
        s_o = sem("s_o")
        s_S = sem("s_S")
        s_sq = sem("s_sq")
        s_nss = sem("s_nss")
        s_rt = sem("s_rt")
        s_mix = sem("s_mix")
        l_dve = sem("l_dve")
        l_act = sem("l_act")
        l_pool = sem("l_pool")
        s_wo = [sem(f"s_wo{n}") for n in range(4)]
        s_wod = sem("s_wod")
        s_x2r = sem("s_x2r")
        s_x2 = sem("s_x2")
        s_wffn = sem("s_wffn")
        s_rw = sem("s_rw")
        s_hss = sem("s_hss")
        s_hn = sem("s_hn")
        s_hrow = sem("s_hrow")
        s_h2T = sem("s_h2T")
        s_h2Ta = sem("s_h2Ta")
        s_h2mm = sem("s_h2mm")
        s_lgt = sem("s_lgt")
        s_gex = sem("s_gex")
        s_route = sem("s_route")
        s_oh = sem("s_oh")
        s_rank = sem("s_rank")
        s_nr = sem("s_nr")
        s_slot = sem("s_slot")
        s_idle = sem("s_idle")
        s_xz = sem("s_xz")
        s_tabz = sem("s_tabz")
        s_tabw = sem("s_tabw")
        s_tabl = sem("s_tabl")
        s_idx = sem("s_idx")
        s_ew = [sem(f"s_ew{b}") for b in range(6)]
        s_ed = sem("s_ed")
        s_xg = [sem("s_xg0"), sem("s_xg1")]
        s_xgT = sem("s_xgT")
        s_xeA = sem("s_xeA")
        s_xeD = sem("s_xeD")
        s_H = sem("s_H")
        s_hs = sem("s_hs")
        s_HT = sem("s_HT")
        s_eth = sem("s_eth")
        s_g = sem("s_g")
        s_Y = sem("s_Y")
        s_yeA = sem("s_yeA")
        s_yeD = sem("s_yeD")
        s_u = sem("s_u")
        s_sc = sem("s_sc")
        s_scur = sem("s_scur")
        s_y2 = sem("s_y2")
        s_fin = sem("s_fin")
        s_fss = sem("s_fss")
        s_frt = sem("s_frt")
        s_out = sem("s_out")

        block = ctx.enter_context(nc.Block())
        w_in_v = w_in[0].rearrange("(k p) n -> p k n", p=P)
        BLOCK_COL = [0, GW, 2 * GW, 3 * GW, 4 * GW + 2 * NH, 5 * GW + 2 * NH]
        x_v = x[0].rearrange("(t p) d -> p t d", p=P)
        w_out_v = w_out[0].rearrange("(k p) n -> p k n", p=P)
        out_v = out[0].rearrange("(t p) d -> p t d", p=P)
        CAP = slots

        @block.sync
        def _(sp):
            sp.dma_start(xn, x_v).then_inc(s_x, 16)
            sp.dma_start(cst[:, :], const).then_inc(s_cst, 16)
            rv = [(vec[0:96, 0, :], gdn_conv_w[0].rearrange("j (b h p) -> (j b h) p", p=P, h=NH)),
                  (vec[0:32, 1, :], rg_conv_w[0].rearrange("j (h p) -> (j h) p", p=P)),
                  (vec[32:40, 1, :], rg_conv_b[0].rearrange("(h p) -> h p", p=P)),
                  (vec[40:48, 1, :], rg_b_rgate[0].rearrange("(h p) -> h p", p=P)),
                  (vec[48:56, 1, :], rg_b_igate[0].rearrange("(h p) -> h p", p=P)),
                  (vec[56:64, 1, :], rg_lambda[0].rearrange("(h p) -> h p", p=P)),
                  (vec[64:72, 1, :], rg_norm_w[0].rearrange("(h p) -> h p", p=P)),
                  (vec[72:88, 1, :], norm_mix_w[0].rearrange("(h p) -> h p", p=P)),
                  (vec[88:89, 1, :], gdn_norm_w)]
            for to, of in rv:
                sp.dma_start(to, of).then_inc(s_vec, 16)
            sp.dma_start(wba, w_in_v[:, :, 4 * GW:4 * GW + 2 * NH]).then_inc(s_wba, 16)
            sp.wait_ge(s_init, 1)
            sp.dma_start(par16[8:16, 0:1], gdn_a_log.rearrange("a h -> h a")).then_inc(s_alog, 16)
            sp.dma_start(par16[8:16, 1:2], gdn_dt_bias.rearrange("a h -> h a")).then_inc(s_alog, 16)

            def load_block(h, b):
                sp.dma_start(fws[:, b], w_in_v[:, :, bass.ds(h * P + BLOCK_COL[b], P)]).then_inc(s_win[b], 16)

            def load_rg(h):
                sp.dma_start(rgw[:, 0, :], rg_w_rgate[0, h]).then_inc(s_rgw, 16)
                sp.dma_start(rgw[:, 1, :], rg_w_igate[0, h]).then_inc(s_rgw, 16)

            for b in range(6):
                load_block(0, b)
            load_rg(0)
            with sp.Fori(1, NH) as h:
                for b in range(6):
                    sp.wait_ge(s_proj, (h - 1) * 6 + b + 1)
                    load_block(h, b)
                sp.wait_ge(s_rgmm, h)
                load_rg(h)
            for n in range(4):
                if n == 0:
                    sp.wait_ge(s_prm, 1)
                if n == 2:
                    sp.wait_ge(s_proj, NH * 6)
                    sp.dma_start(x2, x_v).then_inc(s_x2r, 16)
                if n == 3:
                    sp.wait_ge(s_wod, 1)
                sp.dma_start(wq_view[n], w_out_v[:, :, n * 512:(n + 1) * 512]).then_inc(s_wo[n], 16)
            sp.wait_ge(s_mix, 2 * NH)
            sp.dma_start(wffn, norm_ffn_w.broadcast_to([P, D])).then_inc(s_wffn, 16)

            def load_expert(e, piece):
                half, which = piece // 2, piece % 2
                if piece < 4:
                    src = (expert_w1, expert_w3)[which][0, e].rearrange("(c k p) n -> p c k n", p=P, c=2)[:, half]
                    dst = ew[:, piece].rearrange("p (k n) -> p k n", n=FF)
                else:
                    src = expert_w2[0, e].rearrange("(c k p) n -> p c k n", p=P, c=2)[:, which]
                    dst = ew[:, piece].rearrange("p (k n) -> p k n", n=D)
                sp.dma_start(dst, src).then_inc(s_ew[piece], 16)

            sp.wait_ge(s_wod, 2)
            for piece in (2, 3, 4, 5):
                load_expert(0, piece)
            sp.wait_ge(s_wod, 3)
            sp.dma_start(wfin, norm_final_w.rearrange("(a d) -> a d", a=1).broadcast_to([P, D])).then_inc(s_rw, 16)
            sp.dma_start(rw[:, :, 0:NG], router_w_group[0].rearrange("(k p) n -> p k n", p=P)).then_inc(s_rw, 16)
            sp.dma_start(rw[:, :, NG:], router_w_expert[0].rearrange("(k p) n -> p k n", p=P)).then_inc(s_rw, 16)
            sp.dma_start(rb[:, 0:NG], router_b_group.broadcast_to([P, NG])).then_inc(s_rw, 16)
            sp.dma_start(rb[:, NG:], router_b_expert.broadcast_to([P, NE])).then_inc(s_rw, 16)
            sp.wait_ge(s_wod, 4)
            for piece in (0, 1):
                load_expert(0, piece)
            for t in range(NT):
                sp.wait_ge(s_hn, t + 1)
                sp.dma_start(h_dram.rearrange("(t p j) d -> p t (j d)", p=P, j=2)[:, t], hn[:, t]).then_inc(s_hrow, 16)
            sp.wait_ge(s_nr, 1)
            rounds = sp.value_load(nrounds[0:1, 0:1], min_val=1, max_val=T // CAP)
            with sp.Fori(0, rounds) as r:
                with sp.Fori(1, NE) as e:
                    for piece in range(6):
                        sp.wait_ge(s_ed, (r * NE + e - 1) * 6 + piece + 1)
                        load_expert(e, piece)
                with sp.If(r + 1 < rounds):
                    for piece in range(6):
                        sp.wait_ge(s_ed, (r * NE + NE - 1) * 6 + piece + 1)
                        load_expert(0, piece)
                sp.nop()
            sp.wait_ge(s_sc, rounds * (16 * NE))
            for t in range(NT):
                sp.dma_start(y2[:, t, 0:2 * D], y_dram.rearrange("(t p c) d -> p t (c d)", p=P, c=4)[:, t]).then_inc(s_y2, 16)
            for t in range(NT):
                sp.wait_ge(s_fin, t + 1)
                sp.dma_start(out_v[:, t], y2[:, t, 0:D]).then_inc(s_out, 16)
            sp.wait_ge(s_out, 16 * NT)

        @block.tensor
        def _(pe):
            def mm(o, l, r, start, stop):
                return nc.tensor.matmul(o, l, r, start=start, stop=stop, skip_group_check=True)

            def tr(o, i, n=P):
                return nc.tensor.transpose(o, i, ident[0:n, 0:n])

            pe.wait_ge(s_cst, 16)
            pe.wait_ge(s_vec, 16 * 9)
            tr(bank[7][:, 0:96], vec[0:96, 0, :], 96)
            tr(bank[7][:, 96:185], vec[0:89, 1, :], 89).then_inc(s_vecT, 1)
            for k2 in range(KD // 2):
                if k2 == 0:
                    pe.wait_ge(s_xh, NT)
                if k2 >= 4:
                    pe.wait_ge(s_hT if k2 % 2 == 0 else s_hTa, (k2 - 4) // 2 + 1)
                for k in range(2):
                    for t in range(NT):
                        l = tr(bank[k2 % 4][:, (k * NT + t) * P:(k * NT + t + 1) * P],
                               xn[:, t, (2 * k2 + k) * P:(2 * k2 + k + 1) * P])
                l.then_inc(s_xT, 1)
            pe.wait_ge(s_hT, 4)
            pe.wait_ge(s_hTa, 4)
            pe.wait_ge(s_wba, 16)
            for k in range(KD):
                l = mm(bank[4][0:16, 0:T], wba[:, k, :], hT[:, k, :], k == 0, k == KD - 1)
            l.then_inc(s_ba, 1)

            def project(h):
                for b in range(6):
                    o = bank[b % 2][:, 0:T]
                    pe.wait_ge(s_win[b], h * 16 + 16)
                    if b >= 2 or not isinstance(h, int):
                        pe.wait_ge(s_evac, h * 6 + b - 1)
                    for k in range(KD):
                        l = mm(o, fws[:, b, k, :], hT[:, k, :], k == 0, k == KD - 1)
                        if k == KD - 1:
                            l.then_inc(s_proj, 1)
                        yield

            def heads(h, fill):
                pe.wait_ge(s_rgw, h * 32 + 32)
                pe.wait_ge(s_rx, h + 1)
                mm(bank[5][:, 0:T], rgw[:, 0, :], xc, True, True)
                mm(bank[5][:, T:], rgw[:, 1, :], xc, True, True).then_inc(s_rgmm, 1)
                pe.wait_ge(s_silu, h * 3 + 3)
                for b in range(2):
                    for t in range(NT):
                        tr(bank[2][:, (b * NT + t) * P:(b * NT + t + 1) * P], cq[:, b, t * P:(t + 1) * P])
                for t in range(NT):
                    l = tr(bank[3][:, t * P:(t + 1) * P], cq[:, 2, t * P:(t + 1) * P])
                l.then_inc(s_nat_mm, 1)
                pe.wait_ge(s_sel, h + 1)
                mm(bank[6][:, :], cst[0:16, C_ONE:C_ONE + P], rsel[:, :, :].rearrange("p a b -> p (a b)"), True, True)\
                    .then_inc(s_gb, 1)
                fill(10)
                pe.wait_ge(s_nat, h + 1)
                for t in range(NT):
                    for b in range(2):
                        l = tr(bank[4][:, (t * 2 + b) * P:(t * 2 + b + 1) * P], nat[:, b, t, :])
                l.then_inc(s_back, 1)
                fill(4)
                pe.wait_ge(s_qkT, h + 1)
                for t in range(NT):
                    l = mm(bank[5][:, t * 2 * P:(t + 1) * 2 * P], qkT[:, t, 1, :],
                           qkT[:, t].rearrange("p a b -> p (a b)"), True, True)
                l.then_inc(s_kk, 1)
                fill(5)
                pe.wait_ge(s_atm, h * LEVELS + 1)
                for t in range(NT):
                    l = tr(bank[3][:, T + t * P:T + (t + 1) * P], atm[:, 0, t, :])
                l.then_inc(s_P, 1)
                fill(3)
                for lv in range(1, LEVELS):
                    pe.wait_ge(s_atm, h * LEVELS + lv + 1)
                    pe.wait_ge(s_T, h * LEVELS + lv)
                    for t in range(NT):
                        l = mm(bank[3][:, T + t * P:T + (t + 1) * P], atm[:, lv, t, :], tt[:, t, 0, :], True, True)
                    l.then_inc(s_P, 1)
                    fill(3)
                    pe.wait_ge(s_Pc, h * (LEVELS - 1) + lv)
                    for t in range(NT):
                        mm(bank[2][:, t * 2 * P:t * 2 * P + P], tt[:, t, 1, :], pm[:, t, :], True, True)
                        l = mm(bank[2][:, t * 2 * P + P:(t + 1) * 2 * P], pm[:, t, :], tt[:, t, 1, :], True, True)
                    l.then_inc(s_U, 1)
                    fill(3)
                pe.wait_ge(s_T, h * LEVELS + LEVELS)
                pe.wait_ge(s_kb, h * 2 + 2)
                pe.wait_ge(s_vb, h + 1)
                for t in range(NT):
                    l = mm(bank[6][:, t * P:(t + 1) * P], rhs[:, 1, t, :], tt[:, t, 1, :], True, True)
                l.then_inc(s_w, 1)
                fill(3)
                for c in range(NC):
                    t, lo = c // 2, c % 2 * CH
                    hi = lo + CH
                    l = mm(bank[5][lo:hi, 0:P], tt[lo:hi, t, 1, lo:hi], rhs[lo:hi, 0, t, :], True, c == 0)
                    if c:
                        pe.wait_ge(s_nw, h + 1)
                        pe.wait_ge(s_S, h * 3 + c)
                        l = mm(bank[5][lo:hi, 0:P], nwT[:, c * CH:(c + 1) * CH], S, False, True)
                    l.then_inc(s_v, 1)
                    fill(2)
                    pe.wait_ge(s_vn, h * NC + c + 1)
                    if c < NC - 1:
                        mm(bank[4][:, 0:HD], kdec[lo:hi, t, :], vn[lo:hi, t, :], True, True)
                    if c:
                        pe.wait_ge(s_qg, h + 1)
                        mm(bank[7][:, c * CH:(c + 1) * CH], S, qg[:, c * CH:(c + 1) * CH], True, False)
                    mm(bank[7][:, c * CH:(c + 1) * CH], vn[lo:hi, t, :], aa[lo:hi, t, 0, lo:hi], c == 0, True)\
                        .then_inc(s_o, 1)
                    fill(3)
                fill(4)
                pe.wait_ge(s_sq, h * 2 + 2)
                mm(bank[4][:, :], ones, sq.rearrange("p a b -> p (a b)"), True, True).then_inc(s_nss, 1)

            for _ in project(0):
                pass
            pe.wait_ge(s_eg, 1)
            for q in range(4):
                for t in range(NT):
                    l = tr(bank[7][:, (q * NT + t) * 16:(q * NT + t + 1) * 16],
                           bar[0:16, 8 + q, t * P:(t + 1) * P], 16)
            l.then_inc(s_tokT, 1)
            with pe.Fori(1, NH) as i:
                steps = project(i)

                def fill(n):
                    for _ in range(n):
                        next(steps, None)

                heads(i - 1, fill)
                for _ in steps:
                    pass

            def wo(n, chunks, last):
                for c in chunks:
                    for t in range(NT):
                        l = mm(bank[2 * n + t][:, :], mixT[:, c, t * P:(t + 1) * P], wq_view[n][:, c, :],
                               c == 0, c == KD - 1)
                        if last and c == chunks[-1] and t == NT - 1:
                            l.then_inc(s_wod, 1)
                        yield

            pe.wait_ge(s_wo[0], 16)
            pe.wait_ge(s_mix, 2 * (NH - 1))
            pe.wait_ge(s_evac, NH * 6)
            early = [c for c in range(KD) if c % NH != NH - 1]
            steps = wo(0, early, False)

            def fill_w(n):
                for _ in range(n):
                    next(steps, None)

            heads(NH - 1, fill_w)
            for _ in steps:
                pass
            pe.wait_ge(s_mix, 2 * NH)
            for _ in wo(0, [NH - 1, KD - 1], True):
                pass
            for n in range(1, 4):
                pe.wait_ge(s_wo[n], 16)
                for _ in wo(n, list(range(KD)), True):
                    pass
            for k2 in range(KD // 2):
                if k2 == 0:
                    pe.wait_ge(s_hn, NT)
                    pe.wait_ge(s_x2, 4)
                if k2 >= 4:
                    pe.wait_ge(s_h2T if k2 % 2 == 0 else s_h2Ta, (k2 - 4) // 2 + 1)
                for k in range(2):
                    for t in range(NT):
                        l = tr(bank[k2 % 4][:, (k * NT + t) * P:(k * NT + t + 1) * P],
                               hn[:, t, (2 * k2 + k) * P:(2 * k2 + k + 1) * P])
                l.then_inc(s_h2mm, 1)
            pe.wait_ge(s_rw, 16 * 5)
            pe.wait_ge(s_h2T, 4)
            pe.wait_ge(s_h2Ta, 4)
            for t in range(NT):
                for k in range(KD):
                    l = mm(bank[4][:, t * 64:t * 64 + NG + NE], hT[:, k, t * P:(t + 1) * P], rw[:, k, :],
                           k == 0, k == KD - 1)
            l.then_inc(s_lgt, 1)
            pe.wait_ge(s_oh, 1)
            for t in range(NT):
                for u in range(t + 1):
                    for q in range(2):
                        mm(bank[5][:, t * NE:(t + 1) * NE], cst[:, C_TRI:C_TRI + P] if u == t else ones,
                           oh[:, q, u, :], u == 0 and q == 0, u == t and q == 1)
            for u in range(NT):
                for q in range(2):
                    l = mm(bank[5][:, 2 * NE:3 * NE], ones, oh[:, q, u, :], u == 0 and q == 0, u == 1 and q == 1)
            l.then_inc(s_rank, 1)

            pe.wait_ge(s_nr, 1)
            rounds = pe.value_load(nrounds[0:1, 0:1], min_val=1, max_val=T // CAP)
            with pe.Fori(0, rounds) as r:
                with pe.Fori(0, NE // 2) as e2:
                    for j in range(2):
                        n = pe.snap(r * NE + e2 * 2 + j)
                        pe.wait_ge(s_xg[j], (r * (NE // 2) + e2) * 16 + 16)
                        for c in range(KD // 2):
                            l = tr(bank[c // 4][:, c % 4 * P:(c % 4 + 1) * P], xg[:, j, c * P:(c + 1) * P])
                            if c % 4 == 3:
                                l.then_inc(s_xgT, 1)
                        pe.wait_ge(s_xeA, n + 1)
                        pe.wait_ge(s_xeD, n + 1)
                        for half in range(2):
                            for which in range(2):
                                pe.wait_ge(s_ew[half * 2 + which], n * 16 + 16)
                            for k in range(KD // 2):
                                for which in range(2):
                                    l = mm(bank[2][which * 64:which * 64 + 64, :], xT[:, k, half * 64:half * 64 + 64],
                                           ew[:, half * 2 + which].rearrange("p (k n) -> p k n", n=FF)[:, k, :],
                                           half == 0 and k == 0, half == 1 and k == KD // 2 - 1)
                                    if k == KD // 2 - 1:
                                        l.then_inc(s_ed, 1)
                        pe.wait_ge(s_hs, n + 1)
                        for k in range(FC):
                            l = tr(bank[3][:, k * P:(k + 1) * P], hs[:, k * P:(k + 1) * P])
                        l.then_inc(s_HT, 1)
                        pe.wait_ge(s_g, n + 1)
                        for k in range(FC):
                            if k % 2 == 0:
                                pe.wait_ge(s_ew[4 + k // 2], n * 16 + 16)
                            w2 = ew[:, 4 + k // 2].rearrange("p (k n) -> p k n", n=D)
                            for i in range(2):
                                for half in range(2):
                                    col = half * HD2 + i * 512
                                    l = mm(bank[4 + i][half * 64:half * 64 + 64, :], gT[:, k, :],
                                           w2[:, k % 2, col:col + 512], k == 0, k == FC - 1)
                            if k % 2:
                                l.then_inc(s_ed, 1)

        @block.scalar
        def _(act):
            link = Link(act, l_act)
            act.wait_ge(s_x, 16)
            act.wait_ge(s_init, 1)
            for t in range(NT):
                link(act.activation(junk, xn[:, t], ACT.Square, accum_out=stat[:, t:t + 1]))
            act.activation(stat[:, 2:4], stat[:, 0:2], ACT.Sqrt, scale=1.0 / D, bias=eps_c[:, 0:1]).then_inc(s_xss, 1)
            act.wait_ge(s_par, 1)
            for k2 in range(1, KD // 2, 2):
                act.wait_ge(s_xT, k2 + 1)
                for k in range(2):
                    l = act.activation(hT[:, 2 * k2 + k, :], bank[k2 % 4][:, k * T:(k + 1) * T], ACT.Copy,
                                       scale=mixw[:, 2 * k2 + k:2 * k2 + k + 1])
                l.then_inc(s_hTa, 1)
            act.wait_ge(s_alog, 32)
            act.activation(par16[0:16, 2:3], par16[0:16, 0:1], ACT.Exp).then_inc(s_lex, 1)
            act.wait_ge(s_par, 2)
            act.activation(lamt[:, 1], lamt[:, 0], ACT.Exp, scale=-1.0).then_inc(s_lex, 1)
            act.wait_ge(s_ba, 1)
            act.activation(bar[0:16, 0], bank[4][0:16, 0:T], ACT.Tanh, scale=0.5).then_inc(s_bath, 1)
            act.wait_ge(s_barow, 1)
            act.activation(bar[0:16, 3], bar[0:16, 2], ACT.Exp, scale=-1.0).then_inc(s_bath, 1)
            act.wait_ge(s_barow, 2)
            act.activation(bar[0:16, 10], bar[0:16, 8], ACT.Exp)
            act.activation(bar[0:16, 11], bar[0:16, 7], ACT.Exp).then_inc(s_eg, 1)

            def evac(h, b):
                act.wait_ge(s_proj, h * 6 + b + 1)
                src = bank[b % 2][:, 0:T]
                if b == 3:
                    act.activation(thz, src, ACT.Tanh, scale=0.5)
                act.activation((th[:, 0], th[:, 1], th[:, 2], zr, xr, gg)[b], src, ACT.Copy).then_inc(s_evac, 1)

            def tanh_half(h, b):
                act.wait_ge(s_conv, h * 3 + b + 1)
                act.activation(th[:, b], cq[:, b], ACT.Tanh, scale=0.5).then_inc(s_th, 1)

            def heads(h, evac_next, tanh_next):
                act.wait_ge(s_evac, h * 6 + 6)
                act.activation(gl2, gg, ACT.Square, scale=GELU_C ** 0.5).then_inc(s_gsq, 1)
                act.wait_ge(s_rgmm, h + 1)
                act.wait_ge(s_sel, h + 1)
                act.activation(lru[:, 0], bank[5][:, 0:T], ACT.Tanh, scale=0.5, bias=ph_bias(0)).then_inc(s_ri, 1)
                act.activation(lru[:, 1], bank[5][:, T:], ACT.Tanh, scale=0.5, bias=ph_bias(1)).then_inc(s_ri, 1)
                act.wait_ge(s_gb, h + 1)
                act.activation(egb, bank[6][:, 0:T], ACT.Exp).then_inc(s_exp, 1)
                act.wait_ge(s_diff, h + 1)
                act.activation(gexp, gexp, ACT.Exp).then_inc(s_exp, 1)
                act.wait_ge(s_la, h + 1)
                act.activation(lru[:, 3], lru[:, 2], ACT.Exp)
                act.activation(lru[:, 4], lru[:, 2], ACT.Exp, scale=2.0)
                act.activation(lru[:, 5], lru[:, 2], ACT.Tanh).then_inc(s_a, 1)
                act.wait_ge(s_gv, h + 1)
                act.activation(gl2, gl2, ACT.Tanh, scale=GELU_S).then_inc(s_gth, 1)
                act.wait_ge(s_nat_mm, h + 1)
                for q in range(4):
                    l = act.activation(sq[:, 0, 0:P], bank[2][:, q * P:(q + 1) * P], ACT.Square,
                                       accum_out=ss4[:, q:q + 1])
                    link(l)
                act.activation(sd4[:, :], ss4[:, :], ACT.Sqrt, bias=eps_c[:, 1:2]).then_inc(s_ss, 1)
                act.wait_ge(s_m2, h + 1)
                act.activation(lru[:, 4], lru[:, 5], ACT.Sqrt, scale=-1.0).then_inc(s_mu, 1)
                act.wait_ge(s_back, h + 1)
                act.activation(qkT, bank[4][:, :].rearrange("p (t b i) -> p t b i", t=NT, b=2), ACT.Copy)\
                    .then_inc(s_qkT, 1)
                evac_next(0)
                for lv in range(1, LEVELS):
                    act.wait_ge(s_P, h * LEVELS + lv + 1)
                    act.activation(pm, bank[3][:, T:].rearrange("p (t i) -> p t i", t=NT), ACT.Copy).then_inc(s_Pc, 1)
                    if lv == 2:
                        tanh_next(0)
                        evac_next(1)
                    if lv == 4:
                        tanh_next(1)
                evac_next(2)
                act.wait_ge(s_w, h + 1)
                act.activation(nwT, bank[6][:, 0:T], ACT.Copy, scale=-1.0).then_inc(s_nw, 1)
                for c in range(NC):
                    lo = c % 2 * CH
                    act.wait_ge(s_v, h * NC + c + 1)
                    act.activation(vn[lo:lo + CH, c // 2, :], bank[5][lo:lo + CH, 0:P], ACT.Copy).then_inc(s_vn, 1)
                    if c == 1:
                        tanh_next(2)
                        evac_next(3)
                act.wait_ge(s_y, h + 1)
                act.activation(sq[:, 1], lru[:, 1], ACT.Square, scale=0.5).then_inc(s_sq, 1)
                act.wait_ge(s_o, h * NC + NC)
                act.activation(sq[:, 0], bank[7][:, 0:T], ACT.Square).then_inc(s_sq, 1)
                act.wait_ge(s_nss, h + 1)
                act.activation(rr, bank[4][:, :].rearrange("p (a b) -> p a b", a=2), ACT.Sqrt,
                               scale=1.0 / HD, bias=eps_c[:, 0:1]).then_inc(s_rt, 1)
                evac_next(4)
                evac_next(5)

            def ph_bias(i):
                return ph[:, Q_BR + i:Q_BR + i + 1]

            for b in range(6):
                evac(0, b)
                if 1 <= b <= 3:
                    tanh_half(0, b - 1)
            PER = 4
            with act.Fori(1, NH) as i:
                link.enter(i - 1, PER)
                heads(i - 1, lambda b: evac(i, b), lambda b: tanh_half(i, b))
                link.leave(NH - 1)
            heads(NH - 1, lambda b: None, lambda b: None)

            act.wait_ge(s_x2, 4)
            for t in range(NT):
                link(act.activation(hn[:, t], x2[:, t], ACT.Square, accum_out=stat[:, t:t + 1]))
            act.activation(stat[:, 2:4], stat[:, 0:2], ACT.Sqrt, scale=1.0 / D, bias=eps_c[:, 0:1]).then_inc(s_hss, 1)
            for k2 in range(1, KD // 2, 2):
                act.wait_ge(s_h2mm, k2 + 1)
                act.activation(hT[:, 2 * k2:2 * k2 + 2, :], bank[k2 % 4][:, :].rearrange("p (k i) -> p k i", k=2),
                               ACT.Copy).then_inc(s_h2Ta, 1)
            act.wait_ge(s_gex, 1)
            for t in range(NT):
                act.activation(le[:, t, 0:NG], lg[:, t, 0:NG], ACT.Exp, bias=gts[:, t, 0:1],
                               accum_out=gts[:, t, 1:2])
                l = act.activation(gts[:, t, 3:4], gts[:, t, 2:3], ACT.Exp)
            l.then_inc(s_route, 1)

            act.wait_ge(s_nr, 1)
            rounds = act.value_load(nrounds[0:1, 0:1], min_val=1, max_val=T // CAP)
            with act.Fori(0, rounds) as r:
                with act.Fori(0, NE // 2) as e2:
                    for j in range(2):
                        n = act.snap(r * NE + e2 * 2 + j)
                        act.wait_ge(s_xgT, n * 2 + 2)
                        act.activation(xT[:, 4:8, :], bank[1][:, :].rearrange("p (k i) -> p k i", k=4), ACT.Copy)\
                            .then_inc(s_xeA, 1)
                        act.wait_ge(s_ed, n * 6 + 4)
                        act.activation(hs, bank[2][:, :], ACT.Copy).then_inc(s_hs, 1)
                        act.wait_ge(s_HT, n + 1)
                        act.activation(eth, bank[3][:, :].rearrange("p (k i) -> p k i", k=FC)[:, :, 0:SLOTS],
                                       ACT.Tanh, scale=0.5).then_inc(s_eth, 1)
                        act.wait_ge(s_ed, n * 6 + 6)
                        act.activation(ye[:, j, 512:], bank[5][:, :], ACT.Copy).then_inc(s_yeA, 1)
            for t in range(NT):
                act.wait_ge(s_fss, t + 1)
                link(act.activation(hn[:, t], y2[:, t, 0:D], ACT.Square, accum_out=stat[:, t:t + 1]))
                act.activation(stat[:, 2 + t:3 + t], stat[:, t:t + 1], ACT.Sqrt, scale=1.0 / D,
                               bias=eps_c[:, 0:1]).then_inc(s_frt, 1)



        @block.vector
        def _(dve):
            link = Link(dve, l_dve)
            V = nc.vector

            def log1p(out_, u, tmp, x2_, r_):
                link(V.tensor_scalar(tmp, u, 2.0, None, ALU.add))
                link(V.reciprocal(r_, tmp))
                link(V.tensor_tensor(tmp, u, r_, ALU.mult))
                link(V.tensor_tensor(x2_, tmp, tmp, ALU.mult))
                link(V.tensor_scalar(r_, x2_, 2.0 / 15, None, ALU.mult))
                for c in (13, 11, 9, 7, 5, 3):
                    link(V.scalar_tensor_tensor(r_, r_, 2.0 / c, x2_, ALU.add, ALU.mult))
                link(V.scalar_tensor_tensor(out_, r_, 2.0, tmp, ALU.add, ALU.mult))

            V.memset(eps_c[:, 0:1], EPS)
            V.memset(eps_c[:, 1:2], 4 * EPS)
            link(V.memset(par16, 0.0))
            link(V.memset(cmask, 1.0))
            V.memset(cmask.rearrange("p (c i) -> p c i", c=NC)[:, :, 0:1], 0.0).then_inc(s_init, 1)
            dve.wait_ge(s_vecT, 1)
            V.tensor_copy(mixw[:, :], bank[7][:, 168:184]).then_inc(s_par, 1)
            link(V.tensor_copy(lamt[:, 1], bank[7][:, 152:160]))
            V.scalar_tensor_tensor(lamt[:, 0], lamt[:, 1], -1.0, lamt[:, 1], ALU.mult, ALU.max).then_inc(s_par, 1)
            V.tensor_scalar(lamt[:, 2], bank[7][:, 152:160], -1.0, 0.0, ALU.mult, ALU.max)
            V.tensor_copy(prm[:, 0:Q_BR, :], bank[7][:, 0:Q_BR * NH].rearrange("p (q h) -> p q h", h=NH))
            V.tensor_scalar(prm[:, Q_BR:Q_LAM, :], bank[7][:, Q_BR * NH:Q_LAM * NH].rearrange("p (q h) -> p q h", h=NH),
                            0.5, None, ALU.mult)
            V.tensor_scalar(prm[:, Q_RGN, :], bank[7][:, 160:168], 0.5, None, ALU.mult)
            V.tensor_scalar(gnw[:, :], bank[7][:, 184:185], 0.5, None, ALU.mult)
            dve.wait_ge(s_xss, 1)
            link(V.reciprocal(stat[:, 4:6], stat[:, 2:4]))
            for t in range(NT):
                V.tensor_scalar(xn[:, t], xn[:, t], stat[:, 4 + t:5 + t], None, ALU.mult).then_inc(s_xh, 1)
            for k2 in range(0, KD // 2, 2):
                dve.wait_ge(s_xT, k2 + 1)
                for k in range(2):
                    l = V.tensor_scalar(hT[:, 2 * k2 + k, :], bank[k2 % 4][:, k * T:(k + 1) * T],
                                        mixw[:, 2 * k2 + k:2 * k2 + k + 1], None, ALU.mult)
                l.then_inc(s_hT, 1)
            dve.wait_ge(s_lex, 2)
            log1p(lamt[:, 3], lamt[:, 1], lamt[:, 4], lamt[:, 5], lamt[:, 0])
            link(V.tensor_tensor(lamt[:, 4], lamt[:, 2], lamt[:, 3], ALU.add))
            V.tensor_scalar(prm[:, Q_LAM, :], lamt[:, 4], -0.5 * 8.0, None, ALU.mult)
            B = [bar[0:16, i] for i in range(12)]
            dve.wait_ge(s_bath, 1)
            dve.wait_ge(s_alog, 32)
            link(V.tensor_scalar(B[9], B[0], 0.5, 0.5, ALU.mult, ALU.add))
            link(V.tensor_scalar(B[1], bank[4][0:16, 0:T], par16[0:16, 1:2], None, ALU.add))
            V.scalar_tensor_tensor(B[2], B[1], -1.0, B[1], ALU.mult, ALU.max).then_inc(s_barow, 1)
            V.tensor_scalar(B[4], B[1], 0.0, None, ALU.max)
            V.tensor_copy(rows[:, 1], B[9])
            link(V.tensor_scalar(par16[0:16, 3:4], par16[0:16, 2:3], -1.0, None, ALU.mult))
            dve.wait_ge(s_bath, 2)
            log1p(B[6], B[3], B[5], B[7], B[0])
            link(V.tensor_tensor(B[5], B[4], B[6], ALU.add))
            link(V.tensor_scalar(B[6], B[5], par16[0:16, 3:4], None, ALU.mult))
            link(V.tensor_tensor_scan(B[8], cmask[0:16, :], B[6], 0.0, ALU.mult, ALU.add))
            link(V.tensor_copy(rows[:, 0], B[8]))
            b8 = B[8].rearrange("p (c i) -> p c i", c=NC)
            V.tensor_tensor(B[7].rearrange("p (c i) -> p c i", c=NC), b8[:, :, CH - 1:CH].broadcast_to([16, NC, CH]),
                            b8, ALU.subtract).then_inc(s_barow, 1)

            def conv_taps(h, o, src, q, step):
                for j in range(TAPS - 1, -1, -1):
                    s = TAPS - 1 - j
                    if s == 0:
                        if q == "rx":
                            i = V.tensor_scalar(o, src, pc[:, Q_RGC + j:Q_RGC + j + 1], pc[:, Q_CB:Q_CB + 1],
                                                ALU.mult, ALU.add)
                        else:
                            i = V.tensor_scalar(o, src, pc[:, j * 3 + q:j * 3 + q + 1], None, ALU.mult)
                        link(i)
                    else:
                        w = pc[:, Q_RGC + j:Q_RGC + j + 1] if q == "rx" else pc[:, j * 3 + q:j * 3 + q + 1]
                        i = V.scalar_tensor_tensor(o[:, s:], src[:, 0:T - s], w, o[:, s:], ALU.mult, ALU.add)
                        if s < TAPS - 1:
                            link(i)
                i.then_inc(step, 1)

            def params(h):
                link(V.tensor_copy(pc[:, 0:Q_BR], prm[:, 0:Q_BR, h]))

            def conv(h, b):
                dve.wait_ge(s_evac, h * 6 + b + 1)
                conv_taps(h, cq[:, b], th[:, b], b, s_conv)

            def silu(h, b):
                dve.wait_ge(s_th, h * 3 + b + 1)
                V.scalar_tensor_tensor(cq[:, b], th[:, b], 1.0, cq[:, b], ALU.add, ALU.mult).then_inc(s_silu, 1)

            def conv_rx(h):
                dve.wait_ge(s_evac, h * 6 + 5)
                conv_taps(h, xc, xr, "rx", s_rx)

            def silu_z(h):
                V.scalar_tensor_tensor(sz, thz, 1.0, zr, ALU.add, ALU.mult).then_inc(s_z, 1)

            def select(h):
                link(V.tensor_copy(ph[:, :], prm[:, :, h]))
                link(V.tensor_scalar(rsel[:, 0], rows[:, 0], cst[0:16, bass.ds(h + (C_SEL + NH), 1)], None, ALU.mult))
                V.tensor_scalar(rsel[:, 1], rows[:, 1], cst[0:16, bass.ds(h + C_SEL, 1)], None, ALU.mult)\
                    .then_inc(s_sel, 1)

            def heads(h, pre):
                dve.wait_ge(s_gsq, h + 1)
                V.scalar_tensor_tensor(gl2, gl2, 1.0, gg, ALU.add, ALU.mult).then_inc(s_gv, 1)
                dve.wait_ge(s_exp, h * 2 + 1)
                for t in range(NT):
                    V.tensor_scalar(gexp[:, t], bank[6][:, t * P:(t + 1) * P], ph[:, Q_GC + t:Q_GC + t + 1], 0.0,
                                    ALU.subtract, ALU.min)
                V.tensor_tensor(bm, bank[6][:, T:].rearrange("p (t i) -> p t i", t=NT),
                                cst[:, C_MS:C_MS + P].rearrange("p (a i) -> p a i", a=1).broadcast_to([P, NT, P]),
                                ALU.mult).then_inc(s_diff, 1)
                dve.wait_ge(s_ri, h * 2 + 2)
                V.tensor_scalar(lru[:, 2], lru[:, 0], 1.0, ph[:, Q_LAM:Q_LAM + 1], ALU.add, ALU.mult).then_inc(s_la, 1)
                dve.wait_ge(s_ss, h + 1)
                link(V.reciprocal(r4[:, :], sd4[:, :]))
                V.tensor_tensor(nat.rearrange("p b t i -> p (b t) i"), bank[2][:, :].rearrange("p (q i) -> p q i", q=4),
                                r4[:, :].rearrange("p (q a) -> p q a", a=1).broadcast_to([P, 4, P]), ALU.mult)\
                    .then_inc(s_nat, 1)
                V.tensor_tensor(rhs[:, 0], bank[3][:, 0:T].rearrange("p (t i) -> p t i", t=NT),
                                ph[:, Q_VB:Q_VB + NT].rearrange("p (q a) -> p q a", a=1).broadcast_to([P, NT, P]),
                                ALU.mult).then_inc(s_vb, 1)
                dve.wait_ge(s_gth, h + 1)
                link(V.scalar_tensor_tensor(gg, gl2, 1.0, gg, ALU.add, ALU.mult))
                dve.wait_ge(s_a, h + 1)
                V.scalar_tensor_tensor(lru[:, 5], lru[:, 4], 1.0, lru[:, 5], ALU.add, ALU.mult).then_inc(s_m2, 1)
                dve.wait_ge(s_qkT, h + 1)
                V.scalar_tensor_tensor(qg.rearrange("p (t i) -> p t i", t=NT),
                                       bank[4][:, :].rearrange("p (t b i) -> p t b i", t=NT, b=2)[:, :, 0, :], QSCALE,
                                       egb.rearrange("p (t i) -> p t i", t=NT), ALU.mult, ALU.mult).then_inc(s_qg, 1)
                dve.wait_ge(s_kk, h + 1)
                dve.wait_ge(s_dec, h * 2 + 2)
                V.tensor_tensor(aa.rearrange("p t b i -> p (t b i)"), bank[5][:, :],
                                dec.rearrange("p t b i -> p (t b i)"), ALU.mult).then_inc(s_aa, 1)
                pre(0)
                idb = ident.rearrange("p (a i) -> p a i", a=1).broadcast_to([P, NT, P])
                dve.wait_ge(s_atm, h * LEVELS + 1)
                link(V.tensor_tensor(tt[:, :, 1, :], idb, atm[:, 0], ALU.subtract))
                dve.wait_ge(s_P, h * LEVELS + 1)
                V.tensor_tensor(tt[:, :, 0, :], idb, bank[3][:, T:].rearrange("p (t i) -> p t i", t=NT),
                                ALU.subtract).then_inc(s_T, 1)
                link(V.scalar_tensor_tensor(lru[:, 1], lru[:, 1], 1.0, xc, ALU.add, ALU.mult))
                dve.wait_ge(s_mu, h + 1)
                link(V.scalar_tensor_tensor(lru[:, 2], lru[:, 1], 0.5, lru[:, 4], ALU.mult, ALU.mult))
                link(V.tensor_tensor_scan(lru[:, 0], lru[:, 3], lru[:, 2], 0.0, ALU.mult, ALU.add))
                V.tensor_tensor(lru[:, 1], lru[:, 0], gg, ALU.mult).then_inc(s_y, 1)
                for lv in range(1, LEVELS):
                    dve.wait_ge(s_U, h * (LEVELS - 1) + lv)
                    V.tensor_tensor(tt.rearrange("p t b i -> p (t b i)"), tt.rearrange("p t b i -> p (t b i)"),
                                    bank[2][:, :], ALU.subtract).then_inc(s_T, 1)
                    if lv == 2:
                        pre(1)
                    if lv == 4:
                        pre(2)
                for c in range(NC - 1):
                    dve.wait_ge(s_o, h * NC + c + 1)
                    if c == 0:
                        V.tensor_copy(S, bank[4][:, 0:HD]).then_inc(s_S, 1)
                    else:
                        V.scalar_tensor_tensor(S, S, egb[:, c * CH + CH - 1:c * CH + CH], bank[4][:, 0:HD],
                                               ALU.mult, ALU.add).then_inc(s_S, 1)
                    if c == 0:
                        pre(3)
                    if c == 2:
                        pre(4)
                dve.wait_ge(s_sq, h * 2 + 2)
                link(V.scalar_tensor_tensor(qg, bank[7][:, 0:T], gnw[:, 0:1], sz, ALU.mult, ALU.mult))
                dve.wait_ge(s_rt, h + 1)
                link(V.reciprocal(rr.rearrange("p a b -> p (a b)"), rr.rearrange("p a b -> p (a b)")))
                V.tensor_tensor(mixT[:, h, :], qg, rr[:, 0], ALU.mult).then_inc(s_mix, 1)
                V.scalar_tensor_tensor(mixT[:, h + NH, :], lru[:, 1], ph[:, Q_RGN:Q_RGN + 1], rr[:, 1],
                                       ALU.mult, ALU.mult).then_inc(s_mix, 1)

            params(0)
            for b in range(3):
                conv(0, b)
                silu(0, b)
            conv_rx(0)
            silu_z(0)
            dve.wait_ge(s_tokT, 1)
            link(V.tensor_copy(tkn, bank[7][:, 0:P].rearrange("p (q t i) -> p q t i", q=4, t=NT)))
            V.tensor_copy(prm[:, Q_GC:Q_GC + NT, :], tkn[:, 0, :, NH:])
            V.tensor_scalar(prm[:, Q_VB:Q_VB + NT, :], tkn[:, 1, :, 0:NH], 0.5, None, ALU.mult)
            V.tensor_copy(prm[:, Q_KDEC:Q_KDEC + NT, :], tkn[:, 3, :, NH:])
            V.tensor_tensor(prm[:, Q_KB:Q_KB + NT, :], tkn[:, 1, :, 0:NH], tkn[:, 2, :, NH:], ALU.mult)\
                .then_inc(s_prm, 1)
            dve.wait_ge(s_prm, 1)
            select(0)
            with dve.Fori(1, NH) as i:
                link.enter(i - 1, PER_DVE)

                def pre(n):
                    if n == 0:
                        params(i)
                        conv(i, 0)
                    elif n == 1:
                        silu(i, 0)
                        conv(i, 1)
                    elif n == 2:
                        silu(i, 1)
                    elif n == 3:
                        conv(i, 2)
                    elif n == 4:
                        silu(i, 2)

                heads(i - 1, pre)
                conv_rx(i)
                silu_z(i)
                select(i)
                link.leave(NH - 1)
            heads(NH - 1, lambda n: None)

            dve.wait_ge(s_x2r, 16)
            for n in range(4):
                dve.wait_ge(s_wod, n + 1)
                for t in range(NT):
                    l = V.tensor_tensor(x2[:, t, n * 512:(n + 1) * 512], x2[:, t, n * 512:(n + 1) * 512],
                                        bank[2 * n + t][:, :], ALU.add)
                l.then_inc(s_x2, 1)
            V.memset(lg, -3.0e38)
            V.memset(fill, NONE).then_inc(s_tabz, 1)
            for k in range(2):
                for t in range(NT):
                    V.tensor_scalar(payload[:, k, t, 0:1], cst[:, C_COL + 2:C_COL + 3], 2.0 * P * t, None, ALU.add)
                    l = V.tensor_scalar(payload[:, k, t, 1:2], cst[:, C_COL + 3:C_COL + 4], 4.0 * P * t + 2 * k, None,
                                        ALU.add)
            link(l)
            dve.wait_ge(s_hss, 1)
            dve.wait_ge(s_wffn, 16)
            link(V.reciprocal(stat[:, 4:6], stat[:, 2:4]))
            for t in range(NT):
                V.scalar_tensor_tensor(hn[:, t], x2[:, t], stat[:, 4 + t:5 + t], wffn, ALU.mult, ALU.mult)\
                    .then_inc(s_hn, 1)
            for k2 in range(0, KD // 2, 2):
                dve.wait_ge(s_h2mm, k2 + 1)
                V.tensor_copy(hT[:, 2 * k2:2 * k2 + 2, :], bank[k2 % 4][:, :].rearrange("p (k i) -> p k i", k=2))\
                    .then_inc(s_h2T, 1)
            dve.wait_ge(s_lgt, 1)
            lgp = bank[4][:, 0:P].rearrange("p (t i) -> p t i", t=NT)
            rbb = rb.rearrange("p (a i) -> p a i", a=1).broadcast_to([P, NT, NG + NE])
            link(V.tensor_tensor(lg[:, :, 0:NG], lgp[:, :, 0:NG], rbb[:, :, 0:NG], ALU.add))
            link(V.tensor_tensor(le, lgp[:, :, NG:NG + NE], rbb[:, :, NG:], ALU.add))
            for t in range(NT):
                link(V.max(m8[:, t], lg[:, t]))
                V.tensor_scalar(gts[:, t, 0:1], m8[:, t, 0:1], -1.0, None, ALU.mult)
                link(V.max_index(i8u[:, t], m8[:, t], lg[:, t]))
                link(V.tensor_copy(i8[:, t], i8u[:, t]))
                link(V.tensor_scalar(lm[:, t], cst[:, C_GRP:C_GRP + NE], i8[:, t, 0:1], -1.0e30,
                                     ALU.not_equal, ALU.mult))
                link(V.tensor_tensor(lm[:, t], lm[:, t], le[:, t], ALU.add))
                link(V.max(m8[:, t], lm[:, t]))
                link(V.tensor_tensor(gts[:, t, 2:3], m8[:, t, 1:2], m8[:, t, 0:1], ALU.subtract))
                if t == 0:
                    link(V.max_index(i8u[:, t], m8[:, t], lm[:, t]))
                else:
                    V.max_index(i8u[:, t], m8[:, t], lm[:, t]).then_inc(s_gex, 1)
                    dve.wait_ge(s_gex, 1)
                link(V.tensor_copy(i8[:, t], i8u[:, t]))
                for k in range(2):
                    l = V.tensor_scalar(oh[:, k, t], cst[:, C_IO:C_IO + NE], i8[:, t, k:k + 1], None, ALU.is_equal)
                if t == 0:
                    link(l)
            l.then_inc(s_oh, 1)
            dve.wait_ge(s_route, 1)
            link(V.tensor_scalar(gts[:, :, 4:5], gts[:, :, 3:4], 1.0, None, ALU.add))
            link(V.tensor_tensor(gts[:, :, 5:6], gts[:, :, 4:5], gts[:, :, 1:2], ALU.mult))
            link(V.reciprocal(gcol[:, :, 0:1], gts[:, :, 5:6]))
            link(V.tensor_tensor(gcol[:, :, 1:2], gcol[:, :, 0:1], gts[:, :, 3:4], ALU.mult))
            dve.wait_ge(s_rank, 1)
            for k in range(2):
                for t in range(NT):
                    link(V.tensor_tensor_reduce(rk[:, k, t], oh[:, k, t], bank[5][:, t * NE:(t + 1) * NE], 1.0, 0.0,
                                                ALU.mult, ALU.add, idf[:, 0, t, k:k + 1]))
            link(V.tensor_reduce(idf[:, 1, 0, 0:1], bank[5][:, 2 * NE:3 * NE], AX.X, ALU.max))
            link(V.tensor_scalar(idf[:, 1, 0, 1:2], idf[:, 1, 0, 0:1], float(CAP), 1.0, ALU.is_gt, ALU.add))
            for q in range(2, T // CAP):
                link(V.scalar_tensor_tensor(idf[:, 1, 0, 1:2], idf[:, 1, 0, 0:1], float(q * CAP), idf[:, 1, 0, 1:2],
                                            ALU.is_gt, ALU.add))
            V.tensor_copy(nrounds[:, :], idf[:, 1, 0, 1:2]).then_inc(s_nr, 1)
            dve.wait_ge(s_nr, 1)
            rounds = dve.value_load(nrounds[0:1, 0:1], min_val=1, max_val=T // CAP)
            rank, in_cap, slot = idf[:, 0, :, 0:2], idf[:, 1, :, 2:4], idf[:, 0, :, 2:4]
            with dve.Fori(0, rounds) as r:
                link.enter(r, 8)
                link(V.tensor_scalar(in_cap, rank, 0.0, None, ALU.is_ge))
                link(V.scalar_tensor_tensor(in_cap, rank, float(CAP), in_cap, ALU.is_lt, ALU.mult))
                link(V.scalar_tensor_tensor(slot, rank, float(NE), i8[:, :, 0:2], ALU.mult, ALU.add))
                link(V.scalar_tensor_tensor(slot, slot, -NONE, in_cap, ALU.add, ALU.mult))
                link(V.tensor_scalar(slot_u[:, :, :], slot, NONE, None, ALU.add))
                link(V.tensor_scalar(rank, rank, -float(CAP), None, ALU.add))
                V.tensor_copy(slot_f[:, :, :], slot).then_inc(s_slot, 1)
                dve.wait_ge(s_tabl, (r + 1) * 32)
                link(V.tensor_scalar(gidx[:, :], tabf[:, :, 0], cst[:, C_COL + 1:C_COL + 2], None, ALU.add))
                link(V.tensor_scalar(sidx[:, :], tabf[:, :, 1], cst[:, C_COL + 1:C_COL + 2], None, ALU.add))
                V.tensor_copy(slot_f[:, :, :], slot).then_inc(s_idx, 1)
                with dve.Fori(0, NE // 2) as e2:
                    for j in range(2):
                        n = dve.snap(r * NE + e2 * 2 + j)
                        dve.wait_ge(s_xgT, n * 2 + 1)
                        V.tensor_copy(xT[:, 0:4, :], bank[0][:, :].rearrange("p (k i) -> p k i", k=4)).then_inc(s_xeD, 1)
                        dve.wait_ge(s_eth, n + 1)
                        b3 = bank[3][:, :].rearrange("p (k i) -> p k i", k=FC)
                        V.scalar_tensor_tensor(eth, eth, 1.0, b3[:, :, 0:SLOTS], ALU.add, ALU.mult).then_inc(s_u, 1)
                        dve.wait_ge(s_u, n + 1)
                        V.scalar_tensor_tensor(gT, eth, 0.5, b3[:, :, SLOTS:], ALU.mult, ALU.mult).then_inc(s_g, 1)
                        dve.wait_ge(s_ed, n * 6 + 6)
                        V.tensor_copy(ye[:, j, 0:512], bank[4][:, :]).then_inc(s_yeD, 1)
                link.leave(rounds)
            for t in range(NT):
                dve.wait_ge(s_y2, 16 * NT)
                link(V.scalar_tensor_tensor(y2[:, t, 0:D], y2[:, t, 0:D], gcol[:, t, 0:1], x2[:, t], ALU.mult, ALU.add))
                V.scalar_tensor_tensor(y2[:, t, 0:D], y2[:, t, D:2 * D], gcol[:, t, 1:2], y2[:, t, 0:D],
                                       ALU.mult, ALU.add).then_inc(s_fss, 1)
            for t in range(NT):
                dve.wait_ge(s_frt, t + 1)
                link(V.reciprocal(stat[:, 4 + t:5 + t], stat[:, 2 + t:3 + t]))
                V.scalar_tensor_tensor(y2[:, t, 0:D], y2[:, t, 0:D], stat[:, 4 + t:5 + t], wfin, ALU.mult, ALU.mult)\
                    .then_inc(s_fin, 1)

        @block.gpsimd
        def _(pool):
            G = nc.gpsimd

            def wait(of, value):
                pool.wait_ge(of, value)
                pool.sem_inc(s_idle, 1)

            def heads(h):
                pool.wait_ge(s_exp, h * 2 + 2)
                mq = cst[:, C_MQ:C_MQ + P].rearrange("p (a i) -> p a i", a=1).broadcast_to([P, NT, P])
                G.tensor_tensor(dec[:, :, 0, :], gexp, mq, ALU.mult).then_inc(s_dec, 1)
                G.tensor_tensor(dec[:, :, 1, :], gexp, bm, ALU.mult).then_inc(s_dec, 1)
                pool.wait_ge(s_nat, h + 1)
                for o, q in ((rhs[:, 1], Q_KB), (kdec, Q_KDEC)):
                    G.tensor_tensor(o, nat[:, 1], ph[:, q:q + NT].rearrange("p (q a) -> p q a", a=1)
                                    .broadcast_to([P, NT, P]), ALU.mult).then_inc(s_kb, 1)
                pool.wait_ge(s_aa, h + 1)
                for lv in range(LEVELS):
                    m = cst[:, C_LV + lv * P:C_LV + (lv + 1) * P].rearrange("p (a i) -> p a i", a=1)
                    G.tensor_tensor(atm[:, lv], aa[:, :, 1, :], m.broadcast_to([P, NT, P]), ALU.mult).then_inc(s_atm, 1)

            pool.wait_ge(s_cst, 16)
            with pool.Fori(0, NH) as h:
                heads(h)

            pool.wait_ge(s_wod, 4)
            for j in range(2):
                G.memset(xg[:, j], 0.0).then_inc(s_xz, 1)
            pool.wait_ge(s_tabz, 1)
            pool.wait_ge(s_nr, 1)
            rounds = pool.value_load(nrounds[0:1, 0:1], min_val=1, max_val=T // CAP)

            def gather(e, j, n):
                G.tensor_copy(gcur[:, j:j + 1], gidx[:, bass.ds(e, 1)]).then_inc(l_pool, 1)
                wait(l_pool, n + 1)
                G.indirect_dma_start(xg[:, j, :], None, h_dram, bass.IndirectOffsetOnAxis(gcur[:, j:j + 1], 0),
                                     bounds_check=2 * T - 1, oob_is_err=False).then_inc(s_xg[j], 16)

            def scatter(e, j, n):
                wait(s_yeA, n + 1)
                wait(s_yeD, n + 1)
                G.tensor_copy(scur[:, j:j + 1], sidx[:, bass.ds(e, 1)]).then_inc(s_scur, 1)
                wait(s_scur, n + 1)
                G.indirect_dma_start(y_dram, bass.IndirectOffsetOnAxis(scur[:, j:j + 1], 0), ye[:, j, :], None,
                                     bounds_check=4 * T - 1, oob_is_err=False).then_inc(s_sc, 16)
                wait(s_sc, n * 16 + 16)

            with pool.Fori(0, rounds) as r:
                wait(s_slot, r + 1)
                pool.dma_start(tab_dram.rearrange("(p a) b -> p (a b)", p=P), fill).then_inc(s_tabw, 16)
                wait(s_tabw, r * 80 + 16)
                for k in range(2):
                    for t in range(NT):
                        G.indirect_dma_start(tab_dram, bass.IndirectOffsetOnAxis(slot_u[:, t, k:k + 1], 0),
                                             payload[:, k, t, :], None, bounds_check=SLOTS * NE - 1, oob_is_err=False)\
                            .then_inc(s_tabw, 16)
                wait(s_tabw, r * 80 + 80)
                for half in range(2):
                    pool.dma_start(tabf[half * 64:half * 64 + 64].rearrange("s e b -> s (e b)"),
                                   tab_dram.rearrange("(s e) b -> s (e b)", e=NE)).then_inc(s_tabl, 16)
                wait(s_idx, r + 1)
                pool.wait_ge(s_hrow, 16 * NT)
                pool.wait_ge(s_xz, 2)
                for j in range(2):
                    gather(j, j, r * NE + j)
                with pool.Fori(0, NE // 2 - 1) as e2:
                    for j in range(2):
                        scatter(e2 * 2 + j, j, r * NE + e2 * 2 + j)
                        gather(e2 * 2 + j + 2, j, r * NE + e2 * 2 + j + 2)
                for j in range(2):
                    scatter(NE - 2 + j, j, r * NE + NE - 2 + j)


_INS = ["x", "norm_mix_w", "w_in", "gdn_conv_w", "gdn_a_log", "gdn_dt_bias", "gdn_norm_w", "rg_conv_w", "rg_conv_b",
        "rg_w_rgate", "rg_b_rgate", "rg_w_igate", "rg_b_igate", "rg_lambda", "rg_norm_w", "w_out", "norm_ffn_w",
        "router_w_group", "router_b_group", "router_w_expert", "router_b_expert", "expert_w1", "expert_w3",
        "expert_w2", "norm_final_w"]


def kernel(**inputs):
    import numpy as _np
    import concourse.bacc as _bacc
    from concourse import mybir as _mybir
    from concourse.bass_utils import run_bass_kernel_spmd as _run

    nc = _bacc.Bacc("TRN2", target_bir_lowering=False, num_devices=1)
    arrays, args = {}, []
    for name in _INS:
        a = _np.ascontiguousarray(inputs[name])
        arrays[f"in_{name}_dram"] = a
        args.append(nc.dram_tensor(f"in_{name}_dram", a.shape, _mybir.dt.from_np(a.dtype), kind="ExternalInput").ap())
    arrays["shape_constants"] = constants()
    args.append(nc.dram_tensor("shape_constants", (P, C_END), F32, kind="ExternalInput").ap())
    res = nc.dram_tensor("out_0_dram", (1, T, D), F32, kind="ExternalOutput").ap()
    build(nc, args, res)
    r = _run(nc, [arrays], core_ids=[0])
    return r.results[0]["out_0_dram"]
```

```python
from contextlib import ExitStack

import numpy as np
import concourse.bass as bass
from concourse import mybir

F32 = mybir.dt.float32
I32 = mybir.dt.int32
U32 = mybir.dt.uint32
ALU = mybir.AluOpType
ACT = mybir.ActivationFunctionType
AX = mybir.AxisListType

P = 128
D = 2048
T = 256
NT = T // P
KD = D // P
NH = 8
HD = 128
CH = 64
NC = T // CH
TAPS = 4
GW = NH * HD
NG = 4
EG = 8
NE = NG * EG
FF = 512
FC = FF // P
SLOTS = 64
LEVELS = 6
EPS = 1e-6
QSCALE = float(HD) ** -0.5
GELU_C = 0.044715
GELU_S = 0.7978845608028654
HD2 = D // 2
NP = NE // 2

C_ID = 0
C_MQ = C_ID + P
C_MS = C_MQ + P
C_LV = C_MS + P
C_TRI = C_LV + LEVELS * P
C_ONE = C_TRI + P
C_IO = C_ONE + P
C_GRP = C_IO + SLOTS
C_SEL = C_GRP + NE
C_END = C_SEL + 16

Q_CONV = 0
Q_RGC = 12
Q_CB = 16
Q_BR = 17
Q_BI = 18
Q_LAM = 19
Q_RGN = 20
Q_VB = 21
Q_KB = 23
Q_KDEC = 25
Q_GC = 27
NQ = 29


def constants():
    c = np.zeros((P, C_END), np.float32)
    j, i = np.meshgrid(np.arange(P), np.arange(P), indexing="ij")
    same = j // CH == i // CH
    c[:, C_ID:C_ID + P] = j == i
    c[:, C_MQ:C_MQ + P] = (same & (j <= i)) * QSCALE
    c[:, C_MS:C_MS + P] = same & (j < i)
    for l in range(LEVELS):
        b = 1 << l
        c[:, C_LV + l * P:C_LV + (l + 1) * P] = (j // (2 * b) == i // (2 * b)) & (j // b % 2 == 0) & (i // b % 2 == 1)
    c[:, C_TRI:C_TRI + P] = j < i
    c[:, C_ONE:C_ONE + P] = 1
    c[:, C_IO:C_IO + SLOTS] = np.arange(SLOTS)
    c[:, C_GRP:C_GRP + NE] = np.arange(NE) // EG
    c[:16, C_SEL:C_SEL + 16] = np.eye(16)
    return c


class Link:

    def __init__(self, eng, sem):
        self.eng, self.sem, self.base, self.n = eng, sem, 0, 0

    def __call__(self, ins):
        ins.then_inc(self.sem, 1)
        self.n += 1
        self.eng.wait_ge(self.sem, self.base + self.n)
        return ins

    def enter(self, turn, per):
        if not isinstance(self.base, int) or self.n:
            self.start = self.base + self.n
        else:
            self.start = self.base
        self.base, self.n, self.per = self.start + turn * per, 0, per

    def leave(self, turns):
        assert self.n == self.per, f"{self.sem} per body: {self.n}, not {self.per}"
        self.base, self.n = self.start + turns * self.per, 0


PER_DVE = 23


def build(nc, ins, out, slots=SLOTS):
    (x, norm_mix_w, w_in, gdn_conv_w, gdn_a_log, gdn_dt_bias, gdn_norm_w, rg_conv_w, rg_conv_b, rg_w_rgate,
     rg_b_rgate, rg_w_igate, rg_b_igate, rg_lambda, rg_norm_w, w_out, norm_ffn_w, router_w_group,
     router_b_group, router_w_expert, router_b_expert, expert_w1, expert_w3, expert_w2, norm_final_w, const) = ins

    with ExitStack() as ctx:
        def sb(name, shape, dt=F32):
            return ctx.enter_context(nc.sbuf_tensor(name, shape, dt))

        def sem(name):
            return ctx.enter_context(nc.semaphore(name))

        bank = [ctx.enter_context(nc.psum_tensor(f"bank{i}", [P, 512], F32)) for i in range(8)]

        ew = sb("ew", [P, 6, 4096])
        fw = sb("fw", [P, 6 * 2048])
        hT = sb("hT", [P, KD, T])
        mixT = sb("mixT", [P, KD, T])
        cst = sb("cst", [P, C_END])
        ye = sb("ye", [P, 2, 1024])
        misc = sb("misc", [P, 2688])

        class Region:

            def __init__(self, ap, size):
                self.ap, self.size, self.at = ap, size, 0

            def take(self, *dims):
                n = int(np.prod(dims))
                a = self.ap[:, self.at:self.at + n]
                self.at += n
                assert self.at <= self.size, (self.at, self.size)
                if len(dims) == 1:
                    return a
                names = "abcd"[:len(dims)]
                return a.rearrange(f"p ({' '.join(names)}) -> p {' '.join(names)}", **dict(zip(names, dims)))

        fws = fw[:, :].rearrange("p (s k n) -> p s k n", s=6, k=KD)
        R1 = Region(ew[:, 4:6, :].rearrange("p a b -> p (a b)"), 8192)
        R2 = Region(ye[:, :, :].rearrange("p a b -> p (a b)"), 2048)
        R3 = Region(misc[:, :], 2688)
        cq = R1.take(3, T)
        th = R1.take(3, T)
        nat = R1.take(2, NT, HD)
        rhs = R1.take(2, NT, HD)
        kdec = R1.take(NT, HD)
        qkT = R1.take(NT, 2, P)
        dec = R1.take(NT, 2, P)
        aa = R1.take(NT, 2, P)
        atm = R1.take(LEVELS, NT, P)
        tt = R1.take(NT, 2, P)
        pm = R1.take(NT, P)
        nwT = R1.take(T)
        vn = R1.take(NT, HD)
        qg = R1.take(T)
        egb = R1.take(T)
        sq = R1.take(2, T)
        rr = R2.take(2, T)
        gexp = R2.take(NT, P)
        bm = R2.take(NT, P)
        xc = R2.take(T)
        gg = R2.take(T)
        sz = R2.take(T)
        zr = R2.take(T)
        lru = R3.take(6, T)
        thz = R3.take(T)
        xr = R3.take(T)
        gl2 = R3.take(T)
        S = R3.take(HD)
        rgw = R3.take(2, P)
        prm = sb("prm", [P, NQ, NH])
        pc = sb("pc", [P, NQ])
        ph = sb("ph", [P, NQ])
        gnw = sb("gnw", [P, 1])
        mixw = sb("mixw", [P, KD])
        ss4 = sb("ss4", [P, 4])
        sd4 = sb("sd4", [P, 4])
        r4 = sb("r4", [P, 4])
        eps_c = sb("eps_c", [P, 2])
        stat = sb("stat", [P, 8])
        rows = sb("rows", [16, 2, T])
        rsel = sb("rsel", [16, 2, T])
        R0 = Region(ew[:, 0:4, :].rearrange("p a b -> p (a b)"), 16384)
        xn = R0.take(NT, D)
        junk = R0.take(D)
        wba = R0.take(KD, 16)
        vec = R0.take(2, P)
        bar = R0.take(12, T)
        tkn = R0.take(4, NT, 16)
        lamt = R0.take(6, NH)
        par16 = R0.take(4)
        cmask = R0.take(T)
        wq_slot = [ew[:, 0:2, :], ew[:, 2:4, :], None, ew[:, 0:2, :]]
        wq_view = [None if a is None else a.rearrange("p a (k n) -> p (a k) n", n=512) for a in wq_slot]
        wq_view[2] = fw[:, 0:8192].rearrange("p (k n) -> p k n", n=512)
        x2 = fw[:, 8192:12288].rearrange("p (t d) -> p t d", t=NT)
        hn = fw[:, 0:4096].rearrange("p (t d) -> p t d", t=NT)
        wfin = fw[:, 4096:6144]
        wffn = ye[:, :, :].rearrange("p a b -> p (a b)")
        rw = fw[:, 6144:6144 + KD * 36].rearrange("p (k n) -> p k n", k=KD)
        rb = fw[:, 6720:6756]
        R4 = Region(fw[:, 6756:8192], 1436)
        lg = R4.take(NT, 8)
        le = R4.take(NT, NE)
        lm = R4.take(NT, NE)
        oh = R4.take(2, NT, NE)
        cnt = R4.take(4)
        m8 = R4.take(NT, 8)
        i8 = R4.take(NT, 8)
        gts = R4.take(NT, 8)
        slot = R4.take(NT, NE + 2)
        gate = R4.take(NT, NE)
        gcol = R4.take(NT, 2)
        i8u = sb("i8u", [P, NT, 8], U32)
        nrounds = sb("nrounds", [P, 1], I32)
        R5 = Region(mixT[:, :, :].rearrange("p a b -> p (a b)"), 4096)
        y_pair = ye[:, :, :]
        hs = R5.take(FF)
        eth = R5.take(FC, SLOTS)
        gT = R5.take(FC, SLOTS)
        pick = R5.take(NT, 2, SLOTS)
        place = R5.take(NT, 2, 2, SLOTS)
        placeT = R5.take(2, T)
        R6 = Region(hT[:, :, :].rearrange("p a b -> p (a b)"), 4096)
        xT = R6.take(KD, P)
        junk2 = R6.take(D)

        ident = cst[:, C_ID:C_ID + P]
        ones = cst[:, C_ONE:C_ONE + P]

        s_cst = sem("s_cst")
        s_x = sem("s_x")
        s_vec = sem("s_vec")
        s_wba = sem("s_wba")
        s_win = [sem(f"s_win{b}") for b in range(6)]
        s_rgw = sem("s_rgw")
        s_init = sem("s_init")
        s_vecT = sem("s_vecT")
        s_xss = sem("s_xss")
        s_xh = sem("s_xh")
        s_xT = sem("s_xT")
        s_hT = sem("s_hT")
        s_hTa = sem("s_hTa")
        s_ba = sem("s_ba")
        s_bath = sem("s_bath")
        s_barow = sem("s_barow")
        s_lex = sem("s_lex")
        s_par = sem("s_par")
        s_alog = sem("s_alog")
        s_eg = sem("s_eg")
        s_tokT = sem("s_tokT")
        s_prm = sem("s_prm")
        s_proj = sem("s_proj")
        s_conv = sem("s_conv")
        s_th = sem("s_th")
        s_silu = sem("s_silu")
        s_evac = sem("s_evac")
        s_rx = sem("s_rx")
        s_gsq = sem("s_gsq")
        s_gv = sem("s_gv")
        s_gth = sem("s_gth")
        s_gate = sem("s_gate")
        s_sel = sem("s_sel")
        s_gb = sem("s_gb")
        s_rgmm = sem("s_rgmm")
        s_ri = sem("s_ri")
        s_la = sem("s_la")
        s_a = sem("s_a")
        s_m2 = sem("s_m2")
        s_mu = sem("s_mu")
        s_y = sem("s_y")
        s_nat_mm = sem("s_nat_mm")
        s_ss = sem("s_ss")
        s_nat = sem("s_nat")
        s_vb = sem("s_vb")
        s_diff = sem("s_diff")
        s_exp = sem("s_exp")
        s_dec = sem("s_dec")
        s_kb = sem("s_kb")
        s_back = sem("s_back")
        s_qkT = sem("s_qkT")
        s_qg = sem("s_qg")
        s_kk = sem("s_kk")
        s_aa = sem("s_aa")
        s_atm = sem("s_atm")
        s_P = sem("s_P")
        s_Pc = sem("s_Pc")
        s_U = sem("s_U")
        s_T = sem("s_T")
        s_w = sem("s_w")
        s_nw = sem("s_nw")
        s_v = sem("s_v")
        s_vn = sem("s_vn")
        s_o = sem("s_o")
        s_S = sem("s_S")
        s_sq = sem("s_sq")
        s_nss = sem("s_nss")
        s_rt = sem("s_rt")
        s_mix = sem("s_mix")
        l_dve = sem("l_dve")
        l_act = sem("l_act")
        l_pool = sem("l_pool")
        s_wo = [sem(f"s_wo{n}") for n in range(4)]
        s_wod = sem("s_wod")
        s_x2r = sem("s_x2r")
        s_x2 = sem("s_x2")
        s_wffn = sem("s_wffn")
        s_rw = sem("s_rw")
        s_hss = sem("s_hss")
        s_hn = sem("s_hn")
        s_h2T = sem("s_h2T")
        s_h2Ta = sem("s_h2Ta")
        s_h2mm = sem("s_h2mm")
        s_lgt = sem("s_lgt")
        s_gex = sem("s_gex")
        s_route = sem("s_route")
        s_oh = sem("s_oh")
        s_rank = sem("s_rank")
        s_nr = sem("s_nr")
        s_ew = [sem(f"s_ew{b}") for b in range(6)]
        s_ed = sem("s_ed")
        s_pick = sem("s_pick")
        s_xg = sem("s_xg")
        s_place = sem("s_place")
        s_placeT_mm = sem("s_placeT_mm")
        s_placeT = sem("s_placeT")
        s_comb = sem("s_comb")
        s_add = [sem("s_add0"), sem("s_add1")]
        s_xeA = sem("s_xeA")
        s_xeD = sem("s_xeD")
        s_H = sem("s_H")
        s_hs = sem("s_hs")
        s_HT = sem("s_HT")
        s_eth = sem("s_eth")
        s_g = sem("s_g")
        s_Y = sem("s_Y")
        s_yeA = sem("s_yeA")
        s_yeD = sem("s_yeD")
        s_u = sem("s_u")
        s_fin = sem("s_fin")
        s_frt = sem("s_frt")
        s_out = sem("s_out")

        block = ctx.enter_context(nc.Block())
        w_in_v = w_in[0].rearrange("(k p) n -> p k n", p=P)
        BLOCK_COL = [0, GW, 2 * GW, 3 * GW, 4 * GW + 2 * NH, 5 * GW + 2 * NH]
        x_v = x[0].rearrange("(t p) d -> p t d", p=P)
        w_out_v = w_out[0].rearrange("(k p) n -> p k n", p=P)
        out_v = out[0].rearrange("(t p) d -> p t d", p=P)
        CAP = slots

        @block.sync
        def _(sp):
            sp.dma_start(xn, x_v).then_inc(s_x, 16)
            sp.dma_start(cst[:, :], const).then_inc(s_cst, 16)
            rv = [(vec[0:96, 0, :], gdn_conv_w[0].rearrange("j (b h p) -> (j b h) p", p=P, h=NH)),
                  (vec[0:32, 1, :], rg_conv_w[0].rearrange("j (h p) -> (j h) p", p=P)),
                  (vec[32:40, 1, :], rg_conv_b[0].rearrange("(h p) -> h p", p=P)),
                  (vec[40:48, 1, :], rg_b_rgate[0].rearrange("(h p) -> h p", p=P)),
                  (vec[48:56, 1, :], rg_b_igate[0].rearrange("(h p) -> h p", p=P)),
                  (vec[56:64, 1, :], rg_lambda[0].rearrange("(h p) -> h p", p=P)),
                  (vec[64:72, 1, :], rg_norm_w[0].rearrange("(h p) -> h p", p=P)),
                  (vec[72:88, 1, :], norm_mix_w[0].rearrange("(h p) -> h p", p=P)),
                  (vec[88:89, 1, :], gdn_norm_w)]
            for to, of in rv:
                sp.dma_start(to, of).then_inc(s_vec, 16)
            sp.dma_start(wba, w_in_v[:, :, 4 * GW:4 * GW + 2 * NH]).then_inc(s_wba, 16)
            sp.wait_ge(s_init, 1)
            sp.dma_start(par16[8:16, 0:1], gdn_a_log.rearrange("a h -> h a")).then_inc(s_alog, 16)
            sp.dma_start(par16[8:16, 1:2], gdn_dt_bias.rearrange("a h -> h a")).then_inc(s_alog, 16)

            def load_block(h, b):
                sp.dma_start(fws[:, b], w_in_v[:, :, bass.ds(h * P + BLOCK_COL[b], P)]).then_inc(s_win[b], 16)

            def load_rg(h):
                sp.dma_start(rgw[:, 0, :], rg_w_rgate[0, h]).then_inc(s_rgw, 16)
                sp.dma_start(rgw[:, 1, :], rg_w_igate[0, h]).then_inc(s_rgw, 16)

            for b in range(6):
                load_block(0, b)
            load_rg(0)
            with sp.Fori(1, NH) as h:
                for b in range(6):
                    sp.wait_ge(s_proj, (h - 1) * 6 + b + 1)
                    load_block(h, b)
                sp.wait_ge(s_rgmm, h)
                load_rg(h)
            for n in range(4):
                if n == 0:
                    sp.wait_ge(s_prm, 1)
                if n == 2:
                    sp.wait_ge(s_proj, NH * 6)
                    sp.dma_start(x2, x_v).then_inc(s_x2r, 16)
                if n == 3:
                    sp.wait_ge(s_wod, 1)
                sp.dma_start(wq_view[n], w_out_v[:, :, n * 512:(n + 1) * 512]).then_inc(s_wo[n], 16)
            sp.wait_ge(s_mix, 2 * NH)
            sp.dma_start(wffn, norm_ffn_w.broadcast_to([P, D])).then_inc(s_wffn, 16)

            def load_expert(e, piece):
                half, which = piece // 2, piece % 2
                if piece < 4:
                    src = (expert_w1, expert_w3)[which][0, e].rearrange("(c k p) n -> p c k n", p=P, c=2)[:, half]
                    dst = ew[:, piece].rearrange("p (k n) -> p k n", n=FF)
                else:
                    src = expert_w2[0, e].rearrange("(c k p) n -> p c k n", p=P, c=2)[:, which]
                    dst = ew[:, piece].rearrange("p (k n) -> p k n", n=D)
                sp.dma_start(dst, src).then_inc(s_ew[piece], 16)

            sp.wait_ge(s_wod, 2)
            for piece in (2, 3, 4, 5):
                load_expert(0, piece)
            sp.wait_ge(s_wod, 3)
            sp.dma_start(wfin, norm_final_w.rearrange("(a d) -> a d", a=1).broadcast_to([P, D])).then_inc(s_rw, 16)
            sp.dma_start(rw[:, :, 0:NG], router_w_group[0].rearrange("(k p) n -> p k n", p=P)).then_inc(s_rw, 16)
            sp.dma_start(rw[:, :, NG:], router_w_expert[0].rearrange("(k p) n -> p k n", p=P)).then_inc(s_rw, 16)
            sp.dma_start(rb[:, 0:NG], router_b_group.broadcast_to([P, NG])).then_inc(s_rw, 16)
            sp.dma_start(rb[:, NG:], router_b_expert.broadcast_to([P, NE])).then_inc(s_rw, 16)
            sp.wait_ge(s_wod, 4)
            for piece in (0, 1):
                load_expert(0, piece)
            sp.wait_ge(s_nr, 1)
            rounds = sp.value_load(nrounds[0:1, 0:1], min_val=1, max_val=T // CAP)
            with sp.Fori(0, rounds) as r:
                with sp.Fori(1, NE) as e:
                    for piece in range(6):
                        sp.wait_ge(s_ed, (r * NE + e - 1) * 6 + piece + 1)
                        load_expert(e, piece)
                with sp.If(r + 1 < rounds):
                    for piece in range(6):
                        sp.wait_ge(s_ed, (r * NE + NE - 1) * 6 + piece + 1)
                        load_expert(0, piece)
                sp.nop()
            for t in range(NT):
                sp.wait_ge(s_fin, t + 1)
                sp.dma_start(out_v[:, t], x2[:, t]).then_inc(s_out, 16)
            sp.wait_ge(s_out, 16 * NT)

        @block.tensor
        def _(pe):
            def mm(o, l, r, start, stop):
                return nc.tensor.matmul(o, l, r, start=start, stop=stop, skip_group_check=True)

            def tr(o, i, n=P):
                return nc.tensor.transpose(o, i, ident[0:n, 0:n])

            pe.wait_ge(s_cst, 16)
            pe.wait_ge(s_vec, 16 * 9)
            tr(bank[7][:, 0:96], vec[0:96, 0, :], 96)
            tr(bank[7][:, 96:185], vec[0:89, 1, :], 89).then_inc(s_vecT, 1)
            for k2 in range(KD // 2):
                if k2 == 0:
                    pe.wait_ge(s_xh, NT)
                if k2 >= 4:
                    pe.wait_ge(s_hT if k2 % 2 == 0 else s_hTa, (k2 - 4) // 2 + 1)
                for k in range(2):
                    for t in range(NT):
                        l = tr(bank[k2 % 4][:, (k * NT + t) * P:(k * NT + t + 1) * P],
                               xn[:, t, (2 * k2 + k) * P:(2 * k2 + k + 1) * P])
                l.then_inc(s_xT, 1)
            pe.wait_ge(s_hT, 4)
            pe.wait_ge(s_hTa, 4)
            pe.wait_ge(s_wba, 16)
            for k in range(KD):
                l = mm(bank[4][0:16, 0:T], wba[:, k, :], hT[:, k, :], k == 0, k == KD - 1)
            l.then_inc(s_ba, 1)

            def project(h):
                for b in range(6):
                    o = bank[b % 2][:, 0:T]
                    pe.wait_ge(s_win[b], h * 16 + 16)
                    if b >= 2 or not isinstance(h, int):
                        pe.wait_ge(s_evac, h * 6 + b - 1)
                    for k in range(KD):
                        l = mm(o, fws[:, b, k, :], hT[:, k, :], k == 0, k == KD - 1)
                        if k == KD - 1:
                            l.then_inc(s_proj, 1)
                        yield

            def heads(h, fill):
                pe.wait_ge(s_rgw, h * 32 + 32)
                pe.wait_ge(s_rx, h + 1)
                mm(bank[5][:, 0:T], rgw[:, 0, :], xc, True, True)
                mm(bank[5][:, T:], rgw[:, 1, :], xc, True, True).then_inc(s_rgmm, 1)
                pe.wait_ge(s_silu, h * 3 + 3)
                for b in range(2):
                    for t in range(NT):
                        tr(bank[2][:, (b * NT + t) * P:(b * NT + t + 1) * P], cq[:, b, t * P:(t + 1) * P])
                for t in range(NT):
                    l = tr(bank[3][:, t * P:(t + 1) * P], cq[:, 2, t * P:(t + 1) * P])
                l.then_inc(s_nat_mm, 1)
                pe.wait_ge(s_sel, h + 1)
                mm(bank[6][:, :], cst[0:16, C_ONE:C_ONE + P], rsel[:, :, :].rearrange("p a b -> p (a b)"), True, True)\
                    .then_inc(s_gb, 1)
                fill(10)
                pe.wait_ge(s_nat, h + 1)
                for t in range(NT):
                    for b in range(2):
                        l = tr(bank[4][:, (t * 2 + b) * P:(t * 2 + b + 1) * P], nat[:, b, t, :])
                l.then_inc(s_back, 1)
                fill(4)
                pe.wait_ge(s_qkT, h + 1)
                for t in range(NT):
                    l = mm(bank[5][:, t * 2 * P:(t + 1) * 2 * P], qkT[:, t, 1, :],
                           qkT[:, t].rearrange("p a b -> p (a b)"), True, True)
                l.then_inc(s_kk, 1)
                fill(5)
                pe.wait_ge(s_atm, h * LEVELS + 1)
                for t in range(NT):
                    l = tr(bank[3][:, T + t * P:T + (t + 1) * P], atm[:, 0, t, :])
                l.then_inc(s_P, 1)
                fill(3)
                for lv in range(1, LEVELS):
                    pe.wait_ge(s_atm, h * LEVELS + lv + 1)
                    pe.wait_ge(s_T, h * LEVELS + lv)
                    for t in range(NT):
                        l = mm(bank[3][:, T + t * P:T + (t + 1) * P], atm[:, lv, t, :], tt[:, t, 0, :], True, True)
                    l.then_inc(s_P, 1)
                    fill(3)
                    pe.wait_ge(s_Pc, h * (LEVELS - 1) + lv)
                    for t in range(NT):
                        mm(bank[2][:, t * 2 * P:t * 2 * P + P], tt[:, t, 1, :], pm[:, t, :], True, True)
                        l = mm(bank[2][:, t * 2 * P + P:(t + 1) * 2 * P], pm[:, t, :], tt[:, t, 1, :], True, True)
                    l.then_inc(s_U, 1)
                    fill(3)
                pe.wait_ge(s_T, h * LEVELS + LEVELS)
                pe.wait_ge(s_kb, h * 2 + 2)
                pe.wait_ge(s_vb, h + 1)
                for t in range(NT):
                    l = mm(bank[6][:, t * P:(t + 1) * P], rhs[:, 1, t, :], tt[:, t, 1, :], True, True)
                l.then_inc(s_w, 1)
                fill(3)
                for c in range(NC):
                    t, lo = c // 2, c % 2 * CH
                    hi = lo + CH
                    l = mm(bank[5][lo:hi, 0:P], tt[lo:hi, t, 1, lo:hi], rhs[lo:hi, 0, t, :], True, c == 0)
                    if c:
                        pe.wait_ge(s_nw, h + 1)
                        pe.wait_ge(s_S, h * 3 + c)
                        l = mm(bank[5][lo:hi, 0:P], nwT[:, c * CH:(c + 1) * CH], S, False, True)
                    l.then_inc(s_v, 1)
                    fill(2)
                    pe.wait_ge(s_vn, h * NC + c + 1)
                    if c < NC - 1:
                        mm(bank[4][:, 0:HD], kdec[lo:hi, t, :], vn[lo:hi, t, :], True, True)
                    if c:
                        pe.wait_ge(s_qg, h + 1)
                        mm(bank[7][:, c * CH:(c + 1) * CH], S, qg[:, c * CH:(c + 1) * CH], True, False)
                    mm(bank[7][:, c * CH:(c + 1) * CH], vn[lo:hi, t, :], aa[lo:hi, t, 0, lo:hi], c == 0, True)\
                        .then_inc(s_o, 1)
                    fill(3)
                fill(4)
                pe.wait_ge(s_sq, h * 2 + 2)
                mm(bank[4][:, :], ones, sq.rearrange("p a b -> p (a b)"), True, True).then_inc(s_nss, 1)

            for _ in project(0):
                pass
            pe.wait_ge(s_eg, 1)
            for q in range(4):
                for t in range(NT):
                    l = tr(bank[7][:, (q * NT + t) * 16:(q * NT + t + 1) * 16],
                           bar[0:16, 8 + q, t * P:(t + 1) * P], 16)
            l.then_inc(s_tokT, 1)
            with pe.Fori(1, NH) as i:
                steps = project(i)

                def fill(n):
                    for _ in range(n):
                        next(steps, None)

                heads(i - 1, fill)
                for _ in steps:
                    pass

            def wo(n, chunks, last):
                for c in chunks:
                    for t in range(NT):
                        l = mm(bank[2 * n + t][:, :], mixT[:, c, t * P:(t + 1) * P], wq_view[n][:, c, :],
                               c == 0, c == KD - 1)
                        if last and c == chunks[-1] and t == NT - 1:
                            l.then_inc(s_wod, 1)
                        yield

            pe.wait_ge(s_wo[0], 16)
            pe.wait_ge(s_mix, 2 * (NH - 1))
            pe.wait_ge(s_evac, NH * 6)
            early = [c for c in range(KD) if c % NH != NH - 1]
            steps = wo(0, early, False)

            def fill_w(n):
                for _ in range(n):
                    next(steps, None)

            heads(NH - 1, fill_w)
            for _ in steps:
                pass
            pe.wait_ge(s_mix, 2 * NH)
            for _ in wo(0, [NH - 1, KD - 1], True):
                pass
            for n in range(1, 4):
                pe.wait_ge(s_wo[n], 16)
                for _ in wo(n, list(range(KD)), True):
                    pass
            for k2 in range(KD // 2):
                if k2 == 0:
                    pe.wait_ge(s_hn, NT)
                    pe.wait_ge(s_x2, 4)
                if k2 >= 4:
                    pe.wait_ge(s_h2T if k2 % 2 == 0 else s_h2Ta, (k2 - 4) // 2 + 1)
                for k in range(2):
                    for t in range(NT):
                        l = tr(bank[k2 % 4][:, (k * NT + t) * P:(k * NT + t + 1) * P],
                               hn[:, t, (2 * k2 + k) * P:(2 * k2 + k + 1) * P])
                l.then_inc(s_h2mm, 1)
            pe.wait_ge(s_rw, 16 * 5)
            pe.wait_ge(s_h2T, 4)
            pe.wait_ge(s_h2Ta, 4)
            for t in range(NT):
                for k in range(KD):
                    l = mm(bank[4][:, t * 64:t * 64 + NG + NE], hT[:, k, t * P:(t + 1) * P], rw[:, k, :],
                           k == 0, k == KD - 1)
            l.then_inc(s_lgt, 1)
            pe.wait_ge(s_oh, 1)
            for t in range(NT):
                for u in range(t + 1):
                    for q in range(2):
                        mm(bank[5][:, t * NE:(t + 1) * NE], cst[:, C_TRI:C_TRI + P] if u == t else ones,
                           oh[:, q, u, :], u == 0 and q == 0, u == t and q == 1)
            for u in range(NT):
                for q in range(2):
                    l = mm(bank[5][:, 2 * NE:3 * NE], ones, oh[:, q, u, :], u == 0 and q == 0, u == 1 and q == 1)
            l.then_inc(s_rank, 1)

            pe.wait_ge(s_nr, 1)
            rounds = pe.value_load(nrounds[0:1, 0:1], min_val=1, max_val=T // CAP)

            def gather(n, r, p):
                pe.wait_ge(s_pick, r * (NP + 1) + p + 1)
                for q in range(4):
                    if q >= 2:
                        pe.wait_ge(s_xeA if q % 2 else s_xeD, n * 2 + 1)
                    for c in range(4):
                        for t in range(NT):
                            l = mm(bank[q % 2][:, c * P:(c + 1) * P], hn[:, t, (q * 4 + c) * P:(q * 4 + c + 1) * P],
                                   pick[:, t].rearrange("p a b -> p (a b)"), t == 0, t == NT - 1)
                    l.then_inc(s_xg, 1)

            def combine(m):
                pe.wait_ge(s_placeT, m + 1)
                pe.wait_ge(s_yeA, m * 2 + 2)
                pe.wait_ge(s_yeD, m * 2 + 2)
                for i in range(8):
                    t, col = i // 4, i % 4
                    if i >= 2:
                        pe.wait_ge(s_add[(i - 2) // 4], m * 4 + (i - 2) % 4 + 1)
                    mm(bank[6 + i % 2][:, :], placeT[:, col // 2, t * P:(t + 1) * P],
                       y_pair[:, col // 2, col % 2 * 512:col % 2 * 512 + 512], True, True).then_inc(s_comb, 1)

            def pair(n, r, p, first):
                gather(n, r, p)
                pe.wait_ge(s_xeA, n * 2 + 2)
                pe.wait_ge(s_xeD, n * 2 + 2)
                for j in range(2):
                    e = pe.snap(n * 2 + j)
                    for half in range(2):
                        for which in range(2):
                            pe.wait_ge(s_ew[half * 2 + which], e * 16 + 16)
                        for k in range(KD // 2):
                            for which in range(2):
                                l = mm(bank[2][which * 64:which * 64 + 64, :],
                                       xT[:, half * 8 + k, j * SLOTS:(j + 1) * SLOTS],
                                       ew[:, half * 2 + which].rearrange("p (k n) -> p k n", n=FF)[:, k, :],
                                       half == 0 and k == 0, half == 1 and k == KD // 2 - 1)
                                if k == KD // 2 - 1:
                                    l.then_inc(s_ed, 1)
                    pe.wait_ge(s_hs, e + 1)
                    for k in range(FC):
                        l = tr(bank[3][:, k * P:(k + 1) * P], hs[:, k * P:(k + 1) * P])
                    l.then_inc(s_HT, 1)
                    if j == 0 and not first:
                        combine(pe.snap(n - 1))
                    if j == 1:
                        pe.wait_ge(s_place, n + 1)
                        for v in range(2):
                            for t in range(NT):
                                l = tr(bank[6][:, (v * NT + t) * P:(v * NT + t + 1) * P],
                                       place[:, t, v].rearrange("p a b -> p (a b)"))
                        l.then_inc(s_placeT_mm, 1)
                        pe.wait_ge(s_yeA, n * 2 + 1)
                        pe.wait_ge(s_yeD, n * 2 + 1)
                    pe.wait_ge(s_g, e + 1)
                    for k in range(FC):
                        if k % 2 == 0:
                            pe.wait_ge(s_ew[4 + k // 2], e * 16 + 16)
                        w2 = ew[:, 4 + k // 2].rearrange("p (k n) -> p k n", n=D)
                        for i in range(2):
                            for side in range(2):
                                col = (side ^ j) * HD2 + i * 512
                                l = mm(bank[4 + i][side * 64:side * 64 + 64, :], gT[:, k, :],
                                       w2[:, k % 2, col:col + 512], k == 0, k == FC - 1)
                        if k % 2:
                            l.then_inc(s_ed, 1)

            with pe.Fori(0, rounds) as r:
                pair(pe.snap(r * NP), r, 0, True)
                with pe.Fori(1, NP) as p:
                    pair(pe.snap(r * NP + p), r, p, False)
                combine(pe.snap(r * NP + (NP - 1)))

        @block.scalar
        def _(act):
            link = Link(act, l_act)
            act.wait_ge(s_x, 16)
            act.wait_ge(s_init, 1)
            for t in range(NT):
                link(act.activation(junk, xn[:, t], ACT.Square, accum_out=stat[:, t:t + 1]))
            act.activation(stat[:, 2:4], stat[:, 0:2], ACT.Sqrt, scale=1.0 / D, bias=eps_c[:, 0:1]).then_inc(s_xss, 1)
            act.wait_ge(s_par, 1)
            for k2 in range(1, KD // 2, 2):
                act.wait_ge(s_xT, k2 + 1)
                for k in range(2):
                    l = act.activation(hT[:, 2 * k2 + k, :], bank[k2 % 4][:, k * T:(k + 1) * T], ACT.Copy,
                                       scale=mixw[:, 2 * k2 + k:2 * k2 + k + 1])
                l.then_inc(s_hTa, 1)
            act.wait_ge(s_alog, 32)
            act.activation(par16[0:16, 2:3], par16[0:16, 0:1], ACT.Exp).then_inc(s_lex, 1)
            act.wait_ge(s_par, 2)
            act.activation(lamt[:, 1], lamt[:, 0], ACT.Exp, scale=-1.0).then_inc(s_lex, 1)
            act.wait_ge(s_ba, 1)
            act.activation(bar[0:16, 0], bank[4][0:16, 0:T], ACT.Tanh, scale=0.5).then_inc(s_bath, 1)
            act.wait_ge(s_barow, 1)
            act.activation(bar[0:16, 3], bar[0:16, 2], ACT.Exp, scale=-1.0).then_inc(s_bath, 1)
            act.wait_ge(s_barow, 2)
            act.activation(bar[0:16, 10], bar[0:16, 8], ACT.Exp)
            act.activation(bar[0:16, 11], bar[0:16, 7], ACT.Exp).then_inc(s_eg, 1)

            def evac(h, b):
                act.wait_ge(s_proj, h * 6 + b + 1)
                src = bank[b % 2][:, 0:T]
                if b == 3:
                    act.activation(thz, src, ACT.Tanh, scale=0.5)
                act.activation((th[:, 0], th[:, 1], th[:, 2], zr, xr, gg)[b], src, ACT.Copy).then_inc(s_evac, 1)

            def tanh_half(h, b):
                act.wait_ge(s_conv, h * 3 + b + 1)
                act.activation(th[:, b], cq[:, b], ACT.Tanh, scale=0.5).then_inc(s_th, 1)

            def heads(h, evac_next, tanh_next):
                act.wait_ge(s_evac, h * 6 + 6)
                act.activation(gl2, gg, ACT.Square, scale=GELU_C ** 0.5).then_inc(s_gsq, 1)
                act.wait_ge(s_rgmm, h + 1)
                act.wait_ge(s_sel, h + 1)
                act.activation(lru[:, 0], bank[5][:, 0:T], ACT.Tanh, scale=0.5, bias=ph_bias(0)).then_inc(s_ri, 1)
                act.activation(lru[:, 1], bank[5][:, T:], ACT.Tanh, scale=0.5, bias=ph_bias(1)).then_inc(s_ri, 1)
                act.wait_ge(s_gb, h + 1)
                act.activation(egb, bank[6][:, 0:T], ACT.Exp).then_inc(s_exp, 1)
                act.wait_ge(s_diff, h + 1)
                act.activation(gexp, gexp, ACT.Exp).then_inc(s_exp, 1)
                act.wait_ge(s_la, h + 1)
                act.activation(lru[:, 3], lru[:, 2], ACT.Exp)
                act.activation(lru[:, 4], lru[:, 2], ACT.Exp, scale=2.0)
                act.activation(lru[:, 5], lru[:, 2], ACT.Tanh).then_inc(s_a, 1)
                act.wait_ge(s_gv, h + 1)
                act.activation(gl2, gl2, ACT.Tanh, scale=GELU_S).then_inc(s_gth, 1)
                act.wait_ge(s_nat_mm, h + 1)
                for q in range(4):
                    l = act.activation(sq[:, 0, 0:P], bank[2][:, q * P:(q + 1) * P], ACT.Square,
                                       accum_out=ss4[:, q:q + 1])
                    link(l)
                act.activation(sd4[:, :], ss4[:, :], ACT.Sqrt, bias=eps_c[:, 1:2]).then_inc(s_ss, 1)
                act.wait_ge(s_m2, h + 1)
                act.activation(lru[:, 4], lru[:, 5], ACT.Sqrt, scale=-1.0).then_inc(s_mu, 1)
                act.wait_ge(s_back, h + 1)
                act.activation(qkT, bank[4][:, :].rearrange("p (t b i) -> p t b i", t=NT, b=2), ACT.Copy)\
                    .then_inc(s_qkT, 1)
                evac_next(0)
                for lv in range(1, LEVELS):
                    act.wait_ge(s_P, h * LEVELS + lv + 1)
                    act.activation(pm, bank[3][:, T:].rearrange("p (t i) -> p t i", t=NT), ACT.Copy).then_inc(s_Pc, 1)
                    if lv == 2:
                        tanh_next(0)
                        evac_next(1)
                    if lv == 4:
                        tanh_next(1)
                evac_next(2)
                act.wait_ge(s_w, h + 1)
                act.activation(nwT, bank[6][:, 0:T], ACT.Copy, scale=-1.0).then_inc(s_nw, 1)
                for c in range(NC):
                    lo = c % 2 * CH
                    act.wait_ge(s_v, h * NC + c + 1)
                    act.activation(vn[lo:lo + CH, c // 2, :], bank[5][lo:lo + CH, 0:P], ACT.Copy).then_inc(s_vn, 1)
                    if c == 1:
                        tanh_next(2)
                        evac_next(3)
                act.wait_ge(s_y, h + 1)
                act.activation(sq[:, 1], lru[:, 1], ACT.Square, scale=0.5).then_inc(s_sq, 1)
                act.wait_ge(s_o, h * NC + NC)
                act.activation(sq[:, 0], bank[7][:, 0:T], ACT.Square).then_inc(s_sq, 1)
                act.wait_ge(s_nss, h + 1)
                act.activation(rr, bank[4][:, :].rearrange("p (a b) -> p a b", a=2), ACT.Sqrt,
                               scale=1.0 / HD, bias=eps_c[:, 0:1]).then_inc(s_rt, 1)
                evac_next(4)
                evac_next(5)

            def ph_bias(i):
                return ph[:, Q_BR + i:Q_BR + i + 1]

            for b in range(6):
                evac(0, b)
                if 1 <= b <= 3:
                    tanh_half(0, b - 1)
            PER = 4
            with act.Fori(1, NH) as i:
                link.enter(i - 1, PER)
                heads(i - 1, lambda b: evac(i, b), lambda b: tanh_half(i, b))
                link.leave(NH - 1)
            heads(NH - 1, lambda b: None, lambda b: None)

            act.wait_ge(s_x2, 4)
            for t in range(NT):
                link(act.activation(hn[:, t], x2[:, t], ACT.Square, accum_out=stat[:, t:t + 1]))
            act.activation(stat[:, 2:4], stat[:, 0:2], ACT.Sqrt, scale=1.0 / D, bias=eps_c[:, 0:1]).then_inc(s_hss, 1)
            for k2 in range(1, KD // 2, 2):
                act.wait_ge(s_h2mm, k2 + 1)
                act.activation(hT[:, 2 * k2:2 * k2 + 2, :], bank[k2 % 4][:, :].rearrange("p (k i) -> p k i", k=2),
                               ACT.Copy).then_inc(s_h2Ta, 1)
            act.wait_ge(s_gex, 1)
            for t in range(NT):
                act.activation(le[:, t, 0:NG], lg[:, t, 0:NG], ACT.Exp, bias=gts[:, t, 0:1],
                               accum_out=gts[:, t, 1:2])
                l = act.activation(gts[:, t, 3:4], gts[:, t, 2:3], ACT.Exp)
            l.then_inc(s_route, 1)

            act.wait_ge(s_nr, 1)
            rounds = act.value_load(nrounds[0:1, 0:1], min_val=1, max_val=T // CAP)
            with act.Fori(0, rounds) as r:
                with act.Fori(0, NP) as p:
                    n = act.snap(r * NP + p)
                    for q in (1, 3):
                        act.wait_ge(s_xg, n * 4 + q + 1)
                        act.activation(xT[:, q * 4:q * 4 + 4, :], bank[1][:, :].rearrange("p (k i) -> p k i", k=4),
                                       ACT.Copy).then_inc(s_xeA, 1)
                    for j in range(2):
                        e = act.snap(n * 2 + j)
                        act.wait_ge(s_ed, e * 6 + 4)
                        act.activation(hs, bank[2][:, :], ACT.Copy).then_inc(s_hs, 1)
                        act.wait_ge(s_HT, e + 1)
                        act.activation(eth, bank[3][:, :].rearrange("p (k i) -> p k i", k=FC)[:, :, 0:SLOTS],
                                       ACT.Tanh, scale=0.5).then_inc(s_eth, 1)
                        if j == 1:
                            act.wait_ge(s_placeT_mm, n + 1)
                            act.activation(placeT.rearrange("p v t -> p (v t)"), bank[6][:, :], ACT.Copy)\
                                .then_inc(s_placeT, 1)
                        act.wait_ge(s_ed, e * 6 + 6)
                        for side in range(2):
                            l = act.activation(y_pair[side * 64:side * 64 + 64, side ^ j, 512:],
                                               bank[5][side * 64:side * 64 + 64, :], ACT.Copy)
                        l.then_inc(s_yeA, 1)
            for t in range(NT):
                act.wait_ge(s_add[t], rounds * (4 * NP))
                link(act.activation(junk2, x2[:, t], ACT.Square, accum_out=stat[:, t:t + 1]))
                act.activation(stat[:, 2 + t:3 + t], stat[:, t:t + 1], ACT.Sqrt, scale=1.0 / D,
                               bias=eps_c[:, 0:1]).then_inc(s_frt, 1)

        @block.vector
        def _(dve):
            link = Link(dve, l_dve)
            V = nc.vector

            def log1p(out_, u, tmp, x2_, r_):
                link(V.tensor_scalar(tmp, u, 2.0, None, ALU.add))
                link(V.reciprocal(r_, tmp))
                link(V.tensor_tensor(tmp, u, r_, ALU.mult))
                link(V.tensor_tensor(x2_, tmp, tmp, ALU.mult))
                link(V.tensor_scalar(r_, x2_, 2.0 / 15, None, ALU.mult))
                for c in (13, 11, 9, 7, 5, 3):
                    link(V.scalar_tensor_tensor(r_, r_, 2.0 / c, x2_, ALU.add, ALU.mult))
                link(V.scalar_tensor_tensor(out_, r_, 2.0, tmp, ALU.add, ALU.mult))

            V.memset(eps_c[:, 0:1], EPS)
            V.memset(eps_c[:, 1:2], 4 * EPS)
            link(V.memset(par16, 0.0))
            link(V.memset(cmask, 1.0))
            V.memset(cmask.rearrange("p (c i) -> p c i", c=NC)[:, :, 0:1], 0.0).then_inc(s_init, 1)
            dve.wait_ge(s_vecT, 1)
            V.tensor_copy(mixw[:, :], bank[7][:, 168:184]).then_inc(s_par, 1)
            link(V.tensor_copy(lamt[:, 1], bank[7][:, 152:160]))
            V.scalar_tensor_tensor(lamt[:, 0], lamt[:, 1], -1.0, lamt[:, 1], ALU.mult, ALU.max).then_inc(s_par, 1)
            V.tensor_scalar(lamt[:, 2], bank[7][:, 152:160], -1.0, 0.0, ALU.mult, ALU.max)
            V.tensor_copy(prm[:, 0:Q_BR, :], bank[7][:, 0:Q_BR * NH].rearrange("p (q h) -> p q h", h=NH))
            V.tensor_scalar(prm[:, Q_BR:Q_LAM, :], bank[7][:, Q_BR * NH:Q_LAM * NH].rearrange("p (q h) -> p q h", h=NH),
                            0.5, None, ALU.mult)
            V.tensor_scalar(prm[:, Q_RGN, :], bank[7][:, 160:168], 0.5, None, ALU.mult)
            V.tensor_scalar(gnw[:, :], bank[7][:, 184:185], 0.5, None, ALU.mult)
            dve.wait_ge(s_xss, 1)
            link(V.reciprocal(stat[:, 4:6], stat[:, 2:4]))
            for t in range(NT):
                V.tensor_scalar(xn[:, t], xn[:, t], stat[:, 4 + t:5 + t], None, ALU.mult).then_inc(s_xh, 1)
            for k2 in range(0, KD // 2, 2):
                dve.wait_ge(s_xT, k2 + 1)
                for k in range(2):
                    l = V.tensor_scalar(hT[:, 2 * k2 + k, :], bank[k2 % 4][:, k * T:(k + 1) * T],
                                        mixw[:, 2 * k2 + k:2 * k2 + k + 1], None, ALU.mult)
                l.then_inc(s_hT, 1)
            dve.wait_ge(s_lex, 2)
            log1p(lamt[:, 3], lamt[:, 1], lamt[:, 4], lamt[:, 5], lamt[:, 0])
            link(V.tensor_tensor(lamt[:, 4], lamt[:, 2], lamt[:, 3], ALU.add))
            V.tensor_scalar(prm[:, Q_LAM, :], lamt[:, 4], -0.5 * 8.0, None, ALU.mult)
            B = [bar[0:16, i] for i in range(12)]
            dve.wait_ge(s_bath, 1)
            dve.wait_ge(s_alog, 32)
            link(V.tensor_scalar(B[9], B[0], 0.5, 0.5, ALU.mult, ALU.add))
            link(V.tensor_scalar(B[1], bank[4][0:16, 0:T], par16[0:16, 1:2], None, ALU.add))
            V.scalar_tensor_tensor(B[2], B[1], -1.0, B[1], ALU.mult, ALU.max).then_inc(s_barow, 1)
            V.tensor_scalar(B[4], B[1], 0.0, None, ALU.max)
            V.tensor_copy(rows[:, 1], B[9])
            link(V.tensor_scalar(par16[0:16, 3:4], par16[0:16, 2:3], -1.0, None, ALU.mult))
            dve.wait_ge(s_bath, 2)
            log1p(B[6], B[3], B[5], B[7], B[0])
            link(V.tensor_tensor(B[5], B[4], B[6], ALU.add))
            link(V.tensor_scalar(B[6], B[5], par16[0:16, 3:4], None, ALU.mult))
            link(V.tensor_tensor_scan(B[8], cmask[0:16, :], B[6], 0.0, ALU.mult, ALU.add))
            link(V.tensor_copy(rows[:, 0], B[8]))
            b8 = B[8].rearrange("p (c i) -> p c i", c=NC)
            V.tensor_tensor(B[7].rearrange("p (c i) -> p c i", c=NC), b8[:, :, CH - 1:CH].broadcast_to([16, NC, CH]),
                            b8, ALU.subtract).then_inc(s_barow, 1)

            def conv_taps(h, o, src, q, step):
                for j in range(TAPS - 1, -1, -1):
                    s = TAPS - 1 - j
                    if s == 0:
                        if q == "rx":
                            i = V.tensor_scalar(o, src, pc[:, Q_RGC + j:Q_RGC + j + 1], pc[:, Q_CB:Q_CB + 1],
                                                ALU.mult, ALU.add)
                        else:
                            i = V.tensor_scalar(o, src, pc[:, j * 3 + q:j * 3 + q + 1], None, ALU.mult)
                        link(i)
                    else:
                        w = pc[:, Q_RGC + j:Q_RGC + j + 1] if q == "rx" else pc[:, j * 3 + q:j * 3 + q + 1]
                        i = V.scalar_tensor_tensor(o[:, s:], src[:, 0:T - s], w, o[:, s:], ALU.mult, ALU.add)
                        if s < TAPS - 1:
                            link(i)
                i.then_inc(step, 1)

            def params(h):
                link(V.tensor_copy(pc[:, 0:Q_BR], prm[:, 0:Q_BR, h]))

            def conv(h, b):
                dve.wait_ge(s_evac, h * 6 + b + 1)
                conv_taps(h, cq[:, b], th[:, b], b, s_conv)

            def silu(h, b):
                dve.wait_ge(s_th, h * 3 + b + 1)
                V.scalar_tensor_tensor(cq[:, b], th[:, b], 1.0, cq[:, b], ALU.add, ALU.mult).then_inc(s_silu, 1)

            def conv_rx(h):
                dve.wait_ge(s_evac, h * 6 + 5)
                conv_taps(h, xc, xr, "rx", s_rx)

            def silu_z(h):
                V.scalar_tensor_tensor(sz, thz, 1.0, zr, ALU.add, ALU.mult)

            def select(h):
                link(V.tensor_copy(ph[:, :], prm[:, :, h]))
                link(V.tensor_scalar(rsel[:, 0], rows[:, 0], cst[0:16, bass.ds(h + (C_SEL + NH), 1)], None, ALU.mult))
                V.tensor_scalar(rsel[:, 1], rows[:, 1], cst[0:16, bass.ds(h + C_SEL, 1)], None, ALU.mult)\
                    .then_inc(s_sel, 1)

            def heads(h, pre):
                dve.wait_ge(s_gsq, h + 1)
                V.scalar_tensor_tensor(gl2, gl2, 1.0, gg, ALU.add, ALU.mult).then_inc(s_gv, 1)
                dve.wait_ge(s_exp, h * 2 + 1)
                for t in range(NT):
                    V.tensor_scalar(gexp[:, t], bank[6][:, t * P:(t + 1) * P], ph[:, Q_GC + t:Q_GC + t + 1], 0.0,
                                    ALU.subtract, ALU.min)
                V.tensor_tensor(bm, bank[6][:, T:].rearrange("p (t i) -> p t i", t=NT),
                                cst[:, C_MS:C_MS + P].rearrange("p (a i) -> p a i", a=1).broadcast_to([P, NT, P]),
                                ALU.mult).then_inc(s_diff, 1)
                dve.wait_ge(s_ri, h * 2 + 2)
                V.tensor_scalar(lru[:, 2], lru[:, 0], 1.0, ph[:, Q_LAM:Q_LAM + 1], ALU.add, ALU.mult).then_inc(s_la, 1)
                dve.wait_ge(s_ss, h + 1)
                link(V.reciprocal(r4[:, :], sd4[:, :]))
                V.tensor_tensor(nat.rearrange("p b t i -> p (b t) i"), bank[2][:, :].rearrange("p (q i) -> p q i", q=4),
                                r4[:, :].rearrange("p (q a) -> p q a", a=1).broadcast_to([P, 4, P]), ALU.mult)\
                    .then_inc(s_nat, 1)
                V.tensor_tensor(rhs[:, 0], bank[3][:, 0:T].rearrange("p (t i) -> p t i", t=NT),
                                ph[:, Q_VB:Q_VB + NT].rearrange("p (q a) -> p q a", a=1).broadcast_to([P, NT, P]),
                                ALU.mult).then_inc(s_vb, 1)
                dve.wait_ge(s_gth, h + 1)
                link(V.scalar_tensor_tensor(gg, gl2, 1.0, gg, ALU.add, ALU.mult))
                dve.wait_ge(s_a, h + 1)
                V.scalar_tensor_tensor(lru[:, 5], lru[:, 4], 1.0, lru[:, 5], ALU.add, ALU.mult).then_inc(s_m2, 1)
                dve.wait_ge(s_qkT, h + 1)
                V.scalar_tensor_tensor(qg.rearrange("p (t i) -> p t i", t=NT),
                                       bank[4][:, :].rearrange("p (t b i) -> p t b i", t=NT, b=2)[:, :, 0, :], QSCALE,
                                       egb.rearrange("p (t i) -> p t i", t=NT), ALU.mult, ALU.mult).then_inc(s_qg, 1)
                dve.wait_ge(s_kk, h + 1)
                dve.wait_ge(s_dec, h * 2 + 2)
                V.tensor_tensor(aa.rearrange("p t b i -> p (t b i)"), bank[5][:, :],
                                dec.rearrange("p t b i -> p (t b i)"), ALU.mult).then_inc(s_aa, 1)
                pre(0)
                idb = ident.rearrange("p (a i) -> p a i", a=1).broadcast_to([P, NT, P])
                dve.wait_ge(s_atm, h * LEVELS + 1)
                link(V.tensor_tensor(tt[:, :, 1, :], idb, atm[:, 0], ALU.subtract))
                dve.wait_ge(s_P, h * LEVELS + 1)
                V.tensor_tensor(tt[:, :, 0, :], idb, bank[3][:, T:].rearrange("p (t i) -> p t i", t=NT),
                                ALU.subtract).then_inc(s_T, 1)
                link(V.scalar_tensor_tensor(lru[:, 1], lru[:, 1], 1.0, xc, ALU.add, ALU.mult))
                dve.wait_ge(s_mu, h + 1)
                link(V.scalar_tensor_tensor(lru[:, 2], lru[:, 1], 0.5, lru[:, 4], ALU.mult, ALU.mult))
                link(V.tensor_tensor_scan(lru[:, 0], lru[:, 3], lru[:, 2], 0.0, ALU.mult, ALU.add))
                V.tensor_tensor(lru[:, 1], lru[:, 0], gg, ALU.mult).then_inc(s_y, 1)
                for lv in range(1, LEVELS):
                    dve.wait_ge(s_U, h * (LEVELS - 1) + lv)
                    V.tensor_tensor(tt.rearrange("p t b i -> p (t b i)"), tt.rearrange("p t b i -> p (t b i)"),
                                    bank[2][:, :], ALU.subtract).then_inc(s_T, 1)
                    if lv == 2:
                        pre(1)
                    if lv == 4:
                        pre(2)
                for c in range(NC - 1):
                    dve.wait_ge(s_o, h * NC + c + 1)
                    if c == 0:
                        V.tensor_copy(S, bank[4][:, 0:HD]).then_inc(s_S, 1)
                    else:
                        V.scalar_tensor_tensor(S, S, egb[:, c * CH + CH - 1:c * CH + CH], bank[4][:, 0:HD],
                                               ALU.mult, ALU.add).then_inc(s_S, 1)
                    if c == 0:
                        pre(3)
                    if c == 2:
                        pre(4)
                dve.wait_ge(s_sq, h * 2 + 2)
                link(V.scalar_tensor_tensor(qg, bank[7][:, 0:T], gnw[:, 0:1], sz, ALU.mult, ALU.mult))
                dve.wait_ge(s_rt, h + 1)
                link(V.reciprocal(rr.rearrange("p a b -> p (a b)"), rr.rearrange("p a b -> p (a b)")))
                V.tensor_tensor(mixT[:, h, :], qg, rr[:, 0], ALU.mult).then_inc(s_mix, 1)
                V.scalar_tensor_tensor(mixT[:, h + NH, :], lru[:, 1], ph[:, Q_RGN:Q_RGN + 1], rr[:, 1],
                                       ALU.mult, ALU.mult).then_inc(s_mix, 1)

            params(0)
            for b in range(3):
                conv(0, b)
                silu(0, b)
            conv_rx(0)
            silu_z(0)
            dve.wait_ge(s_tokT, 1)
            link(V.tensor_copy(tkn, bank[7][:, 0:P].rearrange("p (q t i) -> p q t i", q=4, t=NT)))
            V.tensor_copy(prm[:, Q_GC:Q_GC + NT, :], tkn[:, 0, :, NH:])
            V.tensor_scalar(prm[:, Q_VB:Q_VB + NT, :], tkn[:, 1, :, 0:NH], 0.5, None, ALU.mult)
            V.tensor_copy(prm[:, Q_KDEC:Q_KDEC + NT, :], tkn[:, 3, :, NH:])
            V.tensor_tensor(prm[:, Q_KB:Q_KB + NT, :], tkn[:, 1, :, 0:NH], tkn[:, 2, :, NH:], ALU.mult)\
                .then_inc(s_prm, 1)
            dve.wait_ge(s_prm, 1)
            select(0)
            with dve.Fori(1, NH) as i:
                link.enter(i - 1, PER_DVE)

                def pre(n):
                    if n == 0:
                        params(i)
                        conv(i, 0)
                    elif n == 1:
                        silu(i, 0)
                        conv(i, 1)
                    elif n == 2:
                        silu(i, 1)
                    elif n == 3:
                        conv(i, 2)
                    elif n == 4:
                        silu(i, 2)

                heads(i - 1, pre)
                conv_rx(i)
                silu_z(i)
                select(i)
                link.leave(NH - 1)
            heads(NH - 1, lambda n: None)

            dve.wait_ge(s_x2r, 16)
            for n in range(4):
                dve.wait_ge(s_wod, n + 1)
                for t in range(NT):
                    l = V.tensor_tensor(x2[:, t, n * 512:(n + 1) * 512], x2[:, t, n * 512:(n + 1) * 512],
                                        bank[2 * n + t][:, :], ALU.add)
                l.then_inc(s_x2, 1)
            link(V.memset(lg, -3.0e38))
            dve.wait_ge(s_hss, 1)
            dve.wait_ge(s_wffn, 16)
            link(V.reciprocal(stat[:, 4:6], stat[:, 2:4]))
            for t in range(NT):
                V.scalar_tensor_tensor(hn[:, t], x2[:, t], stat[:, 4 + t:5 + t], wffn, ALU.mult, ALU.mult)\
                    .then_inc(s_hn, 1)
            for k2 in range(0, KD // 2, 2):
                dve.wait_ge(s_h2mm, k2 + 1)
                V.tensor_copy(hT[:, 2 * k2:2 * k2 + 2, :], bank[k2 % 4][:, :].rearrange("p (k i) -> p k i", k=2))\
                    .then_inc(s_h2T, 1)
            dve.wait_ge(s_lgt, 1)
            lgp = bank[4][:, 0:P].rearrange("p (t i) -> p t i", t=NT)
            rbb = rb.rearrange("p (a i) -> p a i", a=1).broadcast_to([P, NT, NG + NE])
            link(V.tensor_tensor(lg[:, :, 0:NG], lgp[:, :, 0:NG], rbb[:, :, 0:NG], ALU.add))
            link(V.tensor_tensor(le, lgp[:, :, NG:NG + NE], rbb[:, :, NG:], ALU.add))
            for t in range(NT):
                link(V.max(m8[:, t], lg[:, t]))
                V.tensor_scalar(gts[:, t, 0:1], m8[:, t, 0:1], -1.0, None, ALU.mult)
                link(V.max_index(i8u[:, t], m8[:, t], lg[:, t]))
                link(V.tensor_copy(i8[:, t], i8u[:, t]))
                link(V.tensor_scalar(lm[:, t], cst[:, C_GRP:C_GRP + NE], i8[:, t, 0:1], -1.0e30,
                                     ALU.not_equal, ALU.mult))
                link(V.tensor_tensor(lm[:, t], lm[:, t], le[:, t], ALU.add))
                link(V.max(m8[:, t], lm[:, t]))
                link(V.tensor_tensor(gts[:, t, 2:3], m8[:, t, 1:2], m8[:, t, 0:1], ALU.subtract))
                if t == 0:
                    link(V.max_index(i8u[:, t], m8[:, t], lm[:, t]))
                else:
                    V.max_index(i8u[:, t], m8[:, t], lm[:, t]).then_inc(s_gex, 1)
                    dve.wait_ge(s_gex, 1)
                link(V.tensor_copy(i8[:, t], i8u[:, t]))
                for k in range(2):
                    l = V.tensor_scalar(oh[:, k, t], cst[:, C_IO:C_IO + NE], i8[:, t, k:k + 1], None, ALU.is_equal)
                if t == 0:
                    link(l)
            l.then_inc(s_oh, 1)
            dve.wait_ge(s_route, 1)
            link(V.tensor_scalar(gts[:, :, 4:5], gts[:, :, 3:4], 1.0, None, ALU.add))
            link(V.tensor_tensor(gts[:, :, 5:6], gts[:, :, 4:5], gts[:, :, 1:2], ALU.mult))
            link(V.reciprocal(gcol[:, :, 0:1], gts[:, :, 5:6]))
            link(V.tensor_tensor(gcol[:, :, 1:2], gcol[:, :, 0:1], gts[:, :, 3:4], ALU.mult))
            for t in range(NT):
                link(V.tensor_scalar(gate[:, t], oh[:, 0, t], gcol[:, t, 0:1], None, ALU.mult))
                link(V.scalar_tensor_tensor(gate[:, t], oh[:, 1, t], gcol[:, t, 1:2], gate[:, t], ALU.mult, ALU.add))
            dve.wait_ge(s_rank, 1)
            link(V.memset(slot[:, :, NE:], -1.0))
            link(V.tensor_tensor(le, oh[:, 0], oh[:, 1], ALU.add))
            link(V.scalar_tensor_tensor(slot[:, :, 0:NE], bank[5][:, 0:NT * NE].rearrange("p (t e) -> p t e", t=NT), 1.0,
                                        le, ALU.add, ALU.mult))
            link(V.tensor_scalar(slot[:, :, 0:NE], slot[:, :, 0:NE], -1.0, None, ALU.add))
            link(V.tensor_reduce(cnt[:, 0:1], bank[5][:, 2 * NE:3 * NE], AX.X, ALU.max))
            link(V.tensor_scalar(cnt[:, 1:2], cnt[:, 0:1], float(CAP), 1.0, ALU.is_gt, ALU.add))
            for q in range(2, T // CAP):
                link(V.scalar_tensor_tensor(cnt[:, 1:2], cnt[:, 0:1], float(q * CAP), cnt[:, 1:2],
                                            ALU.is_gt, ALU.add))
            V.tensor_copy(nrounds[:, :], cnt[:, 1:2]).then_inc(s_nr, 1)
            dve.wait_ge(s_nr, 1)
            rounds = dve.value_load(nrounds[0:1, 0:1], min_val=1, max_val=T // CAP)
            iota = cst[:, C_IO:C_IO + CAP]

            def picks(p):
                for t in range(NT):
                    for j in range(2):
                        l = V.tensor_scalar(pick[:, t, j, 0:CAP], iota, slot[:, t, bass.ds(p * 2 + j, 1)], None,
                                            ALU.is_equal)
                l.then_inc(s_pick, 1)

            def adds(m):
                for i in range(8):
                    t, col = i // 4, i % 4
                    x2c = x2[:, t, col * 512:(col + 1) * 512]
                    dve.wait_ge(s_comb, m * 8 + i + 1)
                    V.tensor_tensor(x2c, x2c, bank[6 + i % 2][:, :], ALU.add).then_inc(s_add[t], 1)

            def pair(n, p, first):
                for q in (0, 2):
                    dve.wait_ge(s_xg, n * 4 + q + 1)
                    V.tensor_copy(xT[:, q * 4:q * 4 + 4, :], bank[0][:, :].rearrange("p (k i) -> p k i", k=4))\
                        .then_inc(s_xeD, 1)
                b3 = bank[3][:, :].rearrange("p (k i) -> p k i", k=FC)
                for j in range(2):
                    e = dve.snap(n * 2 + j)
                    dve.wait_ge(s_eth, e + 1)
                    V.scalar_tensor_tensor(eth, eth, 1.0, b3[:, :, 0:SLOTS], ALU.add, ALU.mult).then_inc(s_u, 1)
                    dve.wait_ge(s_u, e + 1)
                    V.scalar_tensor_tensor(gT, eth, 0.5, b3[:, :, SLOTS:], ALU.mult, ALU.mult).then_inc(s_g, 1)
                    if j == 0:
                        picks(p + 1)
                        if not first:
                            adds(dve.snap(n - 1))
                            for t in range(NT):
                                dve.wait_ge(s_add[t], n * 4)
                        for v in range(2):
                            for t in range(NT):
                                for i in range(2):
                                    c = bass.ds(p * 2 + (i ^ v), 1)
                                    l = V.tensor_scalar(place[:, t, v, i, 0:CAP], iota, slot[:, t, c], gate[:, t, c],
                                                        ALU.is_equal, ALU.mult)
                        l.then_inc(s_place, 1)
                    dve.wait_ge(s_ed, e * 6 + 6)
                    for side in range(2):
                        l = V.tensor_copy(y_pair[side * 64:side * 64 + 64, side ^ j, 0:512],
                                          bank[4][side * 64:side * 64 + 64, :])
                    l.then_inc(s_yeD, 1)

            if CAP < SLOTS:
                link(V.memset(pick, 0.0))
                link(V.memset(place, 0.0))
            with dve.Fori(0, rounds) as r:
                link.enter(r, 1)
                picks(0)
                pair(dve.snap(r * NP), 0, True)
                with dve.Fori(1, NP) as p:
                    pair(dve.snap(r * NP + p), p, False)
                adds(dve.snap(r * NP + (NP - 1)))
                link(V.tensor_scalar(slot, slot, -float(CAP), None, ALU.add))
                link.leave(rounds)
            for t in range(NT):
                dve.wait_ge(s_frt, t + 1)
                link(V.reciprocal(stat[:, 4 + t:5 + t], stat[:, 2 + t:3 + t]))
                V.scalar_tensor_tensor(x2[:, t], x2[:, t], stat[:, 4 + t:5 + t], wfin, ALU.mult, ALU.mult)\
                    .then_inc(s_fin, 1)

        @block.gpsimd
        def _(pool):
            G = nc.gpsimd

            def heads(h):
                pool.wait_ge(s_exp, h * 2 + 2)
                mq = cst[:, C_MQ:C_MQ + P].rearrange("p (a i) -> p a i", a=1).broadcast_to([P, NT, P])
                G.tensor_tensor(dec[:, :, 0, :], gexp, mq, ALU.mult).then_inc(s_dec, 1)
                G.tensor_tensor(dec[:, :, 1, :], gexp, bm, ALU.mult).then_inc(s_dec, 1)
                pool.wait_ge(s_nat, h + 1)
                for o, q in ((rhs[:, 1], Q_KB), (kdec, Q_KDEC)):
                    G.tensor_tensor(o, nat[:, 1], ph[:, q:q + NT].rearrange("p (q a) -> p q a", a=1)
                                    .broadcast_to([P, NT, P]), ALU.mult).then_inc(s_kb, 1)
                pool.wait_ge(s_aa, h + 1)
                for lv in range(LEVELS):
                    m = cst[:, C_LV + lv * P:C_LV + (lv + 1) * P].rearrange("p (a i) -> p a i", a=1)
                    G.tensor_tensor(atm[:, lv], aa[:, :, 1, :], m.broadcast_to([P, NT, P]), ALU.mult).then_inc(s_atm, 1)

            pool.wait_ge(s_cst, 16)
            with pool.Fori(0, NH) as h:
                heads(h)



_INS = ["x", "norm_mix_w", "w_in", "gdn_conv_w", "gdn_a_log", "gdn_dt_bias", "gdn_norm_w", "rg_conv_w", "rg_conv_b",
        "rg_w_rgate", "rg_b_rgate", "rg_w_igate", "rg_b_igate", "rg_lambda", "rg_norm_w", "w_out", "norm_ffn_w",
        "router_w_group", "router_b_group", "router_w_expert", "router_b_expert", "expert_w1", "expert_w3",
        "expert_w2", "norm_final_w"]


def kernel(**inputs):
    import numpy as _np
    import concourse.bacc as _bacc
    from concourse import mybir as _mybir
    from concourse.bass_utils import run_bass_kernel_spmd as _run

    nc = _bacc.Bacc("TRN2", target_bir_lowering=False, num_devices=1)
    arrays, args = {}, []
    for name in _INS:
        a = _np.ascontiguousarray(inputs[name])
        arrays[f"in_{name}_dram"] = a
        args.append(nc.dram_tensor(f"in_{name}_dram", a.shape, _mybir.dt.from_np(a.dtype), kind="ExternalInput").ap())
    arrays["shape_constants"] = constants()
    args.append(nc.dram_tensor("shape_constants", (P, C_END), F32, kind="ExternalInput").ap())
    res = nc.dram_tensor("out_0_dram", (1, T, D), F32, kind="ExternalOutput").ap()
    build(nc, args, res)
    r = _run(nc, [arrays], core_ids=[0])
    return r.results[0]["out_0_dram"]
```

```python
from contextlib import ExitStack

import numpy as np
import concourse.bass as bass
from concourse import mybir

F32 = mybir.dt.float32
F32R = mybir.dt.float32r
I32 = mybir.dt.int32
U32 = mybir.dt.uint32
ALU = mybir.AluOpType
ACT = mybir.ActivationFunctionType
AX = mybir.AxisListType

P = 128
D = 2048
T = 256
NT = T // P
KD = D // P
NH = 8
HD = 128
CH = 64
NC = T // CH
TAPS = 4
GW = NH * HD
NG = 4
EG = 8
NE = NG * EG
FF = 512
FC = FF // P
SLOTS = 64
PIECE = 2048
RING = 3
SPLIT = 1280
WOUT = [(n, c) for n in range(4) for c in (0, 2)] + [(n, c) for n in range(4) for c in (1, 3)]
LEVELS = 6
EPS = 1e-6
QSCALE = float(HD) ** -0.5
GELU_C = 0.044715
GELU_S = 0.7978845608028654
HD2 = D // 2
NP = NE // 2

C_ID = 0
C_MQ = C_ID + P
C_MS = C_MQ + P
C_LV = C_MS + P
C_TRI = C_LV + LEVELS * P
C_ONE = C_TRI + P
C_IO = C_ONE + P
C_GRP = C_IO + SLOTS
C_SEL = C_GRP + NE
C_END = C_SEL + 16

Q_CONV = 0
Q_RGC = 12
Q_CB = 16
Q_BR = 17
Q_BI = 18
Q_LAM = 19
Q_RGN = 20
Q_VB = 21
Q_KB = 23
Q_KDEC = 25
Q_GC = 27
NQ = 29


def constants():
    c = np.zeros((P, C_END), np.float32)
    j, i = np.meshgrid(np.arange(P), np.arange(P), indexing="ij")
    same = j // CH == i // CH
    c[:, C_ID:C_ID + P] = j == i
    c[:, C_MQ:C_MQ + P] = (same & (j <= i)) * QSCALE
    c[:, C_MS:C_MS + P] = same & (j < i)
    for l in range(LEVELS):
        b = 1 << l
        c[:, C_LV + l * P:C_LV + (l + 1) * P] = (j // (2 * b) == i // (2 * b)) & (j // b % 2 == 0) & (i // b % 2 == 1)
    c[:, C_TRI:C_TRI + P] = j < i
    c[:, C_ONE:C_ONE + P] = 1
    c[:, C_IO:C_IO + SLOTS] = np.arange(SLOTS)
    c[:, C_GRP:C_GRP + NE] = np.arange(NE) // EG
    c[:16, C_SEL:C_SEL + 16] = np.eye(16)
    return c


class Link:

    def __init__(self, eng, sem):
        self.eng, self.sem, self.base, self.n = eng, sem, 0, 0

    def __call__(self, ins):
        ins.then_inc(self.sem, 1)
        self.n += 1
        self.eng.wait_ge(self.sem, self.base + self.n)
        return ins

    def enter(self, turn, per):
        if not isinstance(self.base, int) or self.n:
            self.start = self.base + self.n
        else:
            self.start = self.base
        self.base, self.n, self.per = self.start + turn * per, 0, per

    def leave(self, turns):
        assert self.n == self.per, f"{self.sem} per body: {self.n}, not {self.per}"
        self.base, self.n = self.start + turns * self.per, 0


PER_DVE = 25


def build(nc, ins, out, slots=SLOTS):
    (x, norm_mix_w, w_in, gdn_conv_w, gdn_a_log, gdn_dt_bias, gdn_norm_w, rg_conv_w, rg_conv_b, rg_w_rgate,
     rg_b_rgate, rg_w_igate, rg_b_igate, rg_lambda, rg_norm_w, w_out, norm_ffn_w, router_w_group,
     router_b_group, router_w_expert, router_b_expert, expert_w1, expert_w3, expert_w2, norm_final_w, const) = ins

    with ExitStack() as ctx:
        def sb(name, shape, dt=F32):
            return ctx.enter_context(nc.sbuf_tensor(name, shape, dt))

        def sem(name):
            return ctx.enter_context(nc.semaphore(name))

        bank = [ctx.enter_context(nc.psum_tensor(f"bank{i}", [P, 512], F32)) for i in range(8)]

        with nc.sbuf_tensor("act_parts", [P, 2, KD, T], F32R) as ap_, nc.sbuf_tensor("w_parts", [P, RING, 2, PIECE],
                                                                                    F32R) as wp_:
            parts, wparts = ap_, wp_
        ew = sb("ew", [P, 6, 4096])
        fw = sb("fw", [P, 6 * 2048])
        hT = sb("hT", [P, KD, T])
        mixT = sb("mixT", [P, KD, T])
        cst = sb("cst", [P, C_END])
        ye = sb("ye", [P, 2, 1024])
        misc = sb("misc", [P, 2688])

        class Region:

            def __init__(self, ap, size):
                self.ap, self.size, self.at = ap, size, 0

            def take(self, *dims):
                n = int(np.prod(dims))
                a = self.ap[:, self.at:self.at + n]
                self.at += n
                assert self.at <= self.size, (self.at, self.size)
                if len(dims) == 1:
                    return a
                names = "abcd"[:len(dims)]
                return a.rearrange(f"p ({' '.join(names)}) -> p {' '.join(names)}", **dict(zip(names, dims)))

        raw = fw[:, 0:RING * PIECE].rearrange("p (s n) -> p s n", s=RING)
        R1 = Region(ew[:, 5, :], 4096)
        R1b = Region(hT[:, :, :].rearrange("p a b -> p (a b)"), 4096)
        R2 = Region(ye[:, :, :].rearrange("p a b -> p (a b)"), 2048)
        R3 = Region(misc[:, :], 2688)
        cq = R1.take(3, T)
        th = R1.take(3, T)
        nat = R1.take(2, NT, HD)
        rhs = R1.take(2, NT, HD)
        kdec = R1.take(NT, HD)
        qkT = R1.take(NT, 2, P)
        dec = R1.take(NT, 2, P)
        aa = R1b.take(NT, 2, P)
        atm = R1b.take(LEVELS, NT, P)
        tt = R1b.take(NT, 2, P)
        pm = R1b.take(NT, P)
        nwT = R1b.take(T)
        vn = R1b.take(NT, HD)
        qg = R1b.take(T)
        egb = R1.take(T)
        sq = R1b.take(2, T)
        rr = R2.take(2, T)
        gexp = R2.take(NT, P)
        bm = R2.take(NT, P)
        xc = R2.take(T)
        gg = R2.take(T)
        sz = R2.take(T)
        zr = R2.take(T)
        lru = R3.take(6, T)
        thz = R3.take(T)
        xr = R3.take(T)
        gl2 = R3.take(T)
        S = R3.take(HD)
        rgw = R3.take(2, P)
        prm = sb("prm", [P, NQ, NH])
        pc = sb("pc", [P, NQ])
        ph = sb("ph", [P, NQ])
        gnw = sb("gnw", [P, 1])
        mixw = sb("mixw", [P, KD])
        ffnw = sb("ffnw", [P, KD])
        sums = sb("sums", [P, NT, 4])
        ss4 = sb("ss4", [P, 4])
        sd4 = sb("sd4", [P, 4])
        r4 = sb("r4", [P, 4])
        eps_c = sb("eps_c", [P, 2])
        stat = sb("stat", [P, 8])
        rows = sb("rows", [16, 2, T])
        rsel = sb("rsel", [16, 2, T])
        xn = mixT[:, :, :].rearrange("p (t k) i -> p t (k i)", t=NT)
        R0 = Region(fw[:, RING * PIECE:], 6144)
        junk = R0.take(D)
        wba = R0.take(KD, 16)
        vec = R0.take(2, P)
        bar = R0.take(12, T)
        tkn = R0.take(4, NT, 16)
        lamt = R0.take(6, NH)
        par16 = R0.take(4)
        cmask = R0.take(T)
        x2 = fw[:, 8192:12288].rearrange("p (t d) -> p t d", t=NT)
        hn = fw[:, 0:4096].rearrange("p (t d) -> p t d", t=NT)
        wfin = fw[:, 4096:6144]
        wffn = ye[:, :, :].rearrange("p a b -> p (a b)")
        rw = fw[:, 6144:6144 + KD * 36].rearrange("p (k n) -> p k n", k=KD)
        rb = fw[:, 6720:6756]
        R4 = Region(fw[:, 6756:8192], 1436)
        yg = R4.take(T)
        junk1 = R4.take(P)
        og = R4.take(T)
        R4.at = 0
        lg = R4.take(NT, 8)
        le = R4.take(NT, NE)
        lm = R4.take(NT, NE)
        oh = R4.take(2, NT, NE)
        cnt = R4.take(4)
        m8 = R4.take(NT, 8)
        i8 = R4.take(NT, 8)
        gts = R4.take(NT, 8)
        slot = R4.take(NT, NE + 2)
        gate = R4.take(NT, NE)
        gcol = R4.take(NT, 2)
        i8u = sb("i8u", [P, NT, 8], U32)
        nrounds = sb("nrounds", [P, 1], I32)
        R5 = Region(ew[:, 0, :], 4096)
        ewp = [ew[:, 5, :], mixT[:, :, :].rearrange("p a b -> p (a b)"), ew[:, 3, :], ew[:, 4, :], ew[:, 2, :],
               ew[:, 1, :]]
        y_pair = ye[:, :, :]
        hs = R5.take(FF)
        eth = R5.take(FC, SLOTS)
        gT = R5.take(FC, SLOTS)
        pick = R5.take(NT, 2, SLOTS)
        place = R5.take(NT, 2, 2, SLOTS)
        placeT = R5.take(2, T)
        R6 = Region(hT[:, :, :].rearrange("p a b -> p (a b)"), 4096)
        xT = R6.take(KD, P)
        junk2 = R6.take(D)
        junk3 = fw[:, 7600:8112]

        ident = cst[:, C_ID:C_ID + P]
        ones = cst[:, C_ONE:C_ONE + P]

        s_cst = sem("s_cst")
        s_x = sem("s_x")
        s_vec = sem("s_vec")
        s_wba = sem("s_wba")
        s_win = [sem(f"s_win{b}") for b in range(RING)]
        s_high = sem("s_high")
        s_restD = sem("s_restD")
        s_restP = sem("s_restP")
        s_hH = sem("s_hH")
        s_hL = sem("s_hL")
        s_mixH = sem("s_mixH")
        s_mixL = sem("s_mixL")
        s_mixLP = sem("s_mixLP")
        s_x2e = sem("s_x2e")
        s_wfin = sem("s_wfin")
        s_rgw = sem("s_rgw")
        s_init = sem("s_init")
        s_vecT = sem("s_vecT")
        s_xss = sem("s_xss")
        s_xh = sem("s_xh")
        s_xT = sem("s_xT")
        s_hT = sem("s_hT")
        s_hTa = sem("s_hTa")
        s_ba = sem("s_ba")
        s_bath = sem("s_bath")
        s_barow = sem("s_barow")
        s_lex = sem("s_lex")
        s_par = sem("s_par")
        s_alog = sem("s_alog")
        s_eg = sem("s_eg")
        s_tokT = sem("s_tokT")
        s_prm = sem("s_prm")
        s_proj = sem("s_proj")
        s_conv = sem("s_conv")
        s_th = sem("s_th")
        s_silu = sem("s_silu")
        s_evac = sem("s_evac")
        s_rx = sem("s_rx")
        s_gsq = sem("s_gsq")
        s_gv = sem("s_gv")
        s_gth = sem("s_gth")
        s_gate = sem("s_gate")
        s_sel = sem("s_sel")
        s_gb = sem("s_gb")
        s_rgmm = sem("s_rgmm")
        s_ri = sem("s_ri")
        s_la = sem("s_la")
        s_a = sem("s_a")
        s_m2 = sem("s_m2")
        s_mu = sem("s_mu")
        s_y = sem("s_y")
        s_nat_mm = sem("s_nat_mm")
        s_ss = sem("s_ss")
        s_nat = sem("s_nat")
        s_vb = sem("s_vb")
        s_diff = sem("s_diff")
        s_exp = sem("s_exp")
        s_dec = sem("s_dec")
        s_kb = sem("s_kb")
        s_back = sem("s_back")
        s_qkT = sem("s_qkT")
        s_qg = sem("s_qg")
        s_kk = sem("s_kk")
        s_aa = sem("s_aa")
        s_atm = sem("s_atm")
        s_P = sem("s_P")
        s_Pc = sem("s_Pc")
        s_U = sem("s_U")
        s_T = sem("s_T")
        s_w = sem("s_w")
        s_nw = sem("s_nw")
        s_v = sem("s_v")
        s_vn = sem("s_vn")
        s_o = sem("s_o")
        s_S = sem("s_S")
        s_sq = sem("s_sq")
        s_nss = sem("s_nss")
        s_rt = sem("s_rt")
        s_mix = sem("s_mix")
        l_dve = sem("l_dve")
        l_act = sem("l_act")
        l_pool = sem("l_pool")
        s_x2r = sem("s_x2r")
        s_x2 = sem("s_x2")
        s_wffn = sem("s_wffn")
        s_rw = sem("s_rw")
        s_hss = sem("s_hss")
        s_sums = sem("s_sums")
        s_rstd = sem("s_rstd")
        s_hscaled = sem("s_hscaled")
        s_sumd = sem("s_sumd")
        s_rws = sem("s_rws")
        s_hn = sem("s_hn")
        s_h2T = sem("s_h2T")
        s_h2mm = sem("s_h2mm")
        s_lgt = sem("s_lgt")
        s_gex = sem("s_gex")
        s_route = sem("s_route")
        s_oh = sem("s_oh")
        s_rank = sem("s_rank")
        s_nr = sem("s_nr")
        s_ew = [sem(f"s_ew{b}") for b in range(6)]
        s_ed = sem("s_ed")
        s_pick = sem("s_pick")
        s_xg = sem("s_xg")
        s_place = sem("s_place")
        s_placeT_mm = sem("s_placeT_mm")
        s_placeT = sem("s_placeT")
        s_comb = sem("s_comb")
        s_add = [sem("s_add0"), sem("s_add1")]
        s_xeA = sem("s_xeA")
        s_xeD = sem("s_xeD")
        s_H = sem("s_H")
        s_hs = sem("s_hs")
        s_HT = sem("s_HT")
        s_eth = sem("s_eth")
        s_g = sem("s_g")
        s_Y = sem("s_Y")
        s_yeA = sem("s_yeA")
        s_yeD = sem("s_yeD")
        s_u = sem("s_u")
        s_fin = sem("s_fin")
        s_frt = sem("s_frt")
        s_out = sem("s_out")

        block = ctx.enter_context(nc.Block())
        w_in_v = w_in[0].rearrange("(k p) n -> p k n", p=P)
        BLOCK_COL = [0, GW, 2 * GW, 3 * GW, 4 * GW + 2 * NH, 5 * GW + 2 * NH]
        x_v = x[0].rearrange("(t p) d -> p t d", p=P)
        w_out_v = w_out[0].rearrange("(k p) n -> p k n", p=P)
        out_v = out[0].rearrange("(t p) d -> p t d", p=P)
        CAP = slots

        @block.sync
        def _(sp):
            sp.dma_start(xn, x_v).then_inc(s_x, 16)
            sp.dma_start(cst[:, :], const).then_inc(s_cst, 16)
            rv = [(vec[0:96, 0, :], gdn_conv_w[0].rearrange("j (b h p) -> (j b h) p", p=P, h=NH)),
                  (vec[0:32, 1, :], rg_conv_w[0].rearrange("j (h p) -> (j h) p", p=P)),
                  (vec[32:40, 1, :], rg_conv_b[0].rearrange("(h p) -> h p", p=P)),
                  (vec[40:48, 1, :], rg_b_rgate[0].rearrange("(h p) -> h p", p=P)),
                  (vec[48:56, 1, :], rg_b_igate[0].rearrange("(h p) -> h p", p=P)),
                  (vec[56:64, 1, :], rg_lambda[0].rearrange("(h p) -> h p", p=P)),
                  (vec[64:72, 1, :], rg_norm_w[0].rearrange("(h p) -> h p", p=P)),
                  (vec[72:88, 1, :], norm_mix_w[0].rearrange("(h p) -> h p", p=P)),
                  (vec[88:89, 1, :], gdn_norm_w),
                  (vec[89:105, 1, :], norm_ffn_w[0].rearrange("(h p) -> h p", p=P))]
            for to, of in rv:
                sp.dma_start(to, of).then_inc(s_vec, 16)
            sp.dma_start(wba, w_in_v[:, :, 4 * GW:4 * GW + 2 * NH]).then_inc(s_wba, 16)
            sp.wait_ge(s_init, 1)
            sp.dma_start(par16[8:16, 0:1], gdn_a_log.rearrange("a h -> h a")).then_inc(s_alog, 16)
            sp.dma_start(par16[8:16, 1:2], gdn_dt_bias.rearrange("a h -> h a")).then_inc(s_alog, 16)

            def slot_free(g):
                sp.wait_ge(s_restD, g - RING + 1)
                sp.wait_ge(s_restP, g - RING + 1)

            def load_block(h, b):
                sp.dma_start(raw[:, b % RING].rearrange("p (k n) -> p k n", k=KD),
                             w_in_v[:, :, bass.ds(h * P + BLOCK_COL[b], P)]).then_inc(s_win[b % RING], 16)

            def load_rg(h):
                sp.dma_start(rgw[:, 0, :], rg_w_rgate[0, h]).then_inc(s_rgw, 16)
                sp.dma_start(rgw[:, 1, :], rg_w_igate[0, h]).then_inc(s_rgw, 16)

            for b in range(6):
                if b >= RING:
                    slot_free(b)
                load_block(0, b)
            load_rg(0)
            with sp.Fori(1, NH) as h:
                for b in range(6):
                    slot_free(h * 6 + b)
                    load_block(h, b)
                sp.wait_ge(s_rgmm, h)
                load_rg(h)
            for m, (n, c) in enumerate(WOUT):
                slot_free(NH * 6 + m)
                sp.dma_start(raw[:, m % RING].rearrange("p (k n) -> p k n", k=4),
                             w_out_v[:, c * 4:c * 4 + 4, n * 512:(n + 1) * 512]).then_inc(s_win[m % RING], 16)
                if m == RING - 1:
                    sp.wait_ge(s_prm, 1)
                    sp.dma_start(x2, x_v).then_inc(s_x2r, 16)
                    sp.dma_start(rw[:, :, 0:NG], router_w_group[0].rearrange("(k p) n -> p k n", p=P)).then_inc(s_rw, 16)
                    sp.dma_start(rw[:, :, NG:], router_w_expert[0].rearrange("(k p) n -> p k n", p=P)).then_inc(s_rw, 16)
                    sp.dma_start(rb[:, 0:NG], router_b_group.broadcast_to([P, NG])).then_inc(s_rw, 16)
                    sp.dma_start(rb[:, NG:], router_b_expert.broadcast_to([P, NE])).then_inc(s_rw, 16)
                if m == 10:
                    sp.wait_ge(s_mix, 2 * NH)
                    sp.dma_start(wffn, norm_ffn_w.broadcast_to([P, D])).then_inc(s_wffn, 16)

            def load_expert(e, piece):
                half, which = piece // 2, piece % 2
                if piece < 4:
                    src = (expert_w1, expert_w3)[which][0, e].rearrange("(c k p) n -> p c k n", p=P, c=2)[:, half]
                    dst = ewp[piece].rearrange("p (k n) -> p k n", n=FF)
                else:
                    src = expert_w2[0, e].rearrange("(c k p) n -> p c k n", p=P, c=2)[:, which]
                    dst = ewp[piece].rearrange("p (k n) -> p k n", n=D)
                sp.dma_start(dst, src).then_inc(s_ew[piece], 16)

            sp.wait_ge(s_mixL, 3)
            sp.wait_ge(s_mixLP, 2)
            load_expert(0, 0)
            load_expert(0, 1)
            for piece in range(2, 6):
                sp.wait_ge(s_proj, NH * 6 + min(12 + piece, 16))
                load_expert(0, piece)
            sp.dma_start(wfin, norm_final_w.rearrange("(a d) -> a d", a=1).broadcast_to([P, D])).then_inc(s_wfin, 16)
            sp.wait_ge(s_nr, 1)
            rounds = sp.value_load(nrounds[0:1, 0:1], min_val=1, max_val=T // CAP)
            with sp.Fori(0, rounds) as r:
                with sp.Fori(1, NE) as e:
                    for piece in range(6):
                        sp.wait_ge(s_ed, (r * NE + e - 1) * 6 + piece + 1)
                        load_expert(e, piece)
                with sp.If(r + 1 < rounds):
                    for piece in range(6):
                        sp.wait_ge(s_ed, (r * NE + NE - 1) * 6 + piece + 1)
                        load_expert(0, piece)
                sp.nop()
            for t in range(NT):
                sp.wait_ge(s_fin, t + 1)
                sp.dma_start(out_v[:, t], x2[:, t]).then_inc(s_out, 16)
            sp.wait_ge(s_out, 16 * NT)

        @block.tensor
        def _(pe):
            def mm(o, l, r, start, stop):
                return nc.tensor.matmul(o, l, r, start=start, stop=stop, skip_group_check=True)

            def tr(o, i, n=P):
                return nc.tensor.transpose(o, i, ident[0:n, 0:n])

            pe.wait_ge(s_cst, 16)
            pe.wait_ge(s_vec, 16 * 10)
            tr(bank[7][:, 0:96], vec[0:96, 0, :], 96)
            tr(bank[7][:, 96:201], vec[0:105, 1, :], 105).then_inc(s_vecT, 1)
            for k2 in range(KD // 2):
                if k2 == 0:
                    pe.wait_ge(s_xh, NT)
                if k2 >= 4:
                    pe.wait_ge(s_hT if k2 % 2 == 0 else s_hTa, (k2 - 4) // 2 + 1)
                for k in range(2):
                    for t in range(NT):
                        l = tr(bank[k2 % 4][:, (k * NT + t) * P:(k * NT + t + 1) * P],
                               xn[:, t, (2 * k2 + k) * P:(2 * k2 + k + 1) * P])
                l.then_inc(s_xT, 1)
            pe.wait_ge(s_hT, 4)
            pe.wait_ge(s_hTa, 4)
            pe.wait_ge(s_wba, 16)
            for k in range(KD):
                l = mm(bank[4][0:16, 0:T], wba[:, k, :], hT[:, k, :], k == 0, k == KD - 1)
            l.then_inc(s_ba, 1)

            def wait_piece(g):
                pe.wait_ge(s_restD, g + 1)
                pe.wait_ge(s_restP, g + 1)

            def project(h):
                for b in range(6):
                    o = bank[b % 2][:, 0:T]
                    wait_piece(h * 6 + b)
                    if b >= 2 or not isinstance(h, int):
                        pe.wait_ge(s_evac, h * 6 + b - 1)
                    w = wparts[:, b % RING].rearrange("p a (k n) -> p a k n", k=KD)
                    for k in range(KD):
                        mm(o, w[:, 0, k, :], parts[:, 0, k, :], k == 0, False)
                        mm(o, w[:, 0, k, :], parts[:, 1, k, :], False, False)
                        l = mm(o, w[:, 1, k, :], parts[:, 0, k, :], False, k == KD - 1)
                        if k == KD - 1:
                            l.then_inc(s_proj, 1)
                        yield

            def begin(h):
                pe.wait_ge(s_silu, h * 3 + 3)
                for b in range(2):
                    for t in range(NT):
                        tr(bank[2][:, (b * NT + t) * P:(b * NT + t + 1) * P], cq[:, b, t * P:(t + 1) * P])
                for t in range(NT):
                    l = tr(bank[3][:, t * P:(t + 1) * P], cq[:, 2, t * P:(t + 1) * P])
                l.then_inc(s_nat_mm, 1)
                pe.wait_ge(s_rgw, h * 32 + 32)
                pe.wait_ge(s_rx, h + 1)
                mm(bank[5][:, 0:T], rgw[:, 0, :], xc, True, True)
                mm(bank[5][:, T:], rgw[:, 1, :], xc, True, True).then_inc(s_rgmm, 1)
                pe.wait_ge(s_sel, h + 1)
                mm(bank[6][:, :], cst[0:16, C_ONE:C_ONE + P], rsel[:, :, :].rearrange("p a b -> p (a b)"), True, True)\
                    .then_inc(s_gb, 1)

            def heads(h, fill, lead):
                fill(lead)
                pe.wait_ge(s_nat, h + 1)
                for t in range(NT):
                    for b in range(2):
                        l = tr(bank[4][:, (t * 2 + b) * P:(t * 2 + b + 1) * P], nat[:, b, t, :])
                l.then_inc(s_back, 1)
                fill(4)
                pe.wait_ge(s_qkT, h + 1)
                for t in range(NT):
                    l = mm(bank[5][:, t * 2 * P:(t + 1) * 2 * P], qkT[:, t, 1, :],
                           qkT[:, t].rearrange("p a b -> p (a b)"), True, True)
                l.then_inc(s_kk, 1)
                fill(5)
                pe.wait_ge(s_atm, h * LEVELS + 1)
                for t in range(NT):
                    l = tr(bank[3][:, T + t * P:T + (t + 1) * P], atm[:, 0, t, :])
                l.then_inc(s_P, 1)
                fill(3)
                for lv in range(1, LEVELS):
                    pe.wait_ge(s_atm, h * LEVELS + lv + 1)
                    pe.wait_ge(s_T, h * LEVELS + lv)
                    for t in range(NT):
                        l = mm(bank[3][:, T + t * P:T + (t + 1) * P], atm[:, lv, t, :], tt[:, t, 0, :], True, True)
                    l.then_inc(s_P, 1)
                    fill(3)
                    pe.wait_ge(s_Pc, h * (LEVELS - 1) + lv)
                    for t in range(NT):
                        mm(bank[2][:, t * 2 * P:t * 2 * P + P], tt[:, t, 1, :], pm[:, t, :], True, True)
                        l = mm(bank[2][:, t * 2 * P + P:(t + 1) * 2 * P], pm[:, t, :], tt[:, t, 1, :], True, True)
                    l.then_inc(s_U, 1)
                    fill(3)
                pe.wait_ge(s_T, h * LEVELS + LEVELS)
                pe.wait_ge(s_kb, h * 2 + 2)
                pe.wait_ge(s_vb, h + 1)
                for t in range(NT):
                    l = mm(bank[6][:, t * P:(t + 1) * P], rhs[:, 1, t, :], tt[:, t, 1, :], True, True)
                l.then_inc(s_w, 1)
                fill(3)
                for c in range(NC):
                    t, lo = c // 2, c % 2 * CH
                    hi = lo + CH
                    l = mm(bank[5][lo:hi, 0:P], tt[lo:hi, t, 1, lo:hi], rhs[lo:hi, 0, t, :], True, c == 0)
                    if c:
                        pe.wait_ge(s_nw, h + 1)
                        pe.wait_ge(s_S, h * 3 + c)
                        l = mm(bank[5][lo:hi, 0:P], nwT[:, c * CH:(c + 1) * CH], S, False, True)
                    l.then_inc(s_v, 1)
                    fill(2)
                    pe.wait_ge(s_vn, h * NC + c + 1)
                    if c < NC - 1:
                        mm(bank[4][:, 0:HD], kdec[lo:hi, t, :], vn[lo:hi, t, :], True, True)
                    if c:
                        pe.wait_ge(s_qg, h + 1)
                        mm(bank[7][:, c * CH:(c + 1) * CH], S, qg[:, c * CH:(c + 1) * CH], True, False)
                    mm(bank[7][:, c * CH:(c + 1) * CH], vn[lo:hi, t, :], aa[lo:hi, t, 0, lo:hi], c == 0, True)\
                        .then_inc(s_o, 1)
                    fill(3)
                fill(4)
            def square_sums(h):
                pe.wait_ge(s_sq, h * 2 + 2)
                mm(bank[4][:, :], ones, sq.rearrange("p a b -> p (a b)"), True, True).then_inc(s_nss, 1)

            pe.wait_ge(s_hL, 4)
            for _ in project(0):
                pass
            pe.wait_ge(s_eg, 1)
            for q in range(4):
                for t in range(NT):
                    l = tr(bank[7][:, (q * NT + t) * 16:(q * NT + t + 1) * 16],
                           bar[0:16, 8 + q, t * P:(t + 1) * P], 16)
            l.then_inc(s_tokT, 1)
            begin(0)
            with pe.Fori(1, NH) as i:
                steps = project(i)

                def fill(n):
                    for _ in range(n):
                        next(steps, None)

                heads(i - 1, fill, 16)
                for _ in steps:
                    pass
                begin(i)
                square_sums(i - 1)

            def wo(m, o, first, last, chunks=range(4)):
                n, c = WOUT[m]
                wait_piece(NH * 6 + m)
                w = wparts[:, m % RING].rearrange("p a (k n) -> p a k n", k=4)
                for k in chunks:
                    for t in range(NT):
                        a = [parts[:, q, c * 4 + k, t * P:(t + 1) * P] for q in range(2)]
                        mm(o[t][:, :], a[0], w[:, 0, k, :], first and k == 0, False)
                        mm(o[t][:, :], a[0], w[:, 1, k, :], False, False)
                        l = mm(o[t][:, :], a[1], w[:, 0, k, :], False, last and k == 3)
                        if k == 3 and t == NT - 1:
                            l.then_inc(s_proj, 1)
                        yield

            def early():
                pe.wait_ge(s_evac, NH * 6)
                for m in range(8):
                    if m < 2:
                        pe.wait_ge(s_mixL, m + 1)
                    elif m % 2 == 0:
                        pe.wait_ge(s_x2e, m // 2)
                    yield from wo(m, bank[0:2], m % 2 == 0, m % 2 == 1)

            steps = early()
            asked, given = 0, 0

            def fill_w(n):
                nonlocal asked, given
                asked += n
                while given < min(64, asked * 64 // 69):
                    next(steps)
                    given += 1

            heads(NH - 1, fill_w, 0)
            for _ in steps:
                pass
            square_sums(NH - 1)
            pe.wait_ge(s_mixLP, 2)
            pe.wait_ge(s_x2e, 4)

            def transposes(n):
                pe.wait_ge(s_x2, n + 1)
                for k in range(4):
                    for t in range(NT):
                        l = tr(bank[2 * n + k // 2][:, (k % 2 * NT + t) * P:(k % 2 * NT + t + 1) * P],
                               x2[:, t, (4 * n + k) * P:(4 * n + k + 1) * P])
                l.then_inc(s_h2mm, 1)

            def logits(n):
                if n == 0:
                    pe.wait_ge(s_rws, 1)
                pe.wait_ge(s_h2T, n + 1)
                for k in range(4 * n, 4 * n + 4):
                    for t in range(NT):
                        l = mm(bank[t][:, 0:NG + NE], hT[:, k, t * P:(t + 1) * P], rw[:, k, :],
                               k == 0, k == KD - 1)
                return l

            for chunks in ((0, 1, 2), (3,)):
                if chunks == (3,):
                    pe.wait_ge(s_mixL, 3)
                for m in (8, 9):
                    for _ in wo(m, bank[0:2], m == 8, m == 9, chunks):
                        pass
            for m in range(10, 16):
                n, second = (m - 8) // 2, m % 2 == 1
                for _ in wo(m, bank[2 * n:2 * n + 2], not second, second):
                    pass
                if n and not second:
                    transposes(n - 1)
                if n and second:
                    logits(n - 1)
            transposes(3)
            logits(3).then_inc(s_lgt, 1)
            pe.wait_ge(s_oh, 1)
            for t in range(NT):
                for u in range(t + 1):
                    for q in range(2):
                        mm(bank[5][:, t * NE:(t + 1) * NE], cst[:, C_TRI:C_TRI + P] if u == t else ones,
                           oh[:, q, u, :], u == 0 and q == 0, u == t and q == 1)
            for u in range(NT):
                for q in range(2):
                    l = mm(bank[5][:, 2 * NE:3 * NE], ones, oh[:, q, u, :], u == 0 and q == 0, u == 1 and q == 1)
            l.then_inc(s_rank, 1)

            pe.wait_ge(s_hn, NT)
            pe.wait_ge(s_nr, 1)
            rounds = pe.value_load(nrounds[0:1, 0:1], min_val=1, max_val=T // CAP)

            def gather(n, r, p):
                pe.wait_ge(s_pick, r * (NP + 1) + p + 1)
                for q in range(4):
                    if q >= 2:
                        pe.wait_ge(s_xeA if q % 2 else s_xeD, n * 2 + 1)
                    for c in range(4):
                        for t in range(NT):
                            l = mm(bank[q % 2][:, c * P:(c + 1) * P], hn[:, t, (q * 4 + c) * P:(q * 4 + c + 1) * P],
                                   pick[:, t].rearrange("p a b -> p (a b)"), t == 0, t == NT - 1)
                    l.then_inc(s_xg, 1)

            def combine(m):
                pe.wait_ge(s_placeT, m + 1)
                pe.wait_ge(s_yeA, m * 2 + 2)
                pe.wait_ge(s_yeD, m * 2 + 2)
                for i in range(8):
                    t, col = i // 4, i % 4
                    if i >= 2:
                        pe.wait_ge(s_add[(i - 2) // 4], m * 4 + (i - 2) % 4 + 1)
                    mm(bank[6 + i % 2][:, :], placeT[:, col // 2, t * P:(t + 1) * P],
                       y_pair[:, col // 2, col % 2 * 512:col % 2 * 512 + 512], True, True).then_inc(s_comb, 1)

            def pair(n, r, p, first):
                gather(n, r, p)
                pe.wait_ge(s_xeA, n * 2 + 2)
                pe.wait_ge(s_xeD, n * 2 + 2)
                for j in range(2):
                    e = pe.snap(n * 2 + j)
                    for half in range(2):
                        for which in range(2):
                            pe.wait_ge(s_ew[half * 2 + which], e * 16 + 16)
                        for k in range(KD // 2):
                            for which in range(2):
                                l = mm(bank[2][which * 64:which * 64 + 64, :],
                                       xT[:, half * 8 + k, j * SLOTS:(j + 1) * SLOTS],
                                       ewp[half * 2 + which].rearrange("p (k n) -> p k n", n=FF)[:, k, :],
                                       half == 0 and k == 0, half == 1 and k == KD // 2 - 1)
                                if k == KD // 2 - 1:
                                    l.then_inc(s_ed, 1)
                    pe.wait_ge(s_hs, e + 1)
                    for k in range(FC):
                        l = tr(bank[3][:, k * P:(k + 1) * P], hs[:, k * P:(k + 1) * P])
                    l.then_inc(s_HT, 1)
                    if j == 0 and not first:
                        combine(pe.snap(n - 1))
                    if j == 1:
                        pe.wait_ge(s_place, n + 1)
                        for v in range(2):
                            for t in range(NT):
                                l = tr(bank[6][:, (v * NT + t) * P:(v * NT + t + 1) * P],
                                       place[:, t, v].rearrange("p a b -> p (a b)"))
                        l.then_inc(s_placeT_mm, 1)
                        pe.wait_ge(s_yeA, n * 2 + 1)
                        pe.wait_ge(s_yeD, n * 2 + 1)
                    pe.wait_ge(s_g, e + 1)
                    for k in range(FC):
                        if k % 2 == 0:
                            pe.wait_ge(s_ew[4 + k // 2], e * 16 + 16)
                        w2 = ewp[4 + k // 2].rearrange("p (k n) -> p k n", n=D)
                        for i in range(2):
                            for side in range(2):
                                col = (side ^ j) * HD2 + i * 512
                                l = mm(bank[4 + i][side * 64:side * 64 + 64, :], gT[:, k, :],
                                       w2[:, k % 2, col:col + 512], k == 0, k == FC - 1)
                        if k % 2:
                            l.then_inc(s_ed, 1)

            with pe.Fori(0, rounds) as r:
                pair(pe.snap(r * NP), r, 0, True)
                with pe.Fori(1, NP) as p:
                    pair(pe.snap(r * NP + p), r, p, False)
                combine(pe.snap(r * NP + (NP - 1)))

        @block.scalar
        def _(act):
            link = Link(act, l_act)
            act.wait_ge(s_x, 16)
            act.wait_ge(s_init, 1)
            for t in range(NT):
                link(act.activation(junk, xn[:, t], ACT.Square, accum_out=stat[:, t:t + 1]))
            act.activation(stat[:, 2:4], stat[:, 0:2], ACT.Sqrt, scale=1.0 / D, bias=eps_c[:, 0:1]).then_inc(s_xss, 1)
            act.wait_ge(s_par, 1)
            for k2 in range(1, KD // 2, 2):
                act.wait_ge(s_xT, k2 + 1)
                for k in range(2):
                    l = act.activation(hT[:, 2 * k2 + k, :], bank[k2 % 4][:, k * T:(k + 1) * T], ACT.Copy,
                                       scale=mixw[:, 2 * k2 + k:2 * k2 + k + 1])
                l.then_inc(s_hTa, 1)
            for c in range(4):
                act.wait_ge(s_hT, c + 1)
                act.wait_ge(s_hTa, c + 1)
                act.activation(parts[:, 0, c * 4:c * 4 + 4, :], hT[:, c * 4:c * 4 + 4, :], ACT.Copy).then_inc(s_hH, 1)

            def high(g, slot, use, halves=(0, 1)):
                act.wait_ge(s_win[slot], use * 16)
                if not (isinstance(g, int) and g < RING):
                    act.wait_ge(s_proj, g - RING + 1)
                for i in halves:
                    cols = slice(i * PIECE // 2, (i + 1) * PIECE // 2)
                    act.activation(wparts[:, slot, 0, cols], raw[:, slot, cols], ACT.Copy).then_inc(s_high, 1)

            for g in range(RING):
                high(g, g, 1)
            act.wait_ge(s_alog, 32)
            act.activation(par16[0:16, 2:3], par16[0:16, 0:1], ACT.Exp).then_inc(s_lex, 1)
            act.wait_ge(s_par, 2)
            act.activation(lamt[:, 1], lamt[:, 0], ACT.Exp, scale=-1.0).then_inc(s_lex, 1)
            act.wait_ge(s_ba, 1)
            act.activation(bar[0:16, 0], bank[4][0:16, 0:T], ACT.Tanh, scale=0.5).then_inc(s_bath, 1)
            act.wait_ge(s_barow, 1)
            act.activation(bar[0:16, 3], bar[0:16, 2], ACT.Exp, scale=-1.0).then_inc(s_bath, 1)
            def evac(h, b, halves=(0, 1)):
                act.wait_ge(s_proj, h * 6 + b + 1)
                src = bank[b % 2][:, 0:T]
                if b == 3:
                    act.activation(thz, src, ACT.Tanh, scale=0.5)
                act.activation((th[:, 0], th[:, 1], th[:, 2], zr, xr, gg)[b], src, ACT.Copy).then_inc(s_evac, 1)
                if halves:
                    high(h * 6 + b + RING, b % RING, h * 2 + b // RING + 2, halves)

            def tanh_half(h, b):
                act.wait_ge(s_conv, h * 3 + b + 1)
                act.activation(th[:, b], cq[:, b], ACT.Tanh, scale=0.5).then_inc(s_th, 1)

            def roots(h):
                act.wait_ge(s_nss, h + 1)
                act.activation(rr, bank[4][:, :].rearrange("p (a b) -> p a b", a=2), ACT.Sqrt,
                               scale=1.0 / HD, bias=eps_c[:, 0:1]).then_inc(s_rt, 1)

            def begin(h):
                act.wait_ge(s_nat_mm, h + 1)
                for q in range(4):
                    l = act.activation(junk1, bank[2][:, q * P:(q + 1) * P], ACT.Square,
                                       accum_out=ss4[:, q:q + 1])
                    link(l)
                act.wait_ge(s_evac, h * 6 + 6)
                act.activation(gl2, gg, ACT.Square, scale=GELU_C ** 0.5).then_inc(s_gsq, 1)
                act.wait_ge(s_rgmm, h + 1)
                act.wait_ge(s_sel, h + 1)
                act.activation(lru[:, 0], bank[5][:, 0:T], ACT.Tanh, scale=0.5, bias=ph_bias(0)).then_inc(s_ri, 1)
                act.activation(lru[:, 1], bank[5][:, T:], ACT.Tanh, scale=0.5, bias=ph_bias(1)).then_inc(s_ri, 1)
                act.wait_ge(s_gb, h + 1)
                act.activation(egb, bank[6][:, 0:T], ACT.Exp).then_inc(s_exp, 1)
                act.wait_ge(s_diff, h + 1)
                act.activation(gexp, gexp, ACT.Exp).then_inc(s_exp, 1)
                act.wait_ge(s_la, h + 1)
                act.activation(lru[:, 3], lru[:, 2], ACT.Exp)
                act.activation(lru[:, 4], lru[:, 2], ACT.Exp, scale=2.0)
                act.activation(lru[:, 5], lru[:, 2], ACT.Tanh).then_inc(s_a, 1)
                act.wait_ge(s_gv, h + 1)
                act.activation(gl2, gl2, ACT.Tanh, scale=GELU_S).then_inc(s_gth, 1)
                if not (isinstance(h, int) and h == 0):
                    roots(h - 1)
                act.activation(sd4[:, :], ss4[:, :], ACT.Sqrt, bias=eps_c[:, 1:2]).then_inc(s_ss, 1)
                act.wait_ge(s_m2, h + 1)
                act.activation(lru[:, 4], lru[:, 5], ACT.Sqrt, scale=-1.0).then_inc(s_mu, 1)

            def heads(h, evac_next, tanh_next, late_next, mix=None):
                if mix is not None:
                    mix()
                act.wait_ge(s_back, h + 1)
                act.activation(qkT, bank[4][:, :].rearrange("p (t b i) -> p t b i", t=NT, b=2), ACT.Copy)\
                    .then_inc(s_qkT, 1)
                high(h * 6 + 8, 2, h * 2 + 3)
                evac_next(0)
                for lv in range(1, LEVELS):
                    act.wait_ge(s_P, h * LEVELS + lv + 1)
                    act.activation(pm, bank[3][:, T:].rearrange("p (t i) -> p t i", t=NT), ACT.Copy).then_inc(s_Pc, 1)
                    if lv == 2:
                        tanh_next(0)
                        evac_next(1)
                    if lv == 3:
                        late_next(1)
                    if lv == 4:
                        tanh_next(1)
                evac_next(2)
                act.wait_ge(s_w, h + 1)
                act.activation(nwT, bank[6][:, 0:T], ACT.Copy, scale=-1.0).then_inc(s_nw, 1)
                for c in range(NC):
                    lo = c % 2 * CH
                    act.wait_ge(s_v, h * NC + c + 1)
                    act.activation(vn[lo:lo + CH, c // 2, :], bank[5][lo:lo + CH, 0:P], ACT.Copy).then_inc(s_vn, 1)
                    if c == 1:
                        tanh_next(2)
                        evac_next(3)
                    if c == 3:
                        late_next(3)
                    if c == 3 and mix is not None:
                        high_out(8)
                act.wait_ge(s_y, h + 1)
                act.activation(sq[:, 1], lru[:, 1], ACT.Square, scale=0.5).then_inc(s_sq, 1)
                act.wait_ge(s_o, h * NC + NC)
                act.activation(sq[:, 0], bank[7][:, 0:T], ACT.Square).then_inc(s_sq, 1)

            def ph_bias(i):
                return ph[:, Q_BR + i:Q_BR + i + 1]

            for b in range(6):
                evac(0, b, (0, 1) if b < 5 else ())
                if b == 0:
                    act.wait_ge(s_barow, 2)
                    act.activation(bar[0:16, 10], bar[0:16, 8], ACT.Exp)
                    act.activation(bar[0:16, 11], bar[0:16, 7], ACT.Exp).then_inc(s_eg, 1)
                if 1 <= b <= 3:
                    tanh_half(0, b - 1)
            begin(0)
            PER = 4
            with act.Fori(1, NH) as i:
                link.enter(i - 1, PER)
                now = {1: (0,), 3: ()}
                heads(i - 1, lambda b: evac(i, b, now.get(b, (0, 1))), lambda b: tanh_half(i, b),
                      lambda b: high(i * 6 + b + RING, b % RING, i * 2 + b // RING + 2,
                                     [q for q in (0, 1) if q not in now[b]]))
                evac(i, 4)
                evac(i, 5, ())
                begin(i)
                link.leave(NH - 1)

            def high_out(m):
                high(NH * 6 + m, m % RING, NH * 2 + m // RING + 1)

            def mix_high():
                act.wait_ge(s_proj, NH * 6)
                act.wait_ge(s_mix, 8)
                for lo, hi in ((0, 4), (8, 12)):
                    act.activation(parts[:, 0, lo:hi, :], mixT[:, lo:hi, :], ACT.Copy).then_inc(s_mixH, 1)

            def mix_high_late(n):
                if n == 3:
                    act.wait_ge(s_mix, 2 * NH - 2)
                    for lo, hi in ((4, 7), (12, 15)):
                        act.activation(parts[:, 0, lo:hi, :], mixT[:, lo:hi, :], ACT.Copy).then_inc(s_mixH, 1)

            at = {("e", 0): 3, ("e", 1): 4, ("t", 1): 5, ("e", 2): 6, ("e", 3): 7}

            def high_at(key):
                if key in at:
                    high_out(at[key])

            heads(NH - 1, lambda b: high_at(("e", b)), lambda b: high_at(("t", b)), mix_high_late, mix_high)
            roots(NH - 1)
            act.wait_ge(s_mix, 2 * NH)
            act.activation(parts[:, 0].rearrange("p (a b) t -> p a b t", b=NH)[:, :, NH - 1, :],
                           mixT[:, :, :].rearrange("p (a b) t -> p a b t", b=NH)[:, :, NH - 1, :], ACT.Copy)\
                .then_inc(s_mixH, 1)
            for m in range(9, 12):
                high_out(m)
            for n in range(4):
                act.wait_ge(s_x2, n + 1)
                for t in range(NT):
                    act.activation(junk3, x2[:, t, n * 512:(n + 1) * 512], ACT.Square,
                                   accum_out=sums[:, t, n:n + 1]).then_inc(s_sums, 1)
                    act.wait_ge(s_sums, n * NT + t + 1)
                for m in range(12 + 2 * n, min(14 + 2 * n, 16)):
                    high_out(m)
                act.wait_ge(s_h2mm, n + 1)
                for i in range(2):
                    l = act.activation(hT[:, 4 * n + 2 * i:4 * n + 2 * i + 2, :],
                                       bank[2 * n + i][:, :].rearrange("p (k i) -> p k i", k=2), ACT.Copy)
                l.then_inc(s_h2T, 1)
            act.wait_ge(s_sumd, 1)
            act.activation(stat[:, 2:4], stat[:, 0:2], ACT.Sqrt, scale=1.0 / D, bias=eps_c[:, 0:1]).then_inc(s_hss, 1)
            act.wait_ge(s_rstd, 1)
            act.wait_ge(s_proj, NH * 6 + 16)
            for t in range(NT):
                act.activation(hn[:, t], x2[:, t], ACT.Copy, scale=stat[:, 4 + t:5 + t]).then_inc(s_hscaled, 1)
            act.wait_ge(s_gex, 1)
            for t in range(NT):
                act.activation(le[:, t, 0:NG], lg[:, t, 0:NG], ACT.Exp, bias=gts[:, t, 0:1],
                               accum_out=gts[:, t, 1:2])
                l = act.activation(gts[:, t, 3:4], gts[:, t, 2:3], ACT.Exp)
            l.then_inc(s_route, 1)

            act.wait_ge(s_nr, 1)
            rounds = act.value_load(nrounds[0:1, 0:1], min_val=1, max_val=T // CAP)
            with act.Fori(0, rounds) as r:
                with act.Fori(0, NP) as p:
                    n = act.snap(r * NP + p)
                    for q in (1, 3):
                        act.wait_ge(s_xg, n * 4 + q + 1)
                        act.activation(xT[:, q * 4:q * 4 + 4, :], bank[1][:, :].rearrange("p (k i) -> p k i", k=4),
                                       ACT.Copy).then_inc(s_xeA, 1)
                    for j in range(2):
                        e = act.snap(n * 2 + j)
                        act.wait_ge(s_ed, e * 6 + 4)
                        act.activation(hs, bank[2][:, :], ACT.Copy).then_inc(s_hs, 1)
                        act.wait_ge(s_HT, e + 1)
                        act.activation(eth, bank[3][:, :].rearrange("p (k i) -> p k i", k=FC)[:, :, 0:SLOTS],
                                       ACT.Tanh, scale=0.5).then_inc(s_eth, 1)
                        if j == 1:
                            act.wait_ge(s_placeT_mm, n + 1)
                            act.activation(placeT.rearrange("p v t -> p (v t)"), bank[6][:, :], ACT.Copy)\
                                .then_inc(s_placeT, 1)
                        act.wait_ge(s_ed, e * 6 + 6)
                        for side in range(2):
                            l = act.activation(y_pair[side * 64:side * 64 + 64, side ^ j, 512:],
                                               bank[5][side * 64:side * 64 + 64, :], ACT.Copy)
                        l.then_inc(s_yeA, 1)
            for t in range(NT):
                act.wait_ge(s_add[t], rounds * (4 * NP))
                link(act.activation(junk2, x2[:, t], ACT.Square, accum_out=stat[:, t:t + 1]))
                act.activation(stat[:, 2 + t:3 + t], stat[:, t:t + 1], ACT.Sqrt, scale=1.0 / D,
                               bias=eps_c[:, 0:1]).then_inc(s_frt, 1)

        @block.vector
        def _(dve):
            link = Link(dve, l_dve)
            V = nc.vector

            def log1p(out_, u, tmp, x2_, r_):
                link(V.tensor_scalar(tmp, u, 2.0, None, ALU.add))
                link(V.reciprocal(r_, tmp))
                link(V.tensor_tensor(tmp, u, r_, ALU.mult))
                link(V.tensor_tensor(x2_, tmp, tmp, ALU.mult))
                link(V.tensor_scalar(r_, x2_, 2.0 / 15, None, ALU.mult))
                for c in (13, 11, 9, 7, 5, 3):
                    link(V.scalar_tensor_tensor(r_, r_, 2.0 / c, x2_, ALU.add, ALU.mult))
                link(V.scalar_tensor_tensor(out_, r_, 2.0, tmp, ALU.add, ALU.mult))

            V.memset(eps_c[:, 0:1], EPS)
            V.memset(eps_c[:, 1:2], 4 * EPS)
            link(V.memset(par16, 0.0))
            link(V.memset(cmask, 1.0))
            V.memset(cmask.rearrange("p (c i) -> p c i", c=NC)[:, :, 0:1], 0.0).then_inc(s_init, 1)
            dve.wait_ge(s_vecT, 1)
            V.tensor_copy(mixw[:, :], bank[7][:, 168:184]).then_inc(s_par, 1)
            link(V.tensor_copy(lamt[:, 1], bank[7][:, 152:160]))
            V.scalar_tensor_tensor(lamt[:, 0], lamt[:, 1], -1.0, lamt[:, 1], ALU.mult, ALU.max).then_inc(s_par, 1)
            V.tensor_scalar(lamt[:, 2], bank[7][:, 152:160], -1.0, 0.0, ALU.mult, ALU.max)
            V.tensor_copy(prm[:, 0:Q_BR, :], bank[7][:, 0:Q_BR * NH].rearrange("p (q h) -> p q h", h=NH))
            V.tensor_scalar(prm[:, Q_BR:Q_LAM, :], bank[7][:, Q_BR * NH:Q_LAM * NH].rearrange("p (q h) -> p q h", h=NH),
                            0.5, None, ALU.mult)
            V.tensor_scalar(prm[:, Q_RGN, :], bank[7][:, 160:168], 0.5, None, ALU.mult)
            V.tensor_scalar(gnw[:, :], bank[7][:, 184:185], 0.5, None, ALU.mult)
            V.tensor_copy(ffnw[:, :], bank[7][:, 185:201])
            dve.wait_ge(s_xss, 1)
            link(V.reciprocal(stat[:, 4:6], stat[:, 2:4]))
            for t in range(NT):
                V.tensor_scalar(xn[:, t], xn[:, t], stat[:, 4 + t:5 + t], None, ALU.mult).then_inc(s_xh, 1)
            for k2 in range(0, KD // 2, 2):
                dve.wait_ge(s_xT, k2 + 1)
                for k in range(2):
                    l = V.tensor_scalar(hT[:, 2 * k2 + k, :], bank[k2 % 4][:, k * T:(k + 1) * T],
                                        mixw[:, 2 * k2 + k:2 * k2 + k + 1], None, ALU.mult)
                l.then_inc(s_hT, 1)
            for c in range(4):
                dve.wait_ge(s_hH, c + 1)
                V.tensor_tensor(parts[:, 1, c * 4:c * 4 + 4, :], hT[:, c * 4:c * 4 + 4, :],
                                parts[:, 0, c * 4:c * 4 + 4, :], ALU.subtract).then_inc(s_hL, 1)

            def rest(g, slot):
                dve.wait_ge(s_high, g * 2 + 2)
                V.tensor_tensor(wparts[:, slot, 1, 0:SPLIT], raw[:, slot, 0:SPLIT], wparts[:, slot, 0, 0:SPLIT],
                                ALU.subtract).then_inc(s_restD, 1)

            for g in range(RING):
                rest(g, g)
            B = [bar[0:16, i] for i in range(12)]
            dve.wait_ge(s_bath, 1)
            dve.wait_ge(s_alog, 32)
            link(V.tensor_scalar(B[9], B[0], 0.5, 0.5, ALU.mult, ALU.add))
            link(V.tensor_scalar(B[1], bank[4][0:16, 0:T], par16[0:16, 1:2], None, ALU.add))
            V.scalar_tensor_tensor(B[2], B[1], -1.0, B[1], ALU.mult, ALU.max).then_inc(s_barow, 1)
            V.tensor_scalar(B[4], B[1], 0.0, None, ALU.max)
            V.tensor_copy(rows[:, 1], B[9])
            link(V.tensor_scalar(par16[0:16, 3:4], par16[0:16, 2:3], -1.0, None, ALU.mult))
            dve.wait_ge(s_bath, 2)
            log1p(B[6], B[3], B[5], B[7], B[0])
            rest(3, 0)
            link(V.tensor_tensor(B[5], B[4], B[6], ALU.add))
            link(V.tensor_scalar(B[6], B[5], par16[0:16, 3:4], None, ALU.mult))
            link(V.tensor_tensor_scan(B[8], cmask[0:16, :], B[6], 0.0, ALU.mult, ALU.add))
            link(V.tensor_copy(rows[:, 0], B[8]))
            b8 = B[8].rearrange("p (c i) -> p c i", c=NC)
            V.tensor_tensor(B[7].rearrange("p (c i) -> p c i", c=NC), b8[:, :, CH - 1:CH].broadcast_to([16, NC, CH]),
                            b8, ALU.subtract).then_inc(s_barow, 1)

            def conv_taps(h, o, src, q, step):
                for j in range(TAPS - 1, -1, -1):
                    s = TAPS - 1 - j
                    if s == 0:
                        if q == "rx":
                            i = V.tensor_scalar(o, src, pc[:, Q_RGC + j:Q_RGC + j + 1], pc[:, Q_CB:Q_CB + 1],
                                                ALU.mult, ALU.add)
                        else:
                            i = V.tensor_scalar(o, src, pc[:, j * 3 + q:j * 3 + q + 1], None, ALU.mult)
                        link(i)
                    else:
                        w = pc[:, Q_RGC + j:Q_RGC + j + 1] if q == "rx" else pc[:, j * 3 + q:j * 3 + q + 1]
                        i = V.scalar_tensor_tensor(o[:, s:], src[:, 0:T - s], w, o[:, s:], ALU.mult, ALU.add)
                        if s < TAPS - 1:
                            link(i)
                i.then_inc(step, 1)

            def params(h):
                link(V.tensor_copy(pc[:, 0:Q_BR], prm[:, 0:Q_BR, h]))

            def conv(h, b):
                dve.wait_ge(s_evac, h * 6 + b + 1)
                conv_taps(h, cq[:, b], th[:, b], b, s_conv)

            def silu(h, b):
                dve.wait_ge(s_th, h * 3 + b + 1)
                V.scalar_tensor_tensor(cq[:, b], th[:, b], 1.0, cq[:, b], ALU.add, ALU.mult).then_inc(s_silu, 1)

            def conv_rx(h):
                dve.wait_ge(s_evac, h * 6 + 5)
                conv_taps(h, xc, xr, "rx", s_rx)

            def silu_z(h):
                V.scalar_tensor_tensor(sz, thz, 1.0, zr, ALU.add, ALU.mult)

            def select(h):
                link(V.tensor_copy(ph[:, :], prm[:, :, h]))
                link(V.tensor_scalar(rsel[:, 0], rows[:, 0], cst[0:16, bass.ds(h + (C_SEL + NH), 1)], None, ALU.mult))
                V.tensor_scalar(rsel[:, 1], rows[:, 1], cst[0:16, bass.ds(h + C_SEL, 1)], None, ALU.mult)\
                    .then_inc(s_sel, 1)

            def begin(h):
                dve.wait_ge(s_gsq, h + 1)
                V.scalar_tensor_tensor(gl2, gl2, 1.0, gg, ALU.add, ALU.mult).then_inc(s_gv, 1)
                dve.wait_ge(s_exp, h * 2 + 1)
                for t in range(NT):
                    V.tensor_scalar(gexp[:, t], bank[6][:, t * P:(t + 1) * P], ph[:, Q_GC + t:Q_GC + t + 1], 0.0,
                                    ALU.subtract, ALU.min)
                V.tensor_tensor(bm, bank[6][:, T:].rearrange("p (t i) -> p t i", t=NT),
                                cst[:, C_MS:C_MS + P].rearrange("p (a i) -> p a i", a=1).broadcast_to([P, NT, P]),
                                ALU.mult).then_inc(s_diff, 1)
                dve.wait_ge(s_ri, h * 2 + 2)
                V.tensor_scalar(lru[:, 2], lru[:, 0], 1.0, ph[:, Q_LAM:Q_LAM + 1], ALU.add, ALU.mult).then_inc(s_la, 1)
                dve.wait_ge(s_ss, h + 1)
                link(V.reciprocal(r4[:, :], sd4[:, :]))
                V.tensor_tensor(nat.rearrange("p b t i -> p (b t) i"), bank[2][:, :].rearrange("p (q i) -> p q i", q=4),
                                r4[:, :].rearrange("p (q a) -> p q a", a=1).broadcast_to([P, 4, P]), ALU.mult)\
                    .then_inc(s_nat, 1)
                V.tensor_tensor(rhs[:, 0], bank[3][:, 0:T].rearrange("p (t i) -> p t i", t=NT),
                                ph[:, Q_VB:Q_VB + NT].rearrange("p (q a) -> p q a", a=1).broadcast_to([P, NT, P]),
                                ALU.mult).then_inc(s_vb, 1)
                dve.wait_ge(s_gth, h + 1)
                link(V.scalar_tensor_tensor(gg, gl2, 1.0, gg, ALU.add, ALU.mult))
                dve.wait_ge(s_a, h + 1)
                V.scalar_tensor_tensor(lru[:, 5], lru[:, 4], 1.0, lru[:, 5], ALU.add, ALU.mult).then_inc(s_m2, 1)

            def invert(h, n):
                dve.wait_ge(s_rt, h + 1)
                link(V.reciprocal(rr[:, n], rr[:, n]))

            def finish(h):
                V.tensor_tensor(mixT[:, h, :], og, rr[:, 0], ALU.mult).then_inc(s_mix, 1)
                V.tensor_tensor(mixT[:, h + NH, :], yg, rr[:, 1], ALU.mult).then_inc(s_mix, 1)
                dve.wait_ge(s_mix, h * 2 + 2)

            def heads(h, pre, between):
                dve.wait_ge(s_qkT, h + 1)
                V.scalar_tensor_tensor(qg.rearrange("p (t i) -> p t i", t=NT),
                                       bank[4][:, :].rearrange("p (t b i) -> p t b i", t=NT, b=2)[:, :, 0, :], QSCALE,
                                       egb.rearrange("p (t i) -> p t i", t=NT), ALU.mult, ALU.mult).then_inc(s_qg, 1)
                dve.wait_ge(s_kk, h + 1)
                dve.wait_ge(s_dec, h * 2 + 2)
                V.tensor_tensor(aa.rearrange("p t b i -> p (t b i)"), bank[5][:, :],
                                dec.rearrange("p t b i -> p (t b i)"), ALU.mult).then_inc(s_aa, 1)
                pre(0)
                idb = ident.rearrange("p (a i) -> p a i", a=1).broadcast_to([P, NT, P])
                dve.wait_ge(s_atm, h * LEVELS + 1)
                link(V.tensor_tensor(tt[:, :, 1, :], idb, atm[:, 0], ALU.subtract))
                dve.wait_ge(s_P, h * LEVELS + 1)
                V.tensor_tensor(tt[:, :, 0, :], idb, bank[3][:, T:].rearrange("p (t i) -> p t i", t=NT),
                                ALU.subtract).then_inc(s_T, 1)
                between("start", 0)
                link(V.scalar_tensor_tensor(lru[:, 1], lru[:, 1], 1.0, xc, ALU.add, ALU.mult))
                dve.wait_ge(s_mu, h + 1)
                link(V.scalar_tensor_tensor(lru[:, 2], lru[:, 1], 0.5, lru[:, 4], ALU.mult, ALU.mult))
                link(V.tensor_tensor_scan(lru[:, 0], lru[:, 3], lru[:, 2], 0.0, ALU.mult, ALU.add))
                V.tensor_tensor(lru[:, 1], lru[:, 0], gg, ALU.mult).then_inc(s_y, 1)
                between("levels", 0)
                for lv in range(1, LEVELS):
                    dve.wait_ge(s_U, h * (LEVELS - 1) + lv)
                    V.tensor_tensor(tt.rearrange("p t b i -> p (t b i)"), tt.rearrange("p t b i -> p (t b i)"),
                                    bank[2][:, :], ALU.subtract).then_inc(s_T, 1)
                    if lv == 2:
                        pre(1)
                    if lv == 4:
                        pre(2)
                    between("levels", lv)
                    if lv == LEVELS - 1:
                        dve.wait_ge(s_y, h + 1)
                        link(V.tensor_scalar(yg, lru[:, 1], ph[:, Q_RGN:Q_RGN + 1], None, ALU.mult))
                for c in range(NC - 1):
                    dve.wait_ge(s_o, h * NC + c + 1)
                    if c == 0:
                        V.tensor_copy(S, bank[4][:, 0:HD]).then_inc(s_S, 1)
                    else:
                        V.scalar_tensor_tensor(S, S, egb[:, c * CH + CH - 1:c * CH + CH], bank[4][:, 0:HD],
                                               ALU.mult, ALU.add).then_inc(s_S, 1)
                    if c == 0:
                        pre(3)
                    if c == 2:
                        pre(4)
                    between("chunks", c)
                dve.wait_ge(s_sq, h * 2 + 2)
                link(V.scalar_tensor_tensor(og, bank[7][:, 0:T], gnw[:, 0:1], sz, ALU.mult, ALU.mult))
            params(0)
            for b in range(3):
                conv(0, b)
                if b:
                    rest(b + 3, b)
                silu(0, b)
            dve.wait_ge(s_lex, 2)
            log1p(lamt[:, 3], lamt[:, 1], lamt[:, 4], lamt[:, 5], lamt[:, 0])
            link(V.tensor_tensor(lamt[:, 4], lamt[:, 2], lamt[:, 3], ALU.add))
            V.tensor_scalar(prm[:, Q_LAM, :], lamt[:, 4], -0.5 * 8.0, None, ALU.mult)
            rest(6, 0)
            conv_rx(0)
            rest(7, 1)
            silu_z(0)
            dve.wait_ge(s_tokT, 1)
            link(V.tensor_copy(tkn, bank[7][:, 0:P].rearrange("p (q t i) -> p q t i", q=4, t=NT)))
            V.tensor_copy(prm[:, Q_GC:Q_GC + NT, :], tkn[:, 0, :, NH:])
            V.tensor_scalar(prm[:, Q_VB:Q_VB + NT, :], tkn[:, 1, :, 0:NH], 0.5, None, ALU.mult)
            V.tensor_copy(prm[:, Q_KDEC:Q_KDEC + NT, :], tkn[:, 3, :, NH:])
            V.tensor_tensor(prm[:, Q_KB:Q_KB + NT, :], tkn[:, 1, :, 0:NH], tkn[:, 2, :, NH:], ALU.mult)\
                .then_inc(s_prm, 1)
            dve.wait_ge(s_prm, 1)
            select(0)
            begin(0)

            def body(i, first):
                def pre(n):
                    if n == 0:
                        params(i)
                        conv(i, 0)
                    elif n == 1:
                        silu(i, 0)
                        conv(i, 1)
                    elif n == 2:
                        silu(i, 1)
                    elif n == 3:
                        conv(i, 2)
                    elif n == 4:
                        silu(i, 2)

                def between(what, n):
                    if what != "levels":
                        return
                    if n == 0:
                        rest(i * 6 + 2, 2)
                    elif n == 1:
                        rest(i * 6 + 3, 0)
                    elif n == 3:
                        if not first:
                            invert(i - 2, 0)
                        rest(i * 6 + 4, 1)
                    elif n == 4 and not first:
                        invert(i - 2, 1)
                    elif n == 5:
                        if not first:
                            finish(i - 2)
                        rest(i * 6 + 5, 2)

                heads(i - 1, pre, between)
                rest(i * 6 + 6, 0)
                conv_rx(i)
                silu_z(i)
                select(i)
                rest(i * 6 + 7, 1)
                begin(i)

            body(1, True)
            with dve.Fori(2, NH) as i:
                link.enter(i - 2, PER_DVE)
                body(i, False)
                link.leave(NH - 2)

            def rest_out(m):
                rest(NH * 6 + m, m % RING)

            def mix_rest(n, view):
                dve.wait_ge(s_mixH, n)
                V.tensor_tensor(view(parts[:, 1]), view(mixT[:, :, :]), view(parts[:, 0]), ALU.subtract)\
                    .then_inc(s_mixL, 1)

            def add_out(n, o, step):
                for t in range(NT):
                    l = V.tensor_tensor(x2[:, t, n * 512:(n + 1) * 512], x2[:, t, n * 512:(n + 1) * 512],
                                        o[t][:, :], ALU.add)
                l.then_inc(step, 1)

            def add_early(n):
                dve.wait_ge(s_proj, NH * 6 + 2 * n + 2)
                add_out(n, bank[0:2], s_x2e)

            def between(what, n):
                if what == "start":
                    rest_out(2)
                elif what == "levels":
                    {0: lambda: (rest_out(3), add_early(0)), 1: lambda: invert(NH - 2, 0), 2: lambda: rest_out(4),
                     3: lambda: add_early(1), 4: lambda: (rest_out(5), invert(NH - 2, 1)),
                     5: lambda: (rest_out(6), finish(NH - 2))}[n]()
                else:
                    {0: lambda: add_early(2), 1: lambda: rest_out(7), 2: lambda: rest_out(8)}[n]()

            dve.wait_ge(s_x2r, 16)
            mix_rest(1, lambda a: a[:, 0:4, :])
            mix_rest(2, lambda a: a[:, 8:12, :])
            heads(NH - 1, lambda n: None, between)
            add_early(3)
            for n in range(2):
                invert(NH - 1, n)
            finish(NH - 1)
            mix_rest(5, lambda a: a.rearrange("p (a b) t -> p a b t", b=NH)[:, :, NH - 1, :])
            dve.wait_ge(s_x2e, 4)
            for m in range(9, 12):
                rest_out(m)
            dve.wait_ge(s_rw, 16 * 4)
            V.tensor_tensor(rw, rw, ffnw[:, :].rearrange("p (k a) -> p k a", a=1).broadcast_to([P, KD, NG + NE]),
                            ALU.mult).then_inc(s_rws, 1)
            for n in range(4):
                dve.wait_ge(s_proj, NH * 6 + 8 + 2 * n + 2)
                add_out(n, bank[2 * n:2 * n + 2], s_x2)
                for m in range(12 + 2 * n, min(14 + 2 * n, 16)):
                    rest_out(m)
            link(V.memset(lg, -3.0e38))
            dve.wait_ge(s_sums, 4 * NT)
            V.tensor_reduce(stat[:, 0:2], sums[:, :, :], AX.X, ALU.add).then_inc(s_sumd, 1)
            dve.wait_ge(s_hss, 1)
            V.reciprocal(stat[:, 4:6], stat[:, 2:4]).then_inc(s_rstd, 1)
            dve.wait_ge(s_rstd, 1)
            dve.wait_ge(s_lgt, 1)
            for t in range(NT):
                lgp = bank[t][:, 0:NG + NE]
                link(V.scalar_tensor_tensor(lg[:, t, 0:NG], lgp[:, 0:NG], stat[:, 4 + t:5 + t], rb[:, 0:NG],
                                            ALU.mult, ALU.add))
                link(V.scalar_tensor_tensor(le[:, t], lgp[:, NG:], stat[:, 4 + t:5 + t], rb[:, NG:],
                                            ALU.mult, ALU.add))
            for t in range(NT):
                link(V.max(m8[:, t], lg[:, t]))
                V.tensor_scalar(gts[:, t, 0:1], m8[:, t, 0:1], -1.0, None, ALU.mult)
                link(V.max_index(i8u[:, t], m8[:, t], lg[:, t]))
                link(V.tensor_copy(i8[:, t], i8u[:, t]))
                link(V.tensor_scalar(lm[:, t], cst[:, C_GRP:C_GRP + NE], i8[:, t, 0:1], -1.0e30,
                                     ALU.not_equal, ALU.mult))
                link(V.tensor_tensor(lm[:, t], lm[:, t], le[:, t], ALU.add))
                link(V.max(m8[:, t], lm[:, t]))
                link(V.tensor_tensor(gts[:, t, 2:3], m8[:, t, 1:2], m8[:, t, 0:1], ALU.subtract))
                if t == 0:
                    link(V.max_index(i8u[:, t], m8[:, t], lm[:, t]))
                else:
                    V.max_index(i8u[:, t], m8[:, t], lm[:, t]).then_inc(s_gex, 1)
                    dve.wait_ge(s_gex, 1)
                link(V.tensor_copy(i8[:, t], i8u[:, t]))
                for k in range(2):
                    l = V.tensor_scalar(oh[:, k, t], cst[:, C_IO:C_IO + NE], i8[:, t, k:k + 1], None, ALU.is_equal)
                if t == 0:
                    link(l)
            l.then_inc(s_oh, 1)
            dve.wait_ge(s_route, 1)
            link(V.tensor_scalar(gts[:, :, 4:5], gts[:, :, 3:4], 1.0, None, ALU.add))
            link(V.tensor_tensor(gts[:, :, 5:6], gts[:, :, 4:5], gts[:, :, 1:2], ALU.mult))
            link(V.reciprocal(gcol[:, :, 0:1], gts[:, :, 5:6]))
            link(V.tensor_tensor(gcol[:, :, 1:2], gcol[:, :, 0:1], gts[:, :, 3:4], ALU.mult))
            for t in range(NT):
                link(V.tensor_scalar(gate[:, t], oh[:, 0, t], gcol[:, t, 0:1], None, ALU.mult))
                link(V.scalar_tensor_tensor(gate[:, t], oh[:, 1, t], gcol[:, t, 1:2], gate[:, t], ALU.mult, ALU.add))
            dve.wait_ge(s_rank, 1)
            link(V.memset(slot[:, :, NE:], -1.0))
            link(V.tensor_tensor(le, oh[:, 0], oh[:, 1], ALU.add))
            link(V.scalar_tensor_tensor(slot[:, :, 0:NE], bank[5][:, 0:NT * NE].rearrange("p (t e) -> p t e", t=NT), 1.0,
                                        le, ALU.add, ALU.mult))
            link(V.tensor_scalar(slot[:, :, 0:NE], slot[:, :, 0:NE], -1.0, None, ALU.add))
            link(V.tensor_reduce(cnt[:, 0:1], bank[5][:, 2 * NE:3 * NE], AX.X, ALU.max))
            link(V.tensor_scalar(cnt[:, 1:2], cnt[:, 0:1], float(CAP), 1.0, ALU.is_gt, ALU.add))
            for q in range(2, T // CAP):
                link(V.scalar_tensor_tensor(cnt[:, 1:2], cnt[:, 0:1], float(q * CAP), cnt[:, 1:2],
                                            ALU.is_gt, ALU.add))
            V.tensor_copy(nrounds[:, :], cnt[:, 1:2]).then_inc(s_nr, 1)
            dve.wait_ge(s_nr, 1)
            rounds = dve.value_load(nrounds[0:1, 0:1], min_val=1, max_val=T // CAP)
            iota = cst[:, C_IO:C_IO + CAP]

            def picks(p):
                for t in range(NT):
                    for j in range(2):
                        l = V.tensor_scalar(pick[:, t, j, 0:CAP], iota, slot[:, t, bass.ds(p * 2 + j, 1)], None,
                                            ALU.is_equal)
                l.then_inc(s_pick, 1)

            def adds(m):
                for i in range(8):
                    t, col = i // 4, i % 4
                    x2c = x2[:, t, col * 512:(col + 1) * 512]
                    dve.wait_ge(s_comb, m * 8 + i + 1)
                    V.tensor_tensor(x2c, x2c, bank[6 + i % 2][:, :], ALU.add).then_inc(s_add[t], 1)

            def pair(n, p, first):
                for q in (0, 2):
                    dve.wait_ge(s_xg, n * 4 + q + 1)
                    V.tensor_copy(xT[:, q * 4:q * 4 + 4, :], bank[0][:, :].rearrange("p (k i) -> p k i", k=4))\
                        .then_inc(s_xeD, 1)
                b3 = bank[3][:, :].rearrange("p (k i) -> p k i", k=FC)
                for j in range(2):
                    e = dve.snap(n * 2 + j)
                    dve.wait_ge(s_eth, e + 1)
                    V.scalar_tensor_tensor(eth, eth, 1.0, b3[:, :, 0:SLOTS], ALU.add, ALU.mult).then_inc(s_u, 1)
                    dve.wait_ge(s_u, e + 1)
                    V.scalar_tensor_tensor(gT, eth, 0.5, b3[:, :, SLOTS:], ALU.mult, ALU.mult).then_inc(s_g, 1)
                    if j == 0:
                        picks(p + 1)
                        if not first:
                            adds(dve.snap(n - 1))
                            for t in range(NT):
                                dve.wait_ge(s_add[t], n * 4)
                        for v in range(2):
                            for t in range(NT):
                                for i in range(2):
                                    c = bass.ds(p * 2 + (i ^ v), 1)
                                    l = V.tensor_scalar(place[:, t, v, i, 0:CAP], iota, slot[:, t, c], gate[:, t, c],
                                                        ALU.is_equal, ALU.mult)
                        l.then_inc(s_place, 1)
                    dve.wait_ge(s_ed, e * 6 + 6)
                    for side in range(2):
                        l = V.tensor_copy(y_pair[side * 64:side * 64 + 64, side ^ j, 0:512],
                                          bank[4][side * 64:side * 64 + 64, :])
                    l.then_inc(s_yeD, 1)

            if CAP < SLOTS:
                link(V.memset(pick, 0.0))
                link(V.memset(place, 0.0))
            with dve.Fori(0, rounds) as r:
                link.enter(r, 1)
                picks(0)
                pair(dve.snap(r * NP), 0, True)
                with dve.Fori(1, NP) as p:
                    pair(dve.snap(r * NP + p), p, False)
                adds(dve.snap(r * NP + (NP - 1)))
                link(V.tensor_scalar(slot, slot, -float(CAP), None, ALU.add))
                link.leave(rounds)
            dve.wait_ge(s_wfin, 16)
            for t in range(NT):
                dve.wait_ge(s_frt, t + 1)
                link(V.reciprocal(stat[:, 4 + t:5 + t], stat[:, 2 + t:3 + t]))
                V.scalar_tensor_tensor(x2[:, t], x2[:, t], stat[:, 4 + t:5 + t], wfin, ALU.mult, ALU.mult)\
                    .then_inc(s_fin, 1)

        @block.gpsimd
        def _(pool):
            G = nc.gpsimd

            def decays(h):
                pool.wait_ge(s_exp, h * 2 + 2)
                mq = cst[:, C_MQ:C_MQ + P].rearrange("p (a i) -> p a i", a=1).broadcast_to([P, NT, P])
                G.tensor_tensor(dec[:, :, 0, :], gexp, mq, ALU.mult).then_inc(s_dec, 1)
                G.tensor_tensor(dec[:, :, 1, :], gexp, bm, ALU.mult).then_inc(s_dec, 1)

            def heads(h):
                pool.wait_ge(s_nat, h + 1)
                for o, q in ((rhs[:, 1], Q_KB), (kdec, Q_KDEC)):
                    G.tensor_tensor(o, nat[:, 1], ph[:, q:q + NT].rearrange("p (q a) -> p q a", a=1)
                                    .broadcast_to([P, NT, P]), ALU.mult).then_inc(s_kb, 1)
                pool.wait_ge(s_aa, h + 1)
                for lv in range(LEVELS):
                    m = cst[:, C_LV + lv * P:C_LV + (lv + 1) * P].rearrange("p (a i) -> p a i", a=1)
                    G.tensor_tensor(atm[:, lv], aa[:, :, 1, :], m.broadcast_to([P, NT, P]), ALU.mult).then_inc(s_atm, 1)

            def rest(g, slot):
                pool.wait_ge(s_high, g * 2 + 2)
                G.tensor_tensor(wparts[:, slot, 1, SPLIT:], raw[:, slot, SPLIT:], wparts[:, slot, 0, SPLIT:],
                                ALU.subtract).then_inc(s_restP, 1)

            pool.wait_ge(s_cst, 16)
            for g in range(8):
                rest(g, g % RING)
            decays(0)
            with pool.Fori(1, NH) as i:
                heads(i - 1)
                for b in range(6):
                    rest(i * 6 + b + 2, (b + 2) % RING)
                decays(i)
            heads(NH - 1)
            for m in range(2, 8):
                rest(NH * 6 + m, m % RING)
            for n, lo, hi in ((3, 4, 7), (4, 12, 15)):
                pool.wait_ge(s_mixH, n)
                G.tensor_tensor(parts[:, 1, lo:hi, :], mixT[:, lo:hi, :], parts[:, 0, lo:hi, :], ALU.subtract)\
                    .then_inc(s_mixLP, 1)
            for m in range(8, 16):
                rest(NH * 6 + m, m % RING)
            pool.wait_ge(s_wffn, 16)
            for t in range(NT):
                pool.wait_ge(s_hscaled, t + 1)
                G.tensor_tensor(hn[:, t], hn[:, t], wffn, ALU.mult).then_inc(s_hn, 1)



_INS = ["x", "norm_mix_w", "w_in", "gdn_conv_w", "gdn_a_log", "gdn_dt_bias", "gdn_norm_w", "rg_conv_w", "rg_conv_b",
        "rg_w_rgate", "rg_b_rgate", "rg_w_igate", "rg_b_igate", "rg_lambda", "rg_norm_w", "w_out", "norm_ffn_w",
        "router_w_group", "router_b_group", "router_w_expert", "router_b_expert", "expert_w1", "expert_w3",
        "expert_w2", "norm_final_w"]


def kernel(**inputs):
    import numpy as _np
    import concourse.bacc as _bacc
    from concourse import mybir as _mybir
    from concourse.bass_utils import run_bass_kernel_spmd as _run

    nc = _bacc.Bacc("TRN2", target_bir_lowering=False, num_devices=1)
    arrays, args = {}, []
    for name in _INS:
        a = _np.ascontiguousarray(inputs[name])
        arrays[f"in_{name}_dram"] = a
        args.append(nc.dram_tensor(f"in_{name}_dram", a.shape, _mybir.dt.from_np(a.dtype), kind="ExternalInput").ap())
    arrays["shape_constants"] = constants()
    args.append(nc.dram_tensor("shape_constants", (P, C_END), F32, kind="ExternalInput").ap())
    res = nc.dram_tensor("out_0_dram", (1, T, D), F32, kind="ExternalOutput").ap()
    build(nc, args, res)
    r = _run(nc, [arrays], core_ids=[0])
    return r.results[0]["out_0_dram"]
```
